# Optimizing a Trainium2 kernel written in Bass

```python
import math
import jax, jax.numpy as jnp
from jax import lax
import numpy as np

D_MODEL = 2048
BATCH = 1
SEQ = 256
DEPTH = 1

D_MIX = D_MODEL
D_CONV = D_MIX // 2
CONV_GROUPS = 16
CONV_WIDTH = 3
D_MLSTM = D_MIX - D_CONV
MLSTM_HEADS = 4
MLSTM_HEAD_DIM = D_MLSTM // MLSTM_HEADS
MLSTM_CHUNK = 64
N_KEYS = 128
N_EXPERTS = N_KEYS * N_KEYS
PEER_HEADS = 8
PEER_TOPK = 16
D_KEY = 256
PEER_BLOCK = 128
EPS = 1e-6

D_IN_PROJ = 3 * D_CONV + 4 * D_MLSTM + 2 * MLSTM_HEADS

kernel_name = "hymba_conv_mlstm_peer_layer"

def rmsnorm(x, g):
    xf = x.astype(jnp.float32)
    y = xf * lax.rsqrt(jnp.mean(xf * xf, axis=-1, keepdims=True) + EPS)
    return (y * g.astype(jnp.float32)).astype(x.dtype)

def short_conv_mixer(xin, gate_b, gate_c, conv_w):
    u = gate_c * xin
    seq = u.shape[1]
    up = jnp.pad(u, ((0, 0), (CONV_WIDTH - 1, 0), (0, 0)))
    y = conv_w[0] * up[:, 0:seq]
    for j in range(1, CONV_WIDTH):
        y = y + conv_w[j] * up[:, j:j + seq]
    return gate_b * y

def mlstm_chunkwise(q, k, v, i_pre, log_f):
    bsz, seq, nh, dh = q.shape
    nc = seq // MLSTM_CHUNK
    L = MLSTM_CHUNK

    def to_chunks(t):
        return t.reshape(bsz, nc, L, nh, dh).transpose(1, 0, 3, 2, 4)

    def gate_chunks(t):
        return t.reshape(bsz, nc, L, nh).transpose(1, 0, 3, 2)

    causal = jnp.tril(jnp.ones((L, L), dtype=bool))

    def step(carry, inp):
        C, n, m = carry
        qc, kc, vc, ic, fc = inp
        b = jnp.cumsum(fc, axis=-1)
        dmat = b[..., :, None] - b[..., None, :] + ic[..., None, :]
        dmat = jnp.where(causal, dmat, -jnp.inf)
        inter = b + m[..., None]
        m_loc = jnp.maximum(inter, jnp.max(dmat, axis=-1))
        sw = jnp.einsum('bhjd,bhld->bhjl', qc, kc) * jnp.exp(dmat - m_loc[..., None])
        ei = jnp.exp(inter - m_loc)
        num = ei[..., None] * jnp.einsum('bhvd,bhjd->bhjv', C, qc) + jnp.einsum('bhjl,bhlv->bhjv', sw, vc)
        nq = ei * jnp.einsum('bhd,bhjd->bhj', n, qc) + jnp.sum(sw, axis=-1)
        h = num / jnp.maximum(jnp.abs(nq), jnp.exp(-m_loc))[..., None]
        b_last = b[..., -1]
        g = b_last[..., None] - b + ic
        m_new = jnp.maximum(b_last + m, jnp.max(g, axis=-1))
        decay = jnp.exp(b_last + m - m_new)
        w = jnp.exp(g - m_new[..., None])
        C_new = decay[..., None, None] * C + jnp.einsum('bhl,bhlv,bhld->bhvd', w, vc, kc)
        n_new = decay[..., None] * n + jnp.einsum('bhl,bhld->bhd', w, kc)
        return (C_new, n_new, m_new), h

    init = (jnp.zeros((bsz, nh, dh, dh), jnp.float32),
            jnp.zeros((bsz, nh, dh), jnp.float32),
            jnp.zeros((bsz, nh), jnp.float32))
    _, h = lax.scan(step, init, (to_chunks(q), to_chunks(k), to_chunks(v),
                                 gate_chunks(i_pre), gate_chunks(log_f)))
    return h.transpose(1, 0, 3, 2, 4).reshape(bsz, seq, nh, dh)

def peer_ffn(xn, w_query, sub_keys_1, sub_keys_2, expert_u, expert_v):
    bsz, seq, d = xn.shape
    t = bsz * seq
    xf = xn.reshape(t, d)
    q = (xf @ w_query).reshape(t, PEER_HEADS, D_KEY)
    q1, q2 = q[..., :D_KEY // 2], q[..., D_KEY // 2:]
    s1 = jnp.einsum('thd,nd->thn', q1, sub_keys_1)
    s2 = jnp.einsum('thd,nd->thn', q2, sub_keys_2)
    v1, i1 = lax.top_k(s1, PEER_TOPK)
    v2, i2 = lax.top_k(s2, PEER_TOPK)
    cand = (v1[..., :, None] + v2[..., None, :]).reshape(t, PEER_HEADS, PEER_TOPK * PEER_TOPK)
    sc, ci = lax.top_k(cand, PEER_TOPK)
    a = ci // PEER_TOPK
    bsel = ci % PEER_TOPK
    idx = jnp.take_along_axis(i1, a, axis=-1) * N_KEYS + jnp.take_along_axis(i2, bsel, axis=-1)
    gate = jax.nn.softmax(sc.astype(jnp.float32), axis=-1).astype(xn.dtype)
    nb = t // PEER_BLOCK

    def block(args):
        xb, ib, gb = args
        u = jnp.take(expert_u, ib, axis=0)
        act = jax.nn.gelu(jnp.einsum('td,thkd->thk', xb, u), approximate=False)
        vv = jnp.take(expert_v, ib, axis=0)
        return jnp.einsum('thk,thkd->td', gb * act, vv)

    y = lax.map(block, (xf.reshape(nb, PEER_BLOCK, d),
                        idx.reshape(nb, PEER_BLOCK, PEER_HEADS, PEER_TOPK),
                        gate.reshape(nb, PEER_BLOCK, PEER_HEADS, PEER_TOPK)))
    return y.reshape(bsz, seq, d)

def setup_inputs(seed: int = 0) -> dict:
    key = jax.random.key(seed)
    ks = jax.random.split(key, 16)
    f32 = jnp.float32
    nrm = lambda k, shape, s: jax.random.normal(k, shape, f32) * s
    x = jax.random.normal(ks[0], (BATCH, SEQ, D_MODEL), f32)
    norm_mix_g = 1.0 + nrm(ks[1], (DEPTH, D_MODEL), 0.02)
    w_in = nrm(ks[2], (DEPTH, D_MODEL, D_IN_PROJ), D_MODEL ** -0.5)
    b_igate = nrm(ks[3], (DEPTH, MLSTM_HEADS), 0.1)
    b_fgate = jnp.linspace(3.0, 6.0, MLSTM_HEADS, dtype=f32)[None, :] + nrm(ks[4], (DEPTH, MLSTM_HEADS), 0.1)
    conv_w = nrm(ks[5], (DEPTH, CONV_WIDTH, D_CONV), CONV_WIDTH ** -0.5)
    mlstm_norm_g = 1.0 + nrm(ks[6], (DEPTH, D_MLSTM), 0.02)
    w_out = nrm(ks[7], (DEPTH, D_MIX, D_MODEL), D_MIX ** -0.5)
    norm_ffn_g = 1.0 + nrm(ks[8], (DEPTH, D_MODEL), 0.02)
    w_query = nrm(ks[9], (DEPTH, D_MODEL, PEER_HEADS * D_KEY), D_MODEL ** -0.5)
    sub_keys_1 = nrm(ks[10], (DEPTH, N_KEYS, D_KEY // 2), (D_KEY // 2) ** -0.5)
    sub_keys_2 = nrm(ks[11], (DEPTH, N_KEYS, D_KEY // 2), (D_KEY // 2) ** -0.5)
    expert_u = nrm(ks[12], (DEPTH, N_EXPERTS, D_MODEL), D_MODEL ** -0.5)
    expert_v = nrm(ks[13], (DEPTH, N_EXPERTS, D_MODEL), PEER_HEADS ** -0.5)
    norm_final_g = 1.0 + nrm(ks[14], (D_MODEL,), 0.02)
    return {"x": x, "norm_mix_g": norm_mix_g, "w_in": w_in, "b_igate": b_igate,
            "b_fgate": b_fgate, "conv_w": conv_w, "mlstm_norm_g": mlstm_norm_g,
            "w_out": w_out, "norm_ffn_g": norm_ffn_g, "w_query": w_query,
            "sub_keys_1": sub_keys_1, "sub_keys_2": sub_keys_2, "expert_u": expert_u,
            "expert_v": expert_v, "norm_final_g": norm_final_g}

def reference(x, norm_mix_g, w_in, b_igate, b_fgate, conv_w, mlstm_norm_g, w_out,
              norm_ffn_g, w_query, sub_keys_1, sub_keys_2, expert_u, expert_v, norm_final_g):
    bsz, seq, _ = x.shape
    split_points = [D_CONV, 2 * D_CONV, 3 * D_CONV,
                    3 * D_CONV + D_MLSTM, 3 * D_CONV + 2 * D_MLSTM,
                    3 * D_CONV + 3 * D_MLSTM, 3 * D_CONV + 4 * D_MLSTM,
                    3 * D_CONV + 4 * D_MLSTM + MLSTM_HEADS]
    for layer in range(DEPTH):
        xn = rmsnorm(x, norm_mix_g[layer])
        proj = xn @ w_in[layer]
        cx, cb, cc, q, k, v, o, ig, fg = jnp.split(proj, split_points, axis=-1)
        conv_out = short_conv_mixer(cx, cb, cc, conv_w[layer])

        shp = (bsz, seq, MLSTM_HEADS, MLSTM_HEAD_DIM)
        qf = q.reshape(shp).astype(jnp.float32)
        kf = k.reshape(shp).astype(jnp.float32) * (MLSTM_HEAD_DIM ** -0.5)
        vf = v.reshape(shp).astype(jnp.float32)
        i_pre = (ig + b_igate[layer]).astype(jnp.float32)
        log_f = jax.nn.log_sigmoid((fg + b_fgate[layer]).astype(jnp.float32))
        h = mlstm_chunkwise(qf, kf, vf, i_pre, log_f)
        h = h * lax.rsqrt(jnp.mean(h * h, axis=-1, keepdims=True) + EPS)
        h = h.reshape(bsz, seq, D_MLSTM) * mlstm_norm_g[layer].astype(jnp.float32)
        mlstm_out = (jax.nn.sigmoid(o.astype(jnp.float32)) * h).astype(x.dtype)

        mix = jnp.concatenate([conv_out, mlstm_out], axis=-1) @ w_out[layer]
        x = x + mix
        xn2 = rmsnorm(x, norm_ffn_g[layer])
        x = x + peer_ffn(xn2, w_query[layer], sub_keys_1[layer], sub_keys_2[layer],
                         expert_u[layer], expert_v[layer])
    return rmsnorm(x, norm_final_g)


_drawn_inputs = setup_inputs


def setup_inputs(seed=0):
    import zlib

    import numpy as np

    out = dict(_drawn_inputs(seed))
    spreads = {}
    factors = {'b_igate': 200.0, 'mlstm_norm_g': 11.384, 'norm_final_g': 21.516, 'norm_ffn_g': 11.915}
    for name, (base, spread) in spreads.items():
        noise = np.random.default_rng([zlib.crc32(name.encode()), seed]).standard_normal(out[name].shape)
        drawn = base * np.exp(spread * noise) if base else spread * noise
        out[name] = __import__('jax').numpy.asarray(drawn.astype(out[name].dtype))
    for name, factor in factors.items():
        out[name] = (out[name] * factor).astype(out[name].dtype)
    return out
```

```python
from contextlib import ExitStack

import concourse.bass as bass
from concourse import mybir

ALU = mybir.AluOpType
ACT = mybir.ActivationFunctionType
AX_X = mybir.AxisListType.X
F32 = mybir.dt.float32
F32R = mybir.dt.float32r
BF16 = mybir.dt.bfloat16
U32 = mybir.dt.uint32

P = 128
EPS = 1e-6
LOWEST = -3.4028234663852886e38


def hybrid_layer(nc, x, norm_mix_g, w_in, b_igate, b_fgate, conv_w, mlstm_norm_g, w_out, norm_ffn_g,
                 w_query, sub_keys_1, sub_keys_2, expert_u, expert_v, norm_final_g, out):
    T, D = x.shape[1], x.shape[2]
    TT = T // P
    C = D // P
    NH = b_igate.shape[1]
    DC = conv_w.shape[2]
    DM = mlstm_norm_g.shape[1]
    DH = DM // NH
    NK, DK = sub_keys_1.shape[1], sub_keys_1.shape[2]
    NE = expert_u.shape[1]
    TILES = NE // P
    PH = w_query.shape[2] // (2 * DK)
    TOPK = 16
    PICKS = PH * TOPK
    UW = 1024
    UC = UW // P
    GATES = 2 * NH
    assert (T, D, TILES, PICKS, NK, DK) == (256, 2048, 128, 128, 128, 128) and DC == DM == UW

    RAWS = 4
    GU = 2
    PASSES_IN = ["q", "k", "v", "o", "cx", "cc", "cb"]
    COLUMN = {"cx": 0, "cb": DC, "cc": 2 * DC, "q": 3 * DC, "k": 3 * DC + DM, "v": 3 * DC + 2 * DM,
              "o": 3 * DC + 3 * DM}
    NIN = len(PASSES_IN)
    PASSES = NIN + 4
    NPU = GU + C * PASSES
    NUU = 2 * TILES
    unit0 = lambda p: GU + C * p

    def slot_of(n):
        return n % RAWS

    def landed_at(n):
        return 16 * (n // RAWS + 1)

    w_in2, w_out2, w_query2 = w_in[0], w_out[0], w_query[0]
    x2 = x[0].rearrange("(a p) d -> p a d", p=P)
    out2 = out[0].rearrange("(a p) d -> p a d", p=P)
    u_rows = expert_u[0].rearrange("(i p) d -> p i d", p=P)
    v_rows = expert_v[0].rearrange("(i p) d -> p i d", p=P)

    def pass_weights(p):
        if p < NIN:
            w, c0 = w_in2, COLUMN[PASSES_IN[p]]
        elif p < NIN + 2:
            w, c0 = w_out2, (p - NIN) * UW
        else:
            w, c0 = w_query2, (p - NIN - 2) * UW
        return w.rearrange("(k r) n -> r k n", r=P)[:, :, c0:c0 + UW]

    gate_cols = w_in2.rearrange("(k r) n -> r k n", r=P)[:, :, w_in2.shape[1] - P:w_in2.shape[1]]

    with ExitStack() as ctx:
        def sb(name, shape, dt=F32):
            return ctx.enter_context(nc.sbuf_tensor(name, shape, dt))

        def sem(name):
            return ctx.enter_context(nc.semaphore(name))

        x1_kept = nc.dram_tensor("x1_kept", (P, TT * D), F32, kind="Internal").ap()

        A = sb("A", [P, TILES * T])
        A3 = A[:, :].rearrange("p (i t) -> p i t", t=T)
        x_hi = sb("x_hi", [P, C * T], F32R)
        x_lo = sb("x_lo", [P, C * T], F32R)
        w_hi = sb("w_hi", [P, 2, UW], F32R)
        w_lo = sb("w_lo", [P, 2, UW], F32R)
        raw = sb("raw", [P, RAWS, UW])
        xh3 = x_hi[:, :].rearrange("p (c t) -> p c t", t=T)
        xl3 = x_lo[:, :].rearrange("p (c t) -> p c t", t=T)
        v_hi = x_hi[:, :].rearrange("p (s n) -> p s n", n=UW)
        v_lo = x_lo[:, :].rearrange("p (s n) -> p s n", n=UW)
        a_hi = w_hi[:, :, 0:T]
        a_lo = w_lo[:, :, 0:T]

        ident = sb("ident", [P, P])
        iota = sb("iota", [P, P], BF16)
        picks = sb("picks", [P, 5, T], BF16)
        hot = sb("hot", [P, 2, 4, 4, P], BF16)
        act_out = sb("act_out", [P, 2, T])
        COLS = 2 * C + UC + 3 * UC
        cols = sb("cols", [P, COLS])
        g_mix, g_ffn = cols[:, 0:C], cols[:, C:2 * C]
        g_ml = cols[:, 2 * C:2 * C + UC]
        taps = cols[:, 2 * C + UC:].rearrange("p (w c) -> p w c", w=3)
        bias_i = sb("bias_i", [NH, 1])
        bias_f = sb("bias_f", [NH, 1])
        stat = sb("stat", [P, 64])

        area = [0]

        def work(words):
            a = A[:, area[0]:area[0] + words]
            area[0] += words
            assert area[0] <= TILES * T
            return a

        proj = {}
        for name in PASSES_IN:
            proj[name] = work(UC * T).rearrange("p (c t) -> p c t", t=T)
        x_res = work(TT * D).rearrange("p (a d) -> p a d", a=TT)
        xs = work(TT * D).rearrange("p (a d) -> p a d", a=TT)
        mixT = work(C * T).rearrange("p (c t) -> p c t", t=T)
        v_nat = work(TT * NH * (DH + 1)).rearrange("p (a h v) -> p a h v", a=TT, h=NH)
        sw = work(NH * 384).rearrange("p (h j) -> p h j", h=NH)
        causal = work(384)
        gate_acc = work(T)
        gate_nat = work(TT * GATES).rearrange("p (a g) -> p a g", a=TT)
        rows = mixT[:, UC:UC + 8, :]
        col_rows = work(P)[0:COLS, :]
        select = work(NH * P).rearrange("p (h m) -> p h m", h=NH)
        aN = work(TT * NH).rearrange("p (a h) -> p a h", a=TT)
        limN = work(TT * NH).rearrange("p (a h) -> p a h", a=TT)
        h_nat = xs.rearrange("p a (h v) -> p a h v", v=DH)[:, :, 0:NH, :]
        mixoT = A[:, 0:C * T].rearrange("p (c t) -> p c t", t=T)
        at = C * T
        qT = A[:, at:at + C * T].rearrange("p (c t) -> p c t", t=T)
        at += C * T
        scores = A[:, at:at + 2 * PH * TT * NK].rearrange("p (g n) -> p g n", n=NK)
        at += 2 * PH * TT * NK
        assert at <= NIN * UC * T
        at = NIN * UC * T + 2 * TT * D
        cand = A[:, at:at + TT * PH * 256].rearrange("p (g n) -> p g n", n=256)
        at += TT * PH * 256
        left = A[:, at:at + 512].rearrange("p (s n) -> p s n", n=256)
        at += 512
        keys = A[:, at:at + 2 * DK].rearrange("p (s d) -> p s d", s=2)
        at += 2 * DK
        keysT = A[:, at:at + 2 * NK].rearrange("p (s n) -> p s n", s=2)
        at += 2 * NK
        top_v = A[:, at:at + 2 * PH * TT * TOPK].rearrange("p (g k) -> p g k", k=TOPK)
        at += 2 * PH * TT * TOPK
        top_i = A[:, at:at + 2 * PH * TT * TOPK].bitcast(U32).rearrange("p (g k) -> p g k", k=TOPK)
        at += 2 * PH * TT * TOPK
        top_f = A[:, at:at + 2 * PH * TT * TOPK].rearrange("p (g k) -> p g k", k=TOPK)
        at += 2 * PH * TT * TOPK
        best_v = A[:, at:at + TT * PICKS].rearrange("p (g k) -> p g k", k=TOPK)
        at += TT * PICKS
        best_i = A[:, at:at + TT * PICKS].bitcast(U32).rearrange("p (g k) -> p g k", k=TOPK)
        at += TT * PICKS
        half_i = A[:, at:at + 2 * TT * PICKS].bitcast(U32).rearrange("p (s g) -> p s g", s=2)
        at += 2 * TT * PICKS
        half_f = A[:, at:at + 2 * TT * PICKS].rearrange("p (s g) -> p s g", s=2)
        at += 2 * TT * PICKS
        assert at <= TILES * T, at
        match = A[:, 0:TT * PICKS * TOPK].rearrange("p (g k a) -> p g k a", k=TOPK, a=TOPK)
        found = A[:, 4096:4096 + 3 * TT * PICKS].rearrange("p (s g) -> p s g", s=3)
        iota16 = A[:, 5120:5120 + TOPK]
        shifted = A[:, 5376:5376 + TT * PICKS].rearrange("p (g k) -> p g k", k=TOPK)
        total = A[:, 5888:5888 + TT * PH]
        rest = A[:, 6144:6144 + 3 * T].rearrange("p (s t) -> p s t", s=3)
        x1_back = A[:, 0:TT * D].rearrange("p (a d) -> p a d", a=TT)
        g_final = A[:, TT * D:TT * D + D]
        y_out = A[:, TT * D + D:2 * TT * D + D].rearrange("p (a d) -> p a d", a=TT)
        FREED = (2 * TT * D + D) // T + 2

        ps = ctx.enter_context(nc.psum_tensor("ps", [P, 8, 512], F32))
        flat = ps[:, :, :].rearrange("p b n -> p (b n)")
        chunks16 = flat.rearrange("p (c t) -> p c t", t=T)
        natural = flat.rearrange("p (a d) -> p a d", a=TT)

        raw_landed = [sem(f"raw_landed{i}") for i in range(RAWS)]
        x_landed, small_landed, keys_landed = sem("x_landed"), sem("small_landed"), sem("keys_landed")
        cols_turned, cols_ready = sem("cols_turned"), sem("cols_ready")
        constants, masks = sem("constants"), sem("masks")
        squares_done, mean_done, root_done, rstd_done = (sem("squares_done"), sem("mean_done"),
                                                         sem("root_done"), sem("rstd_done"))
        newton, scaled, turned, hi_taken, lo_taken = (sem("newton"), sem("scaled"), sem("turned"),
                                                      sem("hi_taken"), sem("lo_taken"))
        hi_split, lo_split, unit_done, pass_out = (sem("hi_split"), sem("lo_split"), sem("unit_done"),
                                                   sem("pass_out"))
        gates_out, gate_step_pe, gate_step_act, gate_step_dve = (
            sem("gates_out"), sem("gate_step_pe"), sem("gate_step_act"), sem("gate_step_dve"))
        v_turned, v_ready, qk_done, expo_in, expo_out, sw_half, sw_ready, pv_done = (
            sem("v_turned"), sem("v_ready"), sem("qk_done"), sem("expo_in"), sem("expo_out"),
            sem("sw_half"), sem("sw_ready"), sem("pv_done"))
        den_ready, h_scaled, h_squared, h_rstd, h_ready, h_turned = (
            sem("den_ready"), sem("h_scaled"), sem("h_squared"), sem("h_rstd"), sem("h_ready"), sem("h_turned"))
        o_sigmoid, conv_step, mix_ready = sem("o_sigmoid"), sem("conv_step"), sem("mix_ready")
        mixo_turned, x1_ready, x1_stored = sem("mixo_turned"), sem("x1_ready"), sem("x1_stored")
        keys_turned, keysT_ready, s_done, s_copied = (sem("keys_turned"), sem("keysT_ready"),
                                                      sem("s_done"), sem("s_copied"))
        top_step, soft_in, soft_out, found_ready, found_turned, picks_ready = (
            sem("top_step"), sem("soft_in"), sem("soft_out"), sem("found_ready"), sem("found_turned"),
            sem("picks_ready"))
        hot_ready, gate_block, gate_stored = sem("hot_ready"), sem("gate_block"), sem("gate_stored")
        u_turned, uh_split, ul_split, u_done, gelu_done, gated = (
            sem("u_turned"), sem("uh_split"), sem("ul_split"), sem("u_done"), sem("gelu_done"), sem("gated"))
        ah_ready, al_ready, vh_split, vl_split, v_done = (
            sem("ah_ready"), sem("al_ready"), sem("vh_split"), sem("vl_split"), sem("v_done"))
        tail_landed, x2_ready, out_ready, out_stored = (
            sem("tail_landed"), sem("x2_ready"), sem("out_ready"), sem("out_stored"))

        HEADS = range(NH)
        TB = T // 4
        NORM_MIX, NORM_FFN, NORM_FINAL = range(3)
        SSQ, MS, ROOT, INV, TMP = (stat[:, 0:TT], stat[:, 2:2 + TT], stat[:, 4:4 + TT],
                                   stat[:, 6:6 + TT], stat[:, 8:8 + TT])
        HN = TT * NH
        NQ, DEN, HSS, HMS, HROOT, HINV, HTMP = (stat[:, 10 + HN * i - 2:10 + HN * i - 2 + HN]
                                                for i in range(7))

        with nc.Block() as block:

            @block.sync
            def _(sp):
                sp.dma_start(x_res, x2).then_inc(x_landed, 16)
                for n in range(GU):
                    sp.dma_start(raw[:, slot_of(n), :].rearrange("p (k m) -> p k m", m=P),
                                 gate_cols[:, n * UC:(n + 1) * UC, :]).then_inc(raw_landed[slot_of(n)], 16)
                for p in range(PASSES):
                    w = pass_weights(p)

                    def load(u, k, j):
                        sp.dma_start(raw[:, slot_of(unit0(p) + j), :], w[:, k, :])\
                            .then_inc(raw_landed[slot_of(unit0(p) + j)], 16)

                    for j in range(RAWS):
                        if unit0(p) + j >= RAWS:
                            sp.wait_ge(lo_split, unit0(p) + j - RAWS + 1)
                        load(unit0(p) + j, j, j)
                    with sp.Fori(1, C // RAWS) as it:
                        for j in range(RAWS):
                            sp.wait_ge(lo_split, it * RAWS + (unit0(p) + j - RAWS + 1))
                            sp.dma_start(raw[:, slot_of(unit0(p) + j), :],
                                         w[:, bass.ds(it * RAWS + j, 1), :])\
                                .then_inc(raw_landed[slot_of(unit0(p) + j)], 16)
                for n in range(RAWS):
                    sp.wait_ge(lo_split, NPU + n - RAWS + 1)
                    sp.dma_start(raw[:, slot_of(NPU + n), :], u_rows[:, n // 2, (n % 2) * UW:(n % 2 + 1) * UW])\
                        .then_inc(raw_landed[slot_of(NPU + n)], 16)
                with sp.Fori(1, NUU // RAWS) as it:
                    for j in range(RAWS):
                        sp.wait_ge(u_turned, it * RAWS + (j - RAWS + 1))
                        sp.dma_start(raw[:, slot_of(NPU + j), :],
                                     u_rows[:, bass.ds(it * 2 + j // 2, 1), (j % 2) * UW:(j % 2 + 1) * UW])\
                            .then_inc(raw_landed[slot_of(NPU + j)], 16)
                for n in range(RAWS):
                    sp.wait_ge(u_turned, NUU + n - RAWS + 1)
                    sp.dma_start(raw[:, slot_of(NPU + n), :], v_rows[:, n // 2, (n % 2) * UW:(n % 2 + 1) * UW])\
                        .then_inc(raw_landed[slot_of(NPU + n)], 16)
                with sp.Fori(1, NUU // RAWS) as it:
                    for j in range(RAWS):
                        sp.wait_ge(vl_split, it * RAWS + (j - RAWS + 1))
                        sp.dma_start(raw[:, slot_of(NPU + j), :],
                                     v_rows[:, bass.ds(it * 2 + j // 2, 1), (j % 2) * UW:(j % 2 + 1) * UW])\
                            .then_inc(raw_landed[slot_of(NPU + j)], 16)
                for a in range(TT):
                    sp.wait_ge(out_ready, a + 1)
                    sp.dma_start(out2[:, a, :], y_out[:, a, :]).then_inc(out_stored, 16)
                sp.wait_ge(out_stored, 16 * TT)

            @block.gpsimd
            def _(pool):
                pool.memset(ident[:, :], 0.0).then_inc(constants, 1)
                pool.iota(iota[:, :], [[1, P]], base=0, channel_multiplier=0,
                          allow_small_or_imprecise_dtypes=True).then_inc(constants, 1)
                pool.wait_ge(constants, 2)
                pool.affine_select(out=ident[:, :], in_=ident[:, :], compare_op=ALU.not_equal, fill=1.0,
                                   base=0, pattern=[[-1, P]], channel_multiplier=1).then_inc(constants, 1)
                pool.memset(causal, 1.0).then_inc(masks, 1)
                pool.memset(select, 0.0).then_inc(masks, 1)
                pool.wait_ge(masks, 2)
                for c0 in (0, 2 * P):
                    pool.affine_select(out=causal[:, c0:c0 + P], in_=causal[:, c0:c0 + P], compare_op=ALU.is_ge,
                                       fill=0.0, base=0, pattern=[[1, P]], channel_multiplier=-1)\
                        .then_inc(masks, 1)
                pool.affine_select(out=select, in_=select, compare_op=ALU.not_equal, fill=1.0, base=0,
                                   pattern=[[-1, NH], [0, P]], channel_multiplier=1).then_inc(masks, 1)
                pool.wait_ge(x1_ready, TT)
                pool.dma_start(x1_kept, x_res.rearrange("p a d -> p (a d)")).then_inc(x1_stored, 16)
                pool.wait_ge(x1_stored, 16)
                pool.wait_ge(al_ready, FREED)
                pool.dma_start(x1_back.rearrange("p a d -> p (a d)"), x1_kept).then_inc(tail_landed, 16)
                pool.dma_start(g_final, norm_final_g.rearrange("(o d) -> o d", o=1).broadcast_to([P, D]))\
                    .then_inc(tail_landed, 16)

            @block.tensor
            def _(pe):
                def turn_x(round_no):
                    if round_no == NORM_MIX:
                        pe.wait_ge(small_landed, 16 * 8)
                        nc.tensor.transpose(ps[:, 7, 0:COLS], col_rows, ident[0:COLS, 0:COLS]).then_inc(cols_turned, 1)
                    pe.wait_ge(scaled, TT * (round_no + 1))
                    for c in range(C):
                        for a in range(TT):
                            last = nc.tensor.transpose(chunks16[:, c, a * P:(a + 1) * P],
                                                       xs[:, a, c * P:(c + 1) * P], ident[:, :])
                        if c % 2 == 1:
                            last.then_inc(turned, 1)
                        if c == C - 3 and round_no == NORM_MIX:
                            pe.wait_ge(cols_ready, 1)

                def project(p):
                    acc = flat[:, (p % 2) * 2048:(p % 2 + 1) * 2048]

                    def unit(u_wait, k, j, first, final):
                        s = (unit0(p) + j) % 2
                        pe.wait_ge(lo_split, u_wait)
                        for c in range(UC):
                            for n, (w, xx) in enumerate(((w_hi, xh3), (w_hi, xl3), (w_lo, xh3))):
                                last = nc.tensor.matmul(
                                    acc[:, c * T:(c + 1) * T], w[:, s, c * P:(c + 1) * P], xx[:, k, :],
                                    start=first and n == 0 and c % 2 == 0, stop=final and n == 2,
                                    skip_group_check=True)
                        last.then_inc(unit_done, 1)

                    if p >= 2 and p < NIN:
                        pe.wait_ge(pass_out, p - 1)
                    for j in range(RAWS):
                        unit(unit0(p) + j + 1, j, j, j == 0, False)
                    with pe.Fori(1, C // RAWS) as it:
                        for j in range(RAWS):
                            unit(it * RAWS + (unit0(p) + j + 1), bass.ds(it * RAWS + j, 1), j, False, False)

                pe.wait_ge(constants, 3)
                turn_x(NORM_MIX)
                pe.wait_ge(lo_taken, C)
                pe.wait_ge(hi_taken, C)
                for n in range(GU):
                    pe.wait_ge(lo_split, n + 1)
                    for c in range(UC):
                        for m, (w, xx) in enumerate(((w_hi, xh3), (w_hi, xl3), (w_lo, xh3))):
                            last = nc.tensor.matmul(ps[:, 4, 0:T], w[:, n % 2, c * P:(c + 1) * P],
                                                    xx[:, n * UC + c, :], start=n == 0 and c == 0 and m == 0,
                                                    stop=n == GU - 1 and c == UC - 1 and m == 2)
                    last.then_inc(unit_done, 1)
                for p in range(NIN):
                    if p == 1:
                        pe.wait_ge(gates_out, 1)
                    project(p)

                pe.wait_ge(pass_out, NIN)
                for a in range(TT):
                    last = nc.tensor.transpose(ps[:, 5, a * P:(a + 1) * P], gate_acc[:, a * P:(a + 1) * P],
                                               ident[:, :])
                last.then_inc(gate_step_pe, 1)
                for a in range(TT):
                    for c in range(UC):
                        last = nc.tensor.transpose(natural[:, 0, a * DM + c * P:a * DM + (c + 1) * P],
                                                   proj["v"][:, c, a * P:(a + 1) * P], ident[:, :])
                    last.then_inc(v_turned, 1)
                pe.wait_ge(gate_step_act, 1)
                for g in range(2):
                    for a in range(TT):
                        last = nc.tensor.transpose(ps[0:NH, 6, g * T + a * P:g * T + (a + 1) * P],
                                                   gate_nat[:, a, g * NH:(g + 1) * NH], ident[:, :])
                last.then_inc(gate_step_pe, 1)
                pe.wait_ge(v_ready, TT + 1)
                for h in HEADS:
                    for l, j0, o in ((0, 0, 0), (1, P, T)):
                        for c in range(DH // P):
                            last = nc.tensor.matmul(ps[:, h, o:o + T - j0],
                                                    proj["k"][:, h * DH // P + c, l * P:(l + 1) * P],
                                                    proj["q"][:, h * DH // P + c, j0:T],
                                                    start=c == 0, stop=c == DH // P - 1)
                    last.then_inc(qk_done, 1)
                pe.wait_ge(gate_step_dve, 10)
                pe.wait_ge(masks, 5)
                for h in HEADS:
                    last = nc.tensor.matmul(ps[:, 4 + h // 2, (h % 2) * T:(h % 2 + 1) * T], select[0:NH, h, :],
                                            rows[0:NH, 4, :], start=True, stop=True)
                last.then_inc(gate_step_pe, 1)
                pe.wait_ge(gate_step_act, 4)
                for r, o in ((3, 0), (6, TT * NH)):
                    for a in range(TT):
                        last = nc.tensor.transpose(ps[:, 7, o + a * NH:o + (a + 1) * NH],
                                                   rows[0:NH, r, a * P:(a + 1) * P], ident[0:NH, 0:NH])
                last.then_inc(gate_step_pe, 1)
                pe.wait_ge(sw_ready, NH)
                for jt in range(TT):
                    for h in HEADS:
                        o = ps[:, (4 if jt == 0 else 0) + h, 0:DH + 1]
                        if jt == 0:
                            last = nc.tensor.matmul(o, sw[:, h, 0:P], v_nat[:, 0, h, :], start=True, stop=True)
                        else:
                            nc.tensor.matmul(o, sw[:, h, P:T], v_nat[:, 0, h, :], start=True, stop=False)
                            last = nc.tensor.matmul(o, sw[:, h, T:T + P], v_nat[:, 1, h, :], start=False, stop=True)
                        last.then_inc(pv_done, 1)
                pe.wait_ge(h_ready, HN)
                for c in range(UC):
                    for a in range(TT):
                        last = nc.tensor.transpose(
                            chunks16[:, c, a * P:(a + 1) * P],
                            h_nat[:, a, c * P // DH, c * P % DH:c * P % DH + P], ident[:, :])
                last.then_inc(h_turned, 1)

                pe.wait_ge(lo_taken, C + 2)
                for p in (NIN, NIN + 1):
                    project(p)
                pe.wait_ge(pass_out, NIN + 2)
                for a in range(TT):
                    for c in range(C):
                        last = nc.tensor.transpose(natural[:, a, c * P:(c + 1) * P],
                                                   mixoT[:, c, a * P:(a + 1) * P], ident[:, :])
                    last.then_inc(mixo_turned, 1)
                turn_x(NORM_FFN)
                pe.wait_ge(lo_taken, C + 2 + C)
                pe.wait_ge(hi_taken, C + 2 + C)
                for p in (NIN + 2, NIN + 3):
                    project(p)
                pe.wait_ge(pass_out, NIN + 4)
                pe.wait_ge(keys_landed, 32)
                for s in range(2):
                    last = nc.tensor.transpose(ps[:, 0, s * P:(s + 1) * P], keys[:, s, :], ident[:, :])
                last.then_inc(keys_turned, 1)
                pe.wait_ge(keysT_ready, 1)
                for a in range(TT):
                    for g in range(2 * PH):
                        last = nc.tensor.matmul(natural[:, a, g * NK:(g + 1) * NK], qT[:, g, a * P:(a + 1) * P],
                                                keysT[:, g % 2, :], start=True, stop=True)
                    last.then_inc(s_done, 1)
                pe.wait_ge(s_copied, TT)
                pe.wait_ge(found_ready, 1)
                for s in range(3):
                    for a in range(TT):
                        last = nc.tensor.transpose(flat[:, s * T + a * P:s * T + (a + 1) * P],
                                                   found[:, s, a * PICKS:(a + 1) * PICKS], ident[:, :])
                last.then_inc(found_turned, 1)
                pe.wait_ge(picks_ready, 3)

                def gate_tokens(b, wait_hot, wait_stored):
                    pe.wait_ge(hot_ready, wait_hot)
                    if wait_stored is not None:
                        pe.wait_ge(gate_stored, wait_stored)
                    for t in range(4):
                        for part in range(3):
                            last = nc.tensor.matmul(ps[:, b, t * P:(t + 1) * P], hot[:, b, t, 1 + part, :],
                                                    hot[:, b, t, 0, :], start=t == 0 and part == 0,
                                                    stop=t == 3 and part == 2, skip_group_check=True)
                    last.then_inc(gate_block, 1)

                for b in range(2):
                    gate_tokens(b, b + 1, None)
                with pe.Fori(1, TB // 2) as it:
                    for b in range(2):
                        gate_tokens(b, it * 2 + (b + 1), it * 2 + (b - 1))

                pe.wait_ge(gate_stored, TB)

                def turn_unit(j, landed, free):
                    pe.wait_ge(raw_landed[slot_of(NPU + j)], landed)
                    if free is not None:
                        pe.wait_ge(ul_split, free)
                    o = (j % 2) * UW
                    for c in range(UC):
                        last = nc.tensor.transpose(flat[:, o + c * P:o + (c + 1) * P],
                                                   raw[:, slot_of(NPU + j), c * P:(c + 1) * P], ident[:, :])
                    last.then_inc(u_turned, 1)

                def score_unit(j, ready, free):
                    pe.wait_ge(ul_split, ready)
                    if free is not None:
                        pe.wait_ge(gelu_done, free)
                    s = (NPU + j) % 2
                    half = j % 2
                    for c in range(UC):
                        for n, (w, xx) in enumerate(((w_hi, xh3), (w_hi, xl3), (w_lo, xh3))):
                            last = nc.tensor.matmul(ps[:, 4 + j // 2 % 2, 0:T], w[:, s, c * P:(c + 1) * P],
                                                    xx[:, half * UC + c, :],
                                                    start=half == 0 and c == 0 and n == 0,
                                                    stop=half == 1 and c == UC - 1 and n == 2)
                    last.then_inc(u_done, 1)

                for n in range(RAWS):
                    if n == 0:
                        turn_unit(0, landed_at(NPU), None)
                    if n < RAWS - 1:
                        turn_unit(n + 1, landed_at(NPU + n + 1), n if n >= 1 else None)
                        score_unit(n, n + 1, None)
                with pe.Fori(1, NUU // RAWS) as it:
                    for j in range(RAWS):
                        turn_unit(j, it * 16 + landed_at(NPU + j), it * RAWS + (j - 1))
                        b = (j - 1) % RAWS
                        score_unit(b, it * RAWS + j, it * 2 + ((j - 1) // 2 - 1) if j != 0 else None)
                score_unit(RAWS - 1, NUU, None)

                pe.wait_ge(gelu_done, TILES)

                def sum_unit(j, v_ok, a_ok, first):
                    pe.wait_ge(vl_split, v_ok)
                    if j % 2 == 0:
                        pe.wait_ge(al_ready, a_ok)
                    half, s, v = j % 2, j // 2 % 2, (NPU + j) % RAWS
                    for a in range(TT):
                        for n, (aa, vv) in enumerate(((a_hi, v_hi), (a_hi, v_lo), (a_lo, v_hi))):
                            for q in range(UW // 512):
                                last = nc.tensor.matmul(
                                    ps[:, a * 4 + half * 2 + q, :], aa[:, s, a * P:(a + 1) * P],
                                    vv[:, v, q * 512:(q + 1) * 512], start=first and n == 0, stop=False,
                                    skip_group_check=True)
                    last.then_inc(v_done, 1)

                for n in range(RAWS):
                    sum_unit(n, n + 1, n // 2 + 1, n < 2)
                with pe.Fori(1, NUU // RAWS) as it:
                    for j in range(RAWS):
                        sum_unit(j, it * RAWS + (j + 1), it * 2 + (j // 2 + 1), False)

            @block.scalar
            def _(act):
                row = 0
                for v in (norm_mix_g[0], norm_ffn_g[0], mlstm_norm_g[0], conv_w[0, 0], conv_w[0, 1], conv_w[0, 2]):
                    n = v.shape[0] // P
                    act.dma_start(col_rows[row:row + n, :], v.rearrange("(c p) -> c p", p=P))\
                        .then_inc(small_landed, 16)
                    row += n
                act.dma_start(bias_i[:, :], b_igate.rearrange("o h -> h o")).then_inc(small_landed, 16)
                act.dma_start(bias_f[:, :], b_fgate.rearrange("o h -> h o")).then_inc(small_landed, 16)

                def squares_of(src, junk, round_no):
                    for a in range(TT):
                        nc.scalar.activation(junk[a], src[:, a, :], ACT.Square,
                                             accum_out=SSQ[:, a:a + 1]).then_inc(squares_done, 1)
                    act.wait_ge(mean_done, round_no + 1)
                    nc.scalar.activation(ROOT, MS, ACT.Sqrt).then_inc(root_done, 1)

                def take_hi(gain, round_no, before):
                    for c in range(C):
                        if c % 2 == 0:
                            act.wait_ge(turned, C // 2 * round_no + c // 2 + 1)
                        nc.scalar.activation(xh3[:, c, :], chunks16[:, c, :], ACT.Copy, scale=gain[:, c:c + 1])\
                            .then_inc(hi_taken, 1)

                def hi_unit(u_landed, j, free, n0):
                    act.wait_ge(raw_landed[slot_of(n0 + j)], u_landed)
                    if free is not None:
                        act.wait_ge(unit_done, free)
                    nc.scalar.activation(w_hi[:, (n0 + j) % 2, :], raw[:, slot_of(n0 + j), :], ACT.Copy)\
                        .then_inc(hi_split, 1)

                def evacuate(p, dst, scale=1.0):
                    act.wait_ge(unit_done, unit0(p) + C)
                    h = (p % 2) * 2048
                    for q in range(2):
                        last = nc.scalar.activation(
                            dst[:, 4 * q:4 * q + 4, :],
                            flat[:, h + q * 1024:h + (q + 1) * 1024].rearrange("p (c t) -> p c t", t=T),
                            ACT.Copy, scale=scale)
                    last.then_inc(pass_out, 1)

                def pass_hi_first(p):
                    for j in range(RAWS):
                        n = unit0(p) + j
                        hi_unit(landed_at(n), j, n - 1 if n >= 2 else None, unit0(p))

                def pass_hi_rest(p):
                    with act.Fori(1, C // RAWS) as it:
                        for j in range(RAWS):
                            n = unit0(p) + j
                            hi_unit(it * 16 + landed_at(n), j, it * RAWS + (n - 1), unit0(p))

                act.wait_ge(x_landed, 16)
                squares_of(x_res, [xs[:, a, :] for a in range(TT)], NORM_MIX)
                act.wait_ge(cols_turned, 1)
                nc.scalar.activation(cols[:, :], ps[:, 7, 0:COLS], ACT.Copy).then_inc(cols_ready, 1)
                act.wait_ge(cols_ready, 1)
                take_hi(g_mix, NORM_MIX, 0)
                for n in range(GU):
                    hi_unit(landed_at(n), n, None, 0)
                for p in range(NIN):
                    pass_hi_first(p)
                    if p == 0:
                        act.wait_ge(unit_done, GU)
                        nc.scalar.activation(gate_acc, ps[:, 4, 0:T], ACT.Copy).then_inc(gates_out, 1)
                    else:
                        evacuate(p - 1, proj[PASSES_IN[p - 1]], DH ** -0.5 if PASSES_IN[p - 1] == "k" else 1.0)
                    pass_hi_rest(p)
                evacuate(NIN - 1, proj[PASSES_IN[NIN - 1]])

                act.wait_ge(gate_step_pe, 1)
                nc.scalar.activation(gate_nat, ps[:, 5, 0:T].rearrange("p (a m) -> p a m", a=TT)[:, :, P - GATES:P],
                                     ACT.Copy).then_inc(gate_step_act, 1)
                for a in range(TT):
                    act.wait_ge(v_turned, a + 1)
                    nc.scalar.activation(v_nat[:, a, :, 0:DH],
                                         natural[:, 0, a * DM:(a + 1) * DM].rearrange("p (h v) -> p h v", v=DH),
                                         ACT.Copy).then_inc(v_ready, 1)
                act.wait_ge(gate_step_dve, 3)
                nc.scalar.activation(rows[0:NH, 5, :], rows[0:NH, 4, :], ACT.Exp, scale=-1.0)\
                    .then_inc(gate_step_act, 1)
                act.wait_ge(gate_step_dve, 4)
                nc.scalar.activation(rows[0:NH, 4, :], rows[0:NH, 6, :], ACT.Ln).then_inc(gate_step_act, 1)
                act.wait_ge(gate_step_dve, 11)
                nc.scalar.activation(rows[0:NH, 6, :], rows[0:NH, 5, :], ACT.Exp, scale=-1.0)\
                    .then_inc(gate_step_act, 1)
                for h in HEADS:
                    act.wait_ge(expo_in, h + 1)
                    nc.scalar.activation(sw[:, h, :], sw[:, h, :], ACT.Exp, scale=-1.0).then_inc(expo_out, 1)
                nc.scalar.activation(proj["o"], proj["o"], ACT.Sigmoid).then_inc(o_sigmoid, 1)
                for g in range(HN):
                    jt, h = g // NH, g % NH
                    act.wait_ge(den_ready, g + 1)
                    nc.scalar.activation(h_nat[:, jt, h, :], ps[:, (4 if jt == 0 else 0) + h, 0:DH], ACT.Copy,
                                         scale=DEN[:, g:g + 1]).then_inc(h_scaled, 1)
                for g in range(HN):
                    jt, h = g // NH, g % NH
                    act.wait_ge(h_scaled, g + 1)
                    nc.scalar.activation(v_nat[:, jt, h, 0:DH], h_nat[:, jt, h, :], ACT.Square,
                                         accum_out=HSS[:, g:g + 1]).then_inc(h_squared, 1)
                act.wait_ge(h_rstd, 1)
                nc.scalar.activation(HROOT, HMS, ACT.Sqrt).then_inc(h_squared, 1)
                for half in range(2):
                    act.wait_ge(unit_done, unit0(NIN))
                    act.wait_ge(mix_ready, half + 1)
                    nc.scalar.activation(xh3[:, half * UC:(half + 1) * UC, :], mixT[:, half * UC:(half + 1) * UC, :],
                                         ACT.Copy).then_inc(hi_taken, 1)
                pass_hi_first(NIN)
                pass_hi_rest(NIN)
                pass_hi_first(NIN + 1)
                evacuate(NIN, mixoT[:, 0:UC, :])
                pass_hi_rest(NIN + 1)
                evacuate(NIN + 1, mixoT[:, UC:2 * UC, :])
                for a in range(TT):
                    act.wait_ge(x1_ready, a + 1)
                squares_of(x_res, [xs[:, a, :] for a in range(TT)], NORM_FFN)
                for s, k in enumerate((sub_keys_1, sub_keys_2)):
                    act.dma_start(keys[:, s, :], k[0]).then_inc(keys_landed, 16)
                take_hi(g_ffn, NORM_FFN, C + 2)
                pass_hi_first(NIN + 2)
                pass_hi_rest(NIN + 2)
                pass_hi_first(NIN + 3)
                evacuate(NIN + 2, qT[:, 0:UC, :])
                pass_hi_rest(NIN + 3)
                evacuate(NIN + 3, qT[:, UC:2 * UC, :])
                act.wait_ge(keys_turned, 1)
                nc.scalar.activation(keysT, ps[:, 0, 0:2 * P].rearrange("p (s n) -> p s n", s=2), ACT.Copy)\
                    .then_inc(keysT_ready, 1)
                for a in range(TT):
                    act.wait_ge(s_done, a + 1)
                    nc.scalar.activation(scores[:, a * 2 * PH:(a + 1) * 2 * PH, :],
                                         natural[:, a, :].rearrange("p (g n) -> p g n", n=NK),
                                         ACT.Copy).then_inc(s_copied, 1)
                act.wait_ge(soft_in, 1)
                nc.scalar.activation(shifted, shifted, ACT.Exp).then_inc(soft_out, 1)

                act.wait_ge(x1_stored, 16)

                def store_gates(b, t0, wait):
                    act.wait_ge(gate_block, wait)
                    nc.scalar.activation(A3[:, :, t0], ps[:, b, :].rearrange("p (t i) -> p i t", t=4),
                                         ACT.Copy).then_inc(gate_stored, 1)

                for b in range(2):
                    store_gates(b, slice(4 * b, 4 * b + 4), b + 1)
                with act.Fori(1, TB // 2) as it:
                    for b in range(2):
                        store_gates(b, bass.ds(it * 8 + b * 4, 4), it * 2 + (b + 1))

                def u_hi(j, turned_at, free):
                    act.wait_ge(u_turned, turned_at)
                    if free is not None:
                        act.wait_ge(u_done, free)
                    nc.scalar.activation(w_hi[:, (NPU + j) % 2, :], flat[:, (j % 2) * UW:(j % 2 + 1) * UW], ACT.Copy)\
                        .then_inc(uh_split, 1)

                def gelu(b, done_at, free):
                    act.wait_ge(u_done, done_at)
                    if free is not None:
                        act.wait_ge(gated, free)
                    nc.scalar.activation(act_out[:, b, :], ps[:, 4 + b, 0:T], ACT.Gelu).then_inc(gelu_done, 1)

                u_hi(0, 1, None)
                u_hi(1, 2, None)
                u_hi(2, 3, 1)
                gelu(0, 2, None)
                u_hi(3, 4, 2)
                with act.Fori(1, NUU // RAWS) as it:
                    u_hi(0, it * 4 + 1, it * 4 - 1)
                    gelu(1, it * 4, it * 2 - 1 if False else None)
                    u_hi(1, it * 4 + 2, it * 4)
                    u_hi(2, it * 4 + 3, it * 4 + 1)
                    gelu(0, it * 4 + 2, it * 2 - 1)
                    u_hi(3, it * 4 + 4, it * 4 + 2)
                gelu(1, NUU, TILES - 2)

                act.wait_ge(gated, TILES)

                def a_hi_of(i, s, free):
                    if free is not None:
                        act.wait_ge(v_done, free)
                    nc.scalar.activation(a_hi[:, s, :], A3[:, i, :], ACT.Copy).then_inc(ah_ready, 1)

                def v_hi_of(j, landed, free):
                    act.wait_ge(raw_landed[slot_of(NPU + j)], landed)
                    if free is not None:
                        act.wait_ge(v_done, free)
                    nc.scalar.activation(v_hi[:, (NPU + j) % RAWS, :], raw[:, slot_of(NPU + j), :], ACT.Copy)\
                        .then_inc(vh_split, 1)

                for n in range(RAWS):
                    if n % 2 == 0:
                        a_hi_of(n // 2, n // 2, None)
                    v_hi_of(n, landed_at(NPU + NUU + n), None)
                with act.Fori(1, NUU // RAWS) as it:
                    for j in range(RAWS):
                        if j % 2 == 0:
                            a_hi_of(bass.ds(it * 2 + j // 2, 1), j // 2, it * RAWS + (j - 2))
                        v_hi_of(j, it * 16 + landed_at(NPU + NUU + j), it * RAWS + (j - 3))
                act.wait_ge(x2_ready, TT)
                squares_of(x1_back, [y_out[:, a, :] for a in range(TT)], NORM_FINAL)

            @block.vector
            def _(dve):
                newtons = [0]

                def chain(ins):
                    newtons[0] += 1
                    ins.then_inc(newton, 1)
                    dve.wait_ge(newton, newtons[0])

                def inverse_root(ms, root, inv, tmp):
                    chain(nc.vector.reciprocal(inv, root))
                    chain(nc.vector.tensor_tensor(tmp, inv, inv, ALU.mult))
                    chain(nc.vector.tensor_tensor(tmp, tmp, ms, ALU.mult))
                    chain(nc.vector.tensor_scalar(tmp, tmp, -0.5, 1.5, ALU.mult, ALU.add))
                    chain(nc.vector.tensor_tensor(inv, inv, tmp, ALU.mult))

                def rstd(round_no):
                    dve.wait_ge(squares_done, TT * (round_no + 1))
                    nc.vector.tensor_scalar(MS, SSQ, 1.0 / D, EPS, ALU.mult, ALU.add).then_inc(mean_done, 1)
                    dve.wait_ge(mean_done, round_no + 1)
                    dve.wait_ge(root_done, round_no + 1)
                    inverse_root(MS, ROOT, INV, TMP)

                def scale_x():
                    for a in range(TT):
                        nc.vector.tensor_scalar(xs[:, a, :], x_res[:, a, :], INV[:, a:a + 1], None, ALU.mult)\
                            .then_inc(scaled, 1)

                def take_lo(gain, hi_before):
                    for c in range(C):
                        if c % 2 == 0:
                            dve.wait_ge(hi_taken, hi_before + c + 2)
                        nc.vector.scalar_tensor_tensor(out=xl3[:, c, :], in0=chunks16[:, c, :],
                                                       scalar=gain[:, c:c + 1], in1=xh3[:, c, :].bitcast(F32),
                                                       op0=ALU.mult, op1=ALU.subtract).then_inc(lo_taken, 1)

                def lo_unit(ready, j, n0):
                    dve.wait_ge(hi_split, ready)
                    nc.vector.tensor_tensor(w_lo[:, (n0 + j) % 2, :], raw[:, slot_of(n0 + j), :],
                                            w_hi[:, (n0 + j) % 2, :].bitcast(F32), ALU.subtract)\
                        .then_inc(lo_split, 1)

                def pass_lo(p):
                    for j in range(RAWS):
                        lo_unit(unit0(p) + j + 1, j, unit0(p))
                    with dve.Fori(1, C // RAWS) as it:
                        for j in range(RAWS):
                            lo_unit(it * RAWS + (unit0(p) + j + 1), j, unit0(p))

                nc.vector.memset(v_nat[:, :, :, DH:DH + 1], 1.0).then_inc(v_ready, 1)
                rstd(NORM_MIX)
                scale_x()
                dve.wait_ge(cols_ready, 1)
                take_lo(g_mix, 0)
                for n in range(GU):
                    lo_unit(n + 1, n, 0)
                for p in range(NIN):
                    pass_lo(p)

                R = lambda n: rows[0:NH, n, :]
                gate_steps = [0]

                def gate_chain(ins):
                    gate_steps[0] += 1
                    ins.then_inc(gate_step_dve, 1)
                    dve.wait_ge(gate_step_dve, gate_steps[0])

                dve.wait_ge(small_landed, 16 * 8)
                dve.wait_ge(gate_step_pe, 2)
                gate_chain(nc.vector.tensor_scalar(R(0), ps[0:NH, 6, 0:T], bias_i[:, 0:1], None, ALU.add))
                gate_chain(nc.vector.tensor_scalar(R(1), ps[0:NH, 6, T:2 * T], bias_f[:, 0:1], None, ALU.add))
                gate_chain(nc.vector.scalar_tensor_tensor(out=R(4), in0=R(1), scalar=-1.0, in1=R(1),
                                                          op0=ALU.mult, op1=ALU.max))
                dve.wait_ge(gate_step_act, 2)
                gate_chain(nc.vector.tensor_scalar(R(6), R(5), 1.0, None, ALU.add))
                dve.wait_ge(gate_step_act, 3)
                gate_chain(nc.vector.scalar_tensor_tensor(out=R(1), in0=R(1), scalar=0.0, in1=R(4),
                                                          op0=ALU.min, op1=ALU.subtract))
                gate_chain(nc.vector.memset(R(7), 1.0))
                gate_chain(nc.vector.tensor_tensor_scan(R(2), R(7), R(1), 0.0, ALU.mult, ALU.add))
                gate_chain(nc.vector.tensor_tensor(R(3), R(0), R(2), ALU.subtract))
                gate_chain(nc.vector.tensor_tensor_scan(R(4), R(3), R(3), 0.0, ALU.max, ALU.max))
                gate_chain(nc.vector.tensor_copy(R(7), R(4)))
                gate_chain(nc.vector.tensor_tensor(R(5), R(2), R(4), ALU.add))
                dve.wait_ge(gate_step_pe, 4)
                gate_chain(nc.vector.tensor_copy(aN, ps[:, 7, 0:TT * NH].rearrange("p (a h) -> p a h", a=TT)))
                gate_chain(nc.vector.tensor_copy(limN, ps[:, 7, TT * NH:2 * TT * NH].rearrange("p (a h) -> p a h", a=TT)))
                for h in HEADS:
                    m = ps[:, 4 + h // 2, (h % 2) * T:(h % 2 + 1) * T]
                    nc.vector.tensor_scalar(sw[:, h, 0:T], m, aN[:, 0, h:h + 1], 0.0, ALU.subtract, ALU.max)
                    nc.vector.tensor_scalar(sw[:, h, T:T + P], m[:, P:T], aN[:, 1, h:h + 1], 0.0,
                                            ALU.subtract, ALU.max).then_inc(expo_in, 1)
                for h in HEADS:
                    dve.wait_ge(expo_out, h + 1)
                    nc.vector.tensor_tensor(sw[:, h, :], sw[:, h, :], causal, ALU.mult).then_inc(sw_half, 1)
                for h in HEADS:
                    dve.wait_ge(sw_half, h + 1)
                    dve.wait_ge(qk_done, h + 1)
                    nc.vector.tensor_tensor(sw[:, h, :], ps[:, h, 0:T + P], sw[:, h, :], ALU.mult)\
                        .then_inc(sw_ready, 1)
                conv_steps = [0]

                def conv_chain(ins):
                    conv_steps[0] += 1
                    ins.then_inc(conv_step, 1)
                    dve.wait_ge(conv_step, conv_steps[0])

                u = proj["cx"]
                conv_chain(nc.vector.tensor_tensor(u, proj["cc"], proj["cx"], ALU.mult))
                for c in range(UC):
                    last = nc.vector.tensor_scalar(mixT[:, c, :], u[:, c, :], taps[:, 2, c:c + 1], None, ALU.mult)
                conv_chain(last)
                for w, lag in ((1, 1), (0, 2)):
                    for c in range(UC):
                        last = nc.vector.scalar_tensor_tensor(
                            out=mixT[:, c, lag:T], in0=u[:, c, 0:T - lag], scalar=taps[:, w, c:c + 1],
                            in1=mixT[:, c, lag:T], op0=ALU.mult, op1=ALU.add)
                    conv_chain(last)
                nc.vector.tensor_tensor(mixT[:, 0:UC, :], mixT[:, 0:UC, :], proj["cb"], ALU.mult).then_inc(mix_ready, 1)
                for g in range(HN):
                    jt, h = g // NH, g % NH
                    dve.wait_ge(pv_done, g + 1)
                    last = nc.vector.tensor_copy(NQ[:, g:g + 1], ps[:, (4 if jt == 0 else 0) + h, DH:DH + 1])
                chain(last)
                chain(nc.vector.scalar_tensor_tensor(out=DEN, in0=NQ, scalar=-1.0, in1=NQ, op0=ALU.mult, op1=ALU.max))
                chain(nc.vector.tensor_tensor(DEN, DEN, limN.rearrange("p a h -> p (a h)"), ALU.max))
                nc.vector.reciprocal(DEN, DEN).then_inc(den_ready, HN)
                dve.wait_ge(h_squared, HN)
                nc.vector.tensor_scalar(HMS, HSS, 1.0 / DH, EPS, ALU.mult, ALU.add).then_inc(h_rstd, 1)
                dve.wait_ge(h_rstd, 1)
                dve.wait_ge(h_squared, HN + 1)
                inverse_root(HMS, HROOT, HINV, HTMP)
                for g in range(HN):
                    jt, h = g // NH, g % NH
                    nc.vector.tensor_scalar(h_nat[:, jt, h, :], h_nat[:, jt, h, :], HINV[:, g:g + 1], None, ALU.mult)\
                        .then_inc(h_ready, 1)
                dve.wait_ge(o_sigmoid, 1)
                dve.wait_ge(h_turned, 1)
                for c in range(UC):
                    last = nc.vector.scalar_tensor_tensor(out=mixT[:, UC + c, :], in0=chunks16[:, c, :],
                                                          scalar=g_ml[:, c:c + 1], in1=proj["o"][:, c, :],
                                                          op0=ALU.mult, op1=ALU.mult)
                last.then_inc(mix_ready, 1)
                for half in range(2):
                    dve.wait_ge(mix_ready, half + 1)
                    dve.wait_ge(hi_taken, C + half + 1)
                    s = slice(half * UC, (half + 1) * UC)
                    nc.vector.tensor_tensor(xl3[:, s, :], mixT[:, s, :], xh3[:, s, :].bitcast(F32), ALU.subtract)\
                        .then_inc(lo_taken, 1)
                for p in (NIN, NIN + 1):
                    pass_lo(p)
                for a in range(TT):
                    dve.wait_ge(mixo_turned, a + 1)
                    nc.vector.tensor_tensor(x_res[:, a, :], natural[:, a, :], x_res[:, a, :], ALU.add)\
                        .then_inc(x1_ready, 1)
                rstd(NORM_FFN)
                scale_x()
                take_lo(g_ffn, C + 2)
                for p in (NIN + 2, NIN + 3):
                    pass_lo(p)

                steps = [0]

                def top_chain(ins):
                    steps[0] += 1
                    ins.then_inc(top_step, 1)
                    dve.wait_ge(top_step, steps[0])

                def top16(src, values, places, spare):
                    top_chain(nc.vector.max(values[:, 0:8], src))
                    nc.vector.max_index(places[:, 0:8], values[:, 0:8], src)
                    top_chain(nc.vector.match_replace(spare, values[:, 0:8], src, LOWEST))
                    top_chain(nc.vector.max(values[:, 8:16], spare))
                    nc.vector.max_index(places[:, 8:16], values[:, 8:16], spare).then_inc(top_step, 1)
                    steps[0] += 1

                for a in range(TT):
                    dve.wait_ge(s_copied, a + 1)
                    for g in range(a * 2 * PH, (a + 1) * 2 * PH):
                        top16(scores[:, g, :], top_v[:, g, :], top_i[:, g, :], left[:, g % 2, 0:NK])
                dve.wait_ge(top_step, steps[0])
                tv = top_v.rearrange("p (g s) k -> p g s k", s=2)
                c4 = cand.rearrange("p g (a b) -> p g a b", b=TOPK)
                top_chain(nc.vector.tensor_tensor(
                    c4, tv[:, :, 0, :].unsqueeze(3).broadcast_to([P, TT * PH, TOPK, TOPK]),
                    tv[:, :, 1, :].unsqueeze(2).broadcast_to([P, TT * PH, TOPK, TOPK]), ALU.add))
                for g in range(TT * PH):
                    top16(cand[:, g, :], best_v[:, g, :], best_i[:, g, :], left[:, g % 2, :])
                dve.wait_ge(top_step, steps[0])
                top_chain(nc.vector.tensor_tensor(shifted, best_v, best_v[:, :, 0:1].broadcast_to([P, TT * PH, TOPK]),
                                                  ALU.subtract))
                nc.vector.tensor_copy(total, shifted[:, :, 0]).then_inc(soft_in, 1)
                flat_i = best_i.rearrange("p g k -> p (g k)")
                top_chain(nc.vector.tensor_scalar(half_i[:, 0, :], flat_i, 4, None, ALU.logical_shift_right))
                top_chain(nc.vector.tensor_scalar(half_i[:, 1, :], flat_i, 15, None, ALU.bitwise_and))
                top_chain(nc.vector.tensor_copy(half_f, half_i))
                top_chain(nc.vector.tensor_copy(top_f, top_i))
                top_chain(nc.vector.tensor_copy(iota16, iota[:, 0:TOPK]))
                tf = top_f.rearrange("p (g s) k -> p g s k", s=2)
                for s in range(2):
                    pick = half_f[:, s, :].rearrange("p (g k) -> p g k", k=TOPK)
                    top_chain(nc.vector.tensor_tensor(
                        match, pick.unsqueeze(3).broadcast_to([P, TT * PH, TOPK, TOPK]),
                        iota16.unsqueeze(1).unsqueeze(1).broadcast_to([P, TT * PH, TOPK, TOPK]), ALU.is_equal))
                    top_chain(nc.vector.tensor_tensor(
                        match, match, tf[:, :, s, :].unsqueeze(2).broadcast_to([P, TT * PH, TOPK, TOPK]), ALU.mult))
                    top_chain(nc.vector.tensor_reduce(found[:, s, :].rearrange("p (g k) -> p g k", k=TOPK), match,
                                                      AX_X, ALU.add))
                dve.wait_ge(soft_out, 1)
                top_chain(nc.vector.tensor_reduce(total, shifted, AX_X, ALU.add))
                top_chain(nc.vector.reciprocal(total, total))
                nc.vector.tensor_tensor(found[:, 2, :].rearrange("p (g k) -> p g k", k=TOPK), shifted,
                                        total.unsqueeze(2).broadcast_to([P, TT * PH, TOPK]), ALU.mult)\
                    .then_inc(found_ready, 1)
                dve.wait_ge(found_turned, 1)
                nc.vector.tensor_copy(picks[:, 0:2, :], flat[:, 0:2 * T].rearrange("p (s t) -> p s t", s=2))
                gate = flat[:, 2 * T:3 * T]
                top_chain(nc.vector.tensor_copy(picks[:, 2, :], gate))
                top_chain(nc.vector.tensor_tensor(rest[:, 0, :], gate, picks[:, 2, :], ALU.subtract))
                top_chain(nc.vector.tensor_copy(picks[:, 3, :], rest[:, 0, :]))
                top_chain(nc.vector.tensor_tensor(rest[:, 1, :], rest[:, 0, :], picks[:, 3, :], ALU.subtract))
                nc.vector.tensor_copy(picks[:, 4, :], rest[:, 1, :]).then_inc(picks_ready, 3)
                dve.wait_ge(picks_ready, 3)

                def one_hots(b, token, free):
                    if free is not None:
                        dve.wait_ge(gate_block, free)
                    for t in range(4):
                        s = token(t)
                        nc.vector.tensor_scalar(hot[:, b, t, 0, :], iota[:, :], picks[:, 0, s], None, ALU.is_equal)
                        for part in range(3):
                            last = nc.vector.tensor_scalar(hot[:, b, t, 1 + part, :], iota[:, :], picks[:, 1, s],
                                                           picks[:, 2 + part, s], ALU.is_equal, ALU.mult)
                    last.then_inc(hot_ready, 1)

                for b in range(2):
                    one_hots(b, lambda t: slice(4 * b + t, 4 * b + t + 1), None)
                with dve.Fori(1, TB // 2) as it:
                    for b in range(2):
                        one_hots(b, lambda t: bass.ds(it * 8 + (4 * b + t), 1), it * 2 + (b - 1))

                dve.wait_ge(gate_stored, TB)

                def u_lo(j, ready):
                    dve.wait_ge(uh_split, ready)
                    s = (NPU + j) % 2
                    nc.vector.tensor_tensor(w_lo[:, s, :], flat[:, (j % 2) * UW:(j % 2 + 1) * UW],
                                            w_hi[:, s, :].bitcast(F32), ALU.subtract).then_inc(ul_split, 1)

                def apply_gate(i, b, ready):
                    dve.wait_ge(gelu_done, ready)
                    nc.vector.tensor_tensor(A3[:, i, :], act_out[:, b, :], A3[:, i, :], ALU.mult).then_inc(gated, 1)

                u_lo(0, 1)
                u_lo(1, 2)
                u_lo(2, 3)
                apply_gate(0, 0, 1)
                u_lo(3, 4)
                with dve.Fori(1, NUU // RAWS) as it:
                    u_lo(0, it * 4 + 1)
                    apply_gate(bass.ds(it * 2 - 1, 1), 1, it * 2)
                    u_lo(1, it * 4 + 2)
                    u_lo(2, it * 4 + 3)
                    apply_gate(bass.ds(it * 2, 1), 0, it * 2 + 1)
                    u_lo(3, it * 4 + 4)
                apply_gate(TILES - 1, 1, TILES)

                def a_lo_of(i, s, ready):
                    dve.wait_ge(ah_ready, ready)
                    nc.vector.tensor_tensor(a_lo[:, s, :], A3[:, i, :], a_hi[:, s, :].bitcast(F32), ALU.subtract)\
                        .then_inc(al_ready, 1)

                def v_lo_of(j, ready):
                    dve.wait_ge(vh_split, ready)
                    s = (NPU + j) % RAWS
                    nc.vector.tensor_tensor(v_lo[:, s, :], raw[:, slot_of(NPU + j), :], v_hi[:, s, :].bitcast(F32),
                                            ALU.subtract).then_inc(vl_split, 1)

                for n in range(RAWS):
                    if n % 2 == 0:
                        a_lo_of(n // 2, n // 2, n // 2 + 1)
                    v_lo_of(n, n + 1)
                with dve.Fori(1, NUU // RAWS) as it:
                    for j in range(RAWS):
                        if j % 2 == 0:
                            a_lo_of(bass.ds(it * 2 + j // 2, 1), j // 2, it * 2 + (j // 2 + 1))
                        v_lo_of(j, it * RAWS + (j + 1))
                dve.wait_ge(v_done, NUU)
                dve.wait_ge(tail_landed, 32)
                for a in range(TT):
                    nc.vector.tensor_tensor(x1_back[:, a, :], natural[:, a, :], x1_back[:, a, :], ALU.add)\
                        .then_inc(x2_ready, 1)
                rstd(NORM_FINAL)
                for a in range(TT):
                    nc.vector.scalar_tensor_tensor(out=y_out[:, a, :], in0=x1_back[:, a, :], scalar=INV[:, a:a + 1],
                                                   in1=g_final, op0=ALU.mult, op1=ALU.mult).then_inc(out_ready, 1)


_INS = ["x", "norm_mix_g", "w_in", "b_igate", "b_fgate", "conv_w", "mlstm_norm_g", "w_out", "norm_ffn_g",
        "w_query", "sub_keys_1", "sub_keys_2", "expert_u", "expert_v", "norm_final_g"]


def kernel(**inputs):
    import numpy as _np
    import concourse.bacc as _bacc
    from concourse import mybir as _mybir
    from concourse.bass_utils import run_bass_kernel_spmd as _run

    nc = _bacc.Bacc("TRN2", target_bir_lowering=False, num_devices=1)
    arrays, args = {}, []
    for name in _INS:
        a = _np.ascontiguousarray(inputs[name])
        arrays[f"in_{name}_dram"] = a
        args.append(nc.dram_tensor(f"in_{name}_dram", a.shape, _mybir.dt.from_np(a.dtype), kind="ExternalInput").ap())
    out = nc.dram_tensor("out_dram", inputs["x"].shape, _mybir.dt.float32, kind="ExternalOutput").ap()
    hybrid_layer(nc, *args, out)
    r = _run(nc, [arrays], core_ids=[0])
    return r.results[0]["out_dram"]
```

```python
from contextlib import ExitStack

import concourse.bass as bass
from concourse import mybir

ALU = mybir.AluOpType
ACT = mybir.ActivationFunctionType
AX_X = mybir.AxisListType.X
F32 = mybir.dt.float32
F32R = mybir.dt.float32r
BF16 = mybir.dt.bfloat16
U32 = mybir.dt.uint32

P = 128
EPS = 1e-6
LOWEST = -3.4028234663852886e38


def hybrid_layer(nc, x, norm_mix_g, w_in, b_igate, b_fgate, conv_w, mlstm_norm_g, w_out, norm_ffn_g,
                 w_query, sub_keys_1, sub_keys_2, expert_u, expert_v, norm_final_g, out):
    T, D = x.shape[1], x.shape[2]
    TT = T // P
    C = D // P
    NH = b_igate.shape[1]
    DC = conv_w.shape[2]
    DM = mlstm_norm_g.shape[1]
    DH = DM // NH
    NK, DK = sub_keys_1.shape[1], sub_keys_1.shape[2]
    NE = expert_u.shape[1]
    TILES = NE // P
    PH = w_query.shape[2] // (2 * DK)
    TOPK = 16
    PICKS = PH * TOPK
    UW = 1024
    UC = UW // P
    GATES = 2 * NH
    assert (T, D, TILES, PICKS, NK, DK) == (256, 2048, 128, 128, 128, 128) and DC == DM == UW

    RAWS = 4
    GU = 2
    PASSES_IN = ["q", "k", "v", "o", "cx", "cc", "cb"]
    COLUMN = {"cx": 0, "cb": DC, "cc": 2 * DC, "q": 3 * DC, "k": 3 * DC + DM, "v": 3 * DC + 2 * DM,
              "o": 3 * DC + 3 * DM}
    NIN = len(PASSES_IN)
    PASSES = NIN + 4
    NPU = GU + C * PASSES
    NUU = 2 * TILES
    TB = T // 4
    PICK_TILES, GATE_TILES = 26, TB // 2
    REST0 = PICK_TILES + GATE_TILES
    REST = TILES - REST0
    B4, Q32, C16 = 4, 32, C
    unit0 = lambda p: GU + C * p

    def slot_of(n):
        return n % RAWS

    def landed_at(n):
        return 16 * (n // RAWS + 1)

    def tile_slot(i):
        return (i + 1) % 2

    def tile_landed_at(i):
        return 16 * (min(i, REST0 - 2 + i % 2) // 2 + 1) + 16 * B4 * max((i - REST0) // 2 + 1, 0)

    w_in2, w_out2, w_query2 = w_in[0], w_out[0], w_query[0]
    x2 = x[0].rearrange("(a p) d -> p a d", p=P)
    out2 = out[0].rearrange("(a p) d -> p a d", p=P)
    u_rows = expert_u[0].rearrange("(i p) d -> p i d", p=P)
    u_quads = expert_u[0].rearrange("(i e q) (b f) -> b q i e f", e=B4, q=Q32, b=B4)
    v_rows = expert_v[0].rearrange("(i p) d -> p i d", p=P)

    def pass_weights(p):
        if p < NIN:
            w, c0 = w_in2, COLUMN[PASSES_IN[p]]
        elif p < NIN + 2:
            w, c0 = w_out2, (p - NIN) * UW
        else:
            w, c0 = w_query2, (p - NIN - 2) * UW
        return w.rearrange("(k r) n -> r k n", r=P)[:, :, c0:c0 + UW]

    gate_cols = w_in2.rearrange("(k r) n -> r k n", r=P)[:, :, w_in2.shape[1] - P:w_in2.shape[1]]

    with ExitStack() as ctx:
        def sb(name, shape, dt=F32):
            return ctx.enter_context(nc.sbuf_tensor(name, shape, dt))

        def sem(name):
            return ctx.enter_context(nc.semaphore(name))

        x_kept = nc.dram_tensor("x_kept", (2, D, T), F32, kind="Internal").ap()
        x1_kept = nc.dram_tensor("x1_kept", (P, TT * D), F32, kind="Internal").ap()

        A = sb("A", [P, TILES * T])
        A3 = A[:, :].rearrange("p (i t) -> p i t", t=T)
        x_hi = sb("x_hi", [P, C * T], F32R)
        x_lo = sb("x_lo", [P, C * T], F32R)
        w_hi = sb("w_hi", [P, 2, UW], F32R)
        w_lo = sb("w_lo", [P, 2, UW], F32R)
        raw = sb("raw", [P, RAWS, UW])
        xh3 = x_hi[:, :].rearrange("p (c t) -> p c t", t=T)
        xl3 = x_lo[:, :].rearrange("p (c t) -> p c t", t=T)
        v_hi = x_hi[:, :].rearrange("p (s n) -> p s n", n=UW)
        v_lo = x_lo[:, :].rearrange("p (s n) -> p s n", n=UW)
        a_hi = w_hi[:, :, 0:T]
        a_lo = w_lo[:, :, 0:T]

        ident = sb("ident", [P, P])
        iota = sb("iota", [P, P], BF16)
        picks = sb("picks", [P, 3, T], BF16)
        parts = sb("parts", [P, 2, T])
        hot = sb("hot", [P, 2, 4, 4, P], BF16)
        hot_j = sb("hot_j", [P, 4, P], BF16)
        turned_u = hot[:, :, :, :, :].rearrange("p s k t n -> p (s k t n)").bitcast(F32)\
            .rearrange("p (s n) -> p s n", s=2)
        act_out = sb("act_out", [P, 2, T])
        COLS = 2 * C + UC + 3 * UC
        bias_i = sb("bias_i", [NH, 1])
        bias_f = sb("bias_f", [NH, 1])
        stat = sb("stat", [P, 64])

        raw_tile = raw[:, :, :].rearrange("p (s h) n -> p s (h n)", h=2)
        area = [0]

        def work(words):
            a = A[:, area[0]:area[0] + words]
            area[0] += words
            assert area[0] <= TILES * T
            return a

        proj = {}
        for name in PASSES_IN:
            proj[name] = work(UC * T).rearrange("p (c t) -> p c t", t=T)
        x_res = work(TT * D).rearrange("p (a d) -> p a d", a=TT)
        xs = work(TT * D).rearrange("p (a d) -> p a d", a=TT)
        mixT = work(C * T).rearrange("p (c t) -> p c t", t=T)
        v_nat = work(TT * NH * (DH + 1)).rearrange("p (a h v) -> p a h v", a=TT, h=NH)
        sw = work(NH * 384).rearrange("p (h j) -> p h j", h=NH)
        causal = work(384)
        gate_acc = work(T)
        gate_nat = work(TT * GATES).rearrange("p (a g) -> p a g", a=TT)
        rows = mixT[:, UC:UC + 8, :]
        col_rows = work(P)[0:COLS, :]
        cols = work(COLS)
        g_mix, g_ffn = cols[:, 0:C], cols[:, C:2 * C]
        g_ml = cols[:, 2 * C:2 * C + UC]
        taps = cols[:, 2 * C + UC:].rearrange("p (w c) -> p w c", w=3)
        select = work(NH * P).rearrange("p (h m) -> p h m", h=NH)
        aN = work(TT * NH).rearrange("p (a h) -> p a h", a=TT)
        limN = work(TT * NH).rearrange("p (a h) -> p a h", a=TT)
        h_nat = xs.rearrange("p a (h v) -> p a h v", v=DH)[:, :, 0:NH, :]
        mixoT = A[:, 0:C * T].rearrange("p (c t) -> p c t", t=T)
        at = C * T
        qT = A[:, at:at + C * T].rearrange("p (c t) -> p c t", t=T)
        at += C * T
        scores = A[:, at:at + 2 * PH * TT * NK].rearrange("p (g n) -> p g n", n=NK)
        at += 2 * PH * TT * NK
        assert at <= NIN * UC * T
        at = NIN * UC * T + 2 * TT * D
        cand = A[:, at:at + TT * PH * 256].rearrange("p (g n) -> p g n", n=256)
        at += TT * PH * 256
        left = A[:, at:at + 512].rearrange("p (s n) -> p s n", n=256)
        at += 512
        keys = A[:, at:at + 2 * DK].rearrange("p (s d) -> p s d", s=2)
        at += 2 * DK
        keysT = A[:, at:at + 2 * NK].rearrange("p (s n) -> p s n", s=2)
        at += 2 * NK
        top_v = A[:, at:at + 2 * PH * TT * TOPK].rearrange("p (g k) -> p g k", k=TOPK)
        at += 2 * PH * TT * TOPK
        top_i = A[:, at:at + 2 * PH * TT * TOPK].bitcast(U32).rearrange("p (g k) -> p g k", k=TOPK)
        at += 2 * PH * TT * TOPK
        top_f = A[:, at:at + 2 * PH * TT * TOPK].rearrange("p (g k) -> p g k", k=TOPK)
        at += 2 * PH * TT * TOPK
        best_v = A[:, at:at + TT * PICKS].rearrange("p (g k) -> p g k", k=TOPK)
        at += TT * PICKS
        best_i = A[:, at:at + TT * PICKS].bitcast(U32).rearrange("p (g k) -> p g k", k=TOPK)
        at += TT * PICKS
        half_i = A[:, at:at + 2 * TT * PICKS].bitcast(U32).rearrange("p (s g) -> p s g", s=2)
        at += 2 * TT * PICKS
        half_f = A[:, at:at + 2 * TT * PICKS].rearrange("p (s g) -> p s g", s=2)
        at += 2 * TT * PICKS
        assert at <= TILES * T, at
        WORK_END = at
        match = scores.rearrange("p g n -> p (g n)").rearrange("p (g k a) -> p g k a", k=TOPK, a=TOPK)
        at = 12288
        found = A[:, at:at + 3 * TT * PICKS].rearrange("p (s g) -> p s g", s=3)
        at += 3 * TT * PICKS
        iota16 = A[:, at:at + TOPK]
        at += TOPK
        shifted = A[:, at:at + TT * PICKS].rearrange("p (g k) -> p g k", k=TOPK)
        at += TT * PICKS
        total = A[:, at:at + TT * PH]
        at += TT * PH
        rest = A[:, at:at + 2 * T].rearrange("p (s t) -> p s t", s=2)
        at += 2 * T
        assert at <= NIN * UC * T and PICK_TILES * T <= 8192
        x1_back = A[:, 0:TT * D].rearrange("p (a d) -> p a d", a=TT)
        g_final = A[:, TT * D:TT * D + D]
        y_out = A[:, TT * D + D:2 * TT * D + D].rearrange("p (a d) -> p a d", a=TT)
        FREED = (2 * TT * D + D) // T + 2

        ps = ctx.enter_context(nc.psum_tensor("ps", [P, 8, 512], F32))
        flat = ps[:, :, :].rearrange("p b n -> p (b n)")
        chunks16 = flat.rearrange("p (c t) -> p c t", t=T)
        natural = flat.rearrange("p (a d) -> p a d", a=TT)

        raw_landed = [sem(f"raw_landed{i}") for i in range(RAWS)]
        x_landed, small_landed, keys_landed = sem("x_landed"), sem("small_landed"), sem("keys_landed")
        cols_turned, cols_ready = sem("cols_turned"), sem("cols_ready")
        constants, masks = sem("constants"), sem("masks")
        squares_done, mean_done, root_done, rstd_done = (sem("squares_done"), sem("mean_done"),
                                                         sem("root_done"), sem("rstd_done"))
        newton, scaled, turned, hi_taken, lo_taken = (sem("newton"), sem("scaled"), sem("turned"),
                                                      sem("hi_taken"), sem("lo_taken"))
        hi_split, lo_split, unit_done, pass_out = (sem("hi_split"), sem("lo_split"), sem("unit_done"),
                                                   sem("pass_out"))
        gates_out, gate_step_pe, gate_step_act, gate_step_dve = (
            sem("gates_out"), sem("gate_step_pe"), sem("gate_step_act"), sem("gate_step_dve"))
        v_turned, v_ready, qk_done, expo_in, expo_out, sw_half, sw_ready, pv_done = (
            sem("v_turned"), sem("v_ready"), sem("qk_done"), sem("expo_in"), sem("expo_out"),
            sem("sw_half"), sem("sw_ready"), sem("pv_done"))
        den_ready, h_scaled, h_squared, h_rstd, h_ready, h_turned = (
            sem("den_ready"), sem("h_scaled"), sem("h_squared"), sem("h_rstd"), sem("h_ready"), sem("h_turned"))
        o_sigmoid, conv_step, mix_ready = sem("o_sigmoid"), sem("conv_step"), sem("mix_ready")
        mixo_turned, x1_ready, x1_stored = sem("mixo_turned"), sem("x1_ready"), sem("x1_stored")
        keys_turned, keysT_ready, s_done, s_copied = (sem("keys_turned"), sem("keysT_ready"),
                                                      sem("s_done"), sem("s_copied"))
        top_step, soft_in, soft_out, found_ready, found_turned, picks_ready = (
            sem("top_step"), sem("soft_in"), sem("soft_out"), sem("found_ready"), sem("found_turned"),
            sem("picks_ready"))
        hot_i_ready, hot_j_ready, hot_ready, parts_ready, gate_block, gate_applied = (
            sem("hot_i_ready"), sem("hot_j_ready"), sem("hot_ready"), sem("parts_ready"), sem("gate_block"),
            sem("gate_applied"))
        tile_landed = [sem(f"tile_landed{i}") for i in range(2)]
        dve_turned, ones_set, cand_used = sem("dve_turned"), sem("ones_set"), sem("cand_used")
        x_kept_sem, x_ordered = sem("x_kept_sem"), [sem(f"x_ordered{i}") for i in range(2)]
        u_turned, uh_split, ul_split, u_done, gelu_done, gated = (
            sem("u_turned"), sem("uh_split"), sem("ul_split"), sem("u_done"), sem("gelu_done"), sem("gated"))
        ah_ready, al_ready, vh_split, vl_split, v_done = (
            sem("ah_ready"), sem("al_ready"), sem("vh_split"), sem("vl_split"), sem("v_done"))
        tail_landed, x2_ready, out_ready, out_stored = (
            sem("tail_landed"), sem("x2_ready"), sem("out_ready"), sem("out_stored"))

        HEADS = range(NH)
        NORM_MIX, NORM_FFN, NORM_FINAL = range(3)
        SSQ, MS, ROOT, INV, TMP = (stat[:, 0:TT], stat[:, 2:2 + TT], stat[:, 4:4 + TT],
                                   stat[:, 6:6 + TT], stat[:, 8:8 + TT])
        HN = TT * NH
        NQ, DEN, HSS, HMS, HROOT, HINV, HTMP = (stat[:, 10 + HN * i - 2:10 + HN * i - 2 + HN]
                                                for i in range(7))

        with nc.Block() as block:

            @block.sync
            def _(sp):
                sp.dma_start(x_res, x2).then_inc(x_landed, 16)
                for n in range(GU):
                    sp.dma_start(raw[:, slot_of(n), :].rearrange("p (k m) -> p k m", m=P),
                                 gate_cols[:, n * UC:(n + 1) * UC, :]).then_inc(raw_landed[slot_of(n)], 16)
                for p in range(PASSES):
                    w = pass_weights(p)

                    def load(k, j):
                        sp.dma_start(raw[:, slot_of(unit0(p) + j), :], w[:, k, :])\
                            .then_inc(raw_landed[slot_of(unit0(p) + j)], 16)

                    for j in range(RAWS):
                        if unit0(p) + j >= RAWS:
                            sp.wait_ge(lo_split, unit0(p) + j - RAWS + 1)
                        load(j, j)
                    with sp.Fori(1, C // RAWS) as it:
                        for j in range(RAWS):
                            sp.wait_ge(lo_split, it * RAWS + (unit0(p) + j - RAWS + 1))
                            load(bass.ds(it * RAWS + j, 1), j)
                def load_tile(s, i):
                    sp.dma_start(raw_tile[:, s, :], u_rows[:, i, :]).then_inc(tile_landed[s], 16)

                def load_quads(s, i):
                    for b in range(B4):
                        sp.dma_start(raw_tile[b * Q32:(b + 1) * Q32, s, :].rearrange("q (e f) -> q e f", e=B4),
                                     u_quads[b, :, i, :, :]).then_inc(tile_landed[s], 16)

                for i in range(2):
                    sp.wait_ge(lo_split, NPU - 2 + 2 * i)
                    load_tile(tile_slot(i), i)
                with sp.Fori(1, REST0 // 2) as it:
                    for i in range(2):
                        sp.wait_ge(u_turned, it * 4 + (2 * i - 2))
                        load_tile(tile_slot(i), bass.ds(it * 2 + i, 1))
                for i in range(2):
                    sp.wait_ge(u_turned, 2 * REST0 + 2 * i - 2)
                    load_quads(tile_slot(i), REST0 + i)
                sp.wait_ge(x_kept_sem, 32)
                for half in range(2):
                    sp.wait_ge(u_done, 2 * REST0 - 1 + half)
                    cs = slice(half * UC, (half + 1) * UC)
                    for n, xx in enumerate((xh3, xl3)):
                        for b in range(B4):
                            sp.dma_start(xx[b * Q32:(b + 1) * Q32, cs, :].bitcast(F32),
                                         x_kept[n].rearrange("(b c q) t -> b q c t", b=B4, q=Q32)[b, :, cs, :])\
                                .then_inc(x_ordered[half], 16)
                with sp.Fori(1, REST // 2) as it:
                    for i in range(2):
                        sp.wait_ge(dve_turned, it * 4 + (2 * i - 2))
                        for b in range(B4):
                            sp.dma_start(
                                raw_tile[b * Q32:(b + 1) * Q32, tile_slot(i), :].rearrange("q (e f) -> q e f", e=B4),
                                u_quads[b, :, bass.ds(it * 2 + (REST0 + i), 1), :, :].rearrange("q i e f -> q (i e) f"))\
                                .then_inc(tile_landed[tile_slot(i)], 16)
                for n in range(RAWS):
                    sp.wait_ge(dve_turned, 2 * REST - (2 if n < 2 else 0))
                    sp.dma_start(raw[:, slot_of(NPU + n), :], v_rows[:, n // 2, (n % 2) * UW:(n % 2 + 1) * UW])\
                        .then_inc(raw_landed[slot_of(NPU + n)], 16)
                with sp.Fori(1, NUU // RAWS) as it:
                    for j in range(RAWS):
                        sp.wait_ge(vl_split, it * RAWS + (j - RAWS + 1))
                        sp.dma_start(raw[:, slot_of(NPU + j), :],
                                     v_rows[:, bass.ds(it * 2 + j // 2, 1), (j % 2) * UW:(j % 2 + 1) * UW])\
                            .then_inc(raw_landed[slot_of(NPU + j)], 16)
                for a in range(TT):
                    sp.wait_ge(out_ready, a + 1)
                    sp.dma_start(out2[:, a, :], y_out[:, a, :]).then_inc(out_stored, 16)
                sp.wait_ge(out_stored, 16 * TT)

            @block.gpsimd
            def _(pool):
                def first_part(b, tokens, made, free):
                    pool.wait_ge(hot_j_ready, made)
                    if free is not None:
                        pool.wait_ge(gate_block, free)
                    nc.gpsimd.tensor_tensor(hot[:, b, 1, :, :], hot_j[:, :, :],
                                            picks[:, 2, tokens].unsqueeze(2).broadcast_to([P, 4, P]), ALU.mult)                        .then_inc(hot_ready, 1)

                def gelu_to_A(i, b, ready):
                    pool.wait_ge(gelu_done, ready)
                    nc.gpsimd.tensor_tensor(A3[:, i, :], act_out[:, b, :], A3[:, i, :], ALU.mult).then_inc(gated, 1)

                pool.memset(ident[:, :], 0.0).then_inc(constants, 1)
                pool.iota(iota[:, :], [[1, P]], base=0, channel_multiplier=0,
                          allow_small_or_imprecise_dtypes=True).then_inc(constants, 1)
                pool.wait_ge(constants, 2)
                pool.affine_select(out=ident[:, :], in_=ident[:, :], compare_op=ALU.not_equal, fill=1.0,
                                   base=0, pattern=[[-1, P]], channel_multiplier=1).then_inc(constants, 1)
                pool.memset(causal, 1.0).then_inc(masks, 1)
                pool.memset(select, 0.0).then_inc(masks, 1)
                pool.wait_ge(masks, 2)
                for c0 in (0, 2 * P):
                    pool.affine_select(out=causal[:, c0:c0 + P], in_=causal[:, c0:c0 + P], compare_op=ALU.is_ge,
                                       fill=0.0, base=0, pattern=[[1, P]], channel_multiplier=-1)\
                        .then_inc(masks, 1)
                pool.affine_select(out=select, in_=select, compare_op=ALU.not_equal, fill=1.0, base=0,
                                   pattern=[[-1, NH], [0, P]], channel_multiplier=1).then_inc(masks, 1)
                pool.wait_ge(x1_ready, TT)
                pool.dma_start(x1_kept, x_res.rearrange("p a d -> p (a d)")).then_inc(x1_stored, 16)
                pool.wait_ge(lo_taken, C + 2 + C)
                for n, xx in enumerate((xh3, xl3)):
                    pool.dma_start(x_kept[n].rearrange("(c p) t -> p c t", p=P), xx.bitcast(F32))                        .then_inc(x_kept_sem, 16)
                pool.wait_ge(x1_stored, 16)
                pool.wait_ge(s_copied, TT)
                for a, b in ((PICK_TILES * T, 8192), (NIN * UC * T, NIN * UC * T + 2 * TT * D), (WORK_END, TILES * T)):
                    pool.memset(A[:, a:b], 1.0).then_inc(ones_set, 1)
                pool.wait_ge(cand_used, 1)
                pool.memset(cand, 1.0).then_inc(ones_set, 1)
                pool.wait_ge(picks_ready, 1)
                first_part(0, slice(0, 4), 1, None)
                for a, b in ((8192, NIN * UC * T), (NIN * UC * T + 2 * TT * D + TT * PH * 256, WORK_END)):
                    pool.memset(A[:, a:b], 1.0).then_inc(ones_set, 1)
                for g in range(1, 4):
                    first_part(g % 2, slice(4 * g, 4 * g + 4), g + 1, g - 1 if g >= 2 else None)
                with pool.Fori(1, TB // 4) as it:
                    for j in range(4):
                        first_part(j % 2, bass.ds(it * 16 + 4 * j, 4), it * 4 + (j + 1), it * 4 + (j - 1))
                pool.wait_ge(gate_applied, TB)
                with pool.Fori(0, REST // 2) as it:
                    gelu_to_A(bass.ds(it * 2 + (REST0 - 1), 1), 1, it * 2 + REST0)
                    gelu_to_A(bass.ds(it * 2 + REST0, 1), 0, it * 2 + (REST0 + 1))
                gelu_to_A(TILES - 1, 1, TILES)
                pool.wait_ge(al_ready, FREED)
                pool.dma_start(x1_back.rearrange("p a d -> p (a d)"), x1_kept).then_inc(tail_landed, 16)
                pool.dma_start(g_final, norm_final_g.rearrange("(o d) -> o d", o=1).broadcast_to([P, D]))\
                    .then_inc(tail_landed, 16)

            @block.tensor
            def _(pe):
                def turn_x(round_no):
                    if round_no == NORM_MIX:
                        pe.wait_ge(small_landed, 16 * 8)
                        nc.tensor.transpose(ps[:, 7, 0:COLS], col_rows, ident[0:COLS, 0:COLS]).then_inc(cols_turned, 1)
                    pe.wait_ge(scaled, TT * (round_no + 1))
                    for c in range(C):
                        for a in range(TT):
                            last = nc.tensor.transpose(chunks16[:, c, a * P:(a + 1) * P],
                                                       xs[:, a, c * P:(c + 1) * P], ident[:, :])
                        if c % 2 == 1:
                            last.then_inc(turned, 1)
                        if c == C - 3 and round_no == NORM_MIX:
                            pe.wait_ge(cols_ready, 1)

                def project(p):
                    acc = flat[:, (p % 2) * 2048:(p % 2 + 1) * 2048]

                    def unit(u_wait, k, j, first, final):
                        s = (unit0(p) + j) % 2
                        pe.wait_ge(lo_split, u_wait)
                        for c in range(UC):
                            for n, (w, xx) in enumerate(((w_hi, xh3), (w_hi, xl3), (w_lo, xh3))):
                                last = nc.tensor.matmul(
                                    acc[:, c * T:(c + 1) * T], w[:, s, c * P:(c + 1) * P], xx[:, k, :],
                                    start=first and n == 0 and c % 2 == 0, stop=final and n == 2,
                                    skip_group_check=True)
                        last.then_inc(unit_done, 1)

                    if p >= 2 and p < NIN:
                        pe.wait_ge(pass_out, p - 1)
                    for j in range(RAWS):
                        unit(unit0(p) + j + 1, j, j, j == 0, False)
                    with pe.Fori(1, C // RAWS) as it:
                        for j in range(RAWS):
                            unit(it * RAWS + (unit0(p) + j + 1), bass.ds(it * RAWS + j, 1), j, False, False)

                pe.wait_ge(constants, 3)
                turn_x(NORM_MIX)
                pe.wait_ge(lo_taken, C)
                pe.wait_ge(hi_taken, C)
                for n in range(GU):
                    pe.wait_ge(lo_split, n + 1)
                    for c in range(UC):
                        for m, (w, xx) in enumerate(((w_hi, xh3), (w_hi, xl3), (w_lo, xh3))):
                            last = nc.tensor.matmul(ps[:, 4, 0:T], w[:, n % 2, c * P:(c + 1) * P],
                                                    xx[:, n * UC + c, :], start=n == 0 and c == 0 and m == 0,
                                                    stop=n == GU - 1 and c == UC - 1 and m == 2)
                    last.then_inc(unit_done, 1)
                for p in range(NIN):
                    if p == 1:
                        pe.wait_ge(gates_out, 1)
                    project(p)

                pe.wait_ge(pass_out, NIN)
                for a in range(TT):
                    last = nc.tensor.transpose(ps[:, 5, a * P:(a + 1) * P], gate_acc[:, a * P:(a + 1) * P],
                                               ident[:, :])
                last.then_inc(gate_step_pe, 1)
                for a in range(TT):
                    for c in range(UC):
                        last = nc.tensor.transpose(natural[:, 0, a * DM + c * P:a * DM + (c + 1) * P],
                                                   proj["v"][:, c, a * P:(a + 1) * P], ident[:, :])
                    last.then_inc(v_turned, 1)
                pe.wait_ge(gate_step_act, 1)
                for g in range(2):
                    for a in range(TT):
                        last = nc.tensor.transpose(ps[0:NH, 6, g * T + a * P:g * T + (a + 1) * P],
                                                   gate_nat[:, a, g * NH:(g + 1) * NH], ident[:, :])
                last.then_inc(gate_step_pe, 1)
                pe.wait_ge(v_ready, TT + 1)
                for h in HEADS:
                    for l, j0, o in ((0, 0, 0), (1, P, T)):
                        for c in range(DH // P):
                            last = nc.tensor.matmul(ps[:, h, o:o + T - j0],
                                                    proj["k"][:, h * DH // P + c, l * P:(l + 1) * P],
                                                    proj["q"][:, h * DH // P + c, j0:T],
                                                    start=c == 0, stop=c == DH // P - 1)
                    last.then_inc(qk_done, 1)
                pe.wait_ge(gate_step_dve, 10)
                pe.wait_ge(masks, 5)
                for h in HEADS:
                    last = nc.tensor.matmul(ps[:, 4 + h // 2, (h % 2) * T:(h % 2 + 1) * T], select[0:NH, h, :],
                                            rows[0:NH, 4, :], start=True, stop=True)
                last.then_inc(gate_step_pe, 1)
                pe.wait_ge(gate_step_act, 4)
                for r, o in ((3, 0), (6, TT * NH)):
                    for a in range(TT):
                        last = nc.tensor.transpose(ps[:, 7, o + a * NH:o + (a + 1) * NH],
                                                   rows[0:NH, r, a * P:(a + 1) * P], ident[0:NH, 0:NH])
                last.then_inc(gate_step_pe, 1)
                pe.wait_ge(sw_ready, NH)
                for jt in range(TT):
                    for h in HEADS:
                        o = ps[:, (4 if jt == 0 else 0) + h, 0:DH + 1]
                        if jt == 0:
                            last = nc.tensor.matmul(o, sw[:, h, 0:P], v_nat[:, 0, h, :], start=True, stop=True)
                        else:
                            nc.tensor.matmul(o, sw[:, h, P:T], v_nat[:, 0, h, :], start=True, stop=False)
                            last = nc.tensor.matmul(o, sw[:, h, T:T + P], v_nat[:, 1, h, :], start=False, stop=True)
                        last.then_inc(pv_done, 1)
                pe.wait_ge(h_ready, HN)
                for c in range(UC):
                    for a in range(TT):
                        last = nc.tensor.transpose(
                            chunks16[:, c, a * P:(a + 1) * P],
                            h_nat[:, a, c * P // DH, c * P % DH:c * P % DH + P], ident[:, :])
                last.then_inc(h_turned, 1)

                pe.wait_ge(lo_taken, C + 2)
                for p in (NIN, NIN + 1):
                    project(p)
                pe.wait_ge(pass_out, NIN + 2)
                for a in range(TT):
                    for c in range(C):
                        last = nc.tensor.transpose(natural[:, a, c * P:(c + 1) * P],
                                                   mixoT[:, c, a * P:(a + 1) * P], ident[:, :])
                    last.then_inc(mixo_turned, 1)
                turn_x(NORM_FFN)
                pe.wait_ge(lo_taken, C + 2 + C)
                pe.wait_ge(hi_taken, C + 2 + C)
                for p in (NIN + 2, NIN + 3):
                    project(p)
                pe.wait_ge(pass_out, NIN + 4)
                pe.wait_ge(keys_landed, 32)
                for s in range(2):
                    last = nc.tensor.transpose(ps[:, 0, s * P:(s + 1) * P], keys[:, s, :], ident[:, :])
                last.then_inc(keys_turned, 1)
                pe.wait_ge(keysT_ready, 1)
                for a in range(TT):
                    for g in range(2 * PH):
                        last = nc.tensor.matmul(natural[:, a, g * NK:(g + 1) * NK], qT[:, g, a * P:(a + 1) * P],
                                                keysT[:, g % 2, :], start=True, stop=True)
                    last.then_inc(s_done, 1)
                pe.wait_ge(s_copied, TT)

                def turn_unit(j, landed, free):
                    s = tile_slot(j // 2)
                    if j % 2 == 0:
                        pe.wait_ge(tile_landed[s], landed)
                    if free is not None:
                        pe.wait_ge(ul_split, free)
                    o = (j % 2) * UW
                    for c in range(UC):
                        last = nc.tensor.transpose(flat[:, o + c * P:o + (c + 1) * P],
                                                   raw_tile[:, s, o + c * P:o + (c + 1) * P], ident[:, :])
                    last.then_inc(u_turned, 1)

                def score_unit(j, ready, free):
                    pe.wait_ge(ul_split, ready)
                    if free is not None:
                        pe.wait_ge(gelu_done, free)
                    for c in range(UC):
                        for n, (w, xx) in enumerate(((w_hi, xh3), (w_hi, xl3), (w_lo, xh3))):
                            last = nc.tensor.matmul(ps[:, 4 + j // 2, 0:T], w[:, j % 2, c * P:(c + 1) * P],
                                                    xx[:, (j % 2) * UC + c, :],
                                                    start=j % 2 == 0 and c == 0 and n == 0,
                                                    stop=j % 2 == 1 and c == UC - 1 and n == 2)
                    last.then_inc(u_done, 1)

                def turn_and_score(j, it, u0):
                    turn_unit(j, it * 16 + tile_landed_at(u0 // 2 + j // 2), it * 4 + (u0 + j - 1))
                    score_unit((j - 1) % 4, it * 4 + (u0 + j),
                               None if j in (0, 2) else it * 2 + (u0 // 2 + (j - 1) // 2 - 1))

                turn_unit(0, tile_landed_at(0), None)
                turn_unit(1, None, None)
                score_unit(0, 1, None)
                turn_unit(2, tile_landed_at(1), 1)
                score_unit(1, 2, None)
                turn_unit(3, None, 2)
                score_unit(2, 3, None)
                with pe.Fori(1, PICK_TILES // 2) as it:
                    for j in range(4):
                        turn_and_score(j, it, 0)
                pe.wait_ge(found_ready, 1)
                for s in range(3):
                    for a in range(TT):
                        last = nc.tensor.transpose(flat[:, 6 * 512 + s * T + a * P:6 * 512 + s * T + (a + 1) * P],
                                                   found[:, s, a * PICKS:(a + 1) * PICKS], ident[:, :])
                last.then_inc(found_turned, 1)

                def gate_tokens(b, made, applied):
                    pe.wait_ge(hot_i_ready, made)
                    pe.wait_ge(hot_ready, made)
                    pe.wait_ge(parts_ready, made)
                    if applied is not None:
                        pe.wait_ge(gate_applied, applied)
                    for t in range(4):
                        for part in range(3):
                            last = nc.tensor.matmul(ps[:, 6 + b, t * P:(t + 1) * P], hot[:, b, 1 + part, t, :],
                                                    hot[:, b, 0, t, :], start=t == 0 and part == 0,
                                                    stop=t == 3 and part == 2, skip_group_check=True)
                    last.then_inc(gate_block, 1)

                def gate_body(it, first):
                    for j in range(4):
                        turn_and_score(j, it, 2 * PICK_TILES)
                        if not (first and j == 0):
                            if first and j == 1:
                                pe.wait_ge(picks_ready, 1)
                            gate_tokens((j - 1) % 2, it * 4 + j, None if first and j < 3 else it * 4 + (j - 2))

                gate_body(0, True)
                with pe.Fori(1, TB // 4) as it:
                    gate_body(it, False)
                gate_tokens(1, TB, TB - 2)
                score_unit(3, 2 * REST0, None)

                def rest_body(it):
                    for j in range(4):
                        score_unit(j, it * 4 + (2 * REST0 + j + 1),
                                   it * 2 + (REST0 + j // 2 - 1) if j % 2 == 0 else None)

                for j in range(4):
                    if j < 2:
                        pe.wait_ge(x_ordered[j], 16 * 2 * B4)
                    score_unit(j, 2 * REST0 + j + 1, REST0 + j // 2 - 1 if j % 2 == 0 else None)
                with pe.Fori(1, REST // 2) as it:
                    rest_body(it)

                pe.wait_ge(gelu_done, TILES)

                def sum_unit(j, v_ok, a_ok, first):
                    pe.wait_ge(vl_split, v_ok)
                    if j % 2 == 0:
                        pe.wait_ge(al_ready, a_ok)
                    half, s, v = j % 2, j // 2, (NPU + j) % RAWS
                    for a in range(TT):
                        for n, (aa, vv) in enumerate(((a_hi, v_hi), (a_hi, v_lo), (a_lo, v_hi))):
                            for q in range(UW // 512):
                                last = nc.tensor.matmul(
                                    ps[:, a * 4 + half * 2 + q, :], aa[:, s, a * P:(a + 1) * P],
                                    vv[:, v, q * 512:(q + 1) * 512], start=first and n == 0, stop=False,
                                    skip_group_check=True)
                    last.then_inc(v_done, 1)

                for n in range(RAWS):
                    sum_unit(n, n + 1, n // 2 + 1, n < 2)
                with pe.Fori(1, NUU // RAWS) as it:
                    for j in range(RAWS):
                        sum_unit(j, it * RAWS + (j + 1), it * 2 + (j // 2 + 1), False)

            @block.scalar
            def _(act):
                row = 0
                for v in (norm_mix_g[0], norm_ffn_g[0], mlstm_norm_g[0], conv_w[0, 0], conv_w[0, 1], conv_w[0, 2]):
                    n = v.shape[0] // P
                    act.dma_start(col_rows[row:row + n, :], v.rearrange("(c p) -> c p", p=P))\
                        .then_inc(small_landed, 16)
                    row += n
                act.dma_start(bias_i[:, :], b_igate.rearrange("o h -> h o")).then_inc(small_landed, 16)
                act.dma_start(bias_f[:, :], b_fgate.rearrange("o h -> h o")).then_inc(small_landed, 16)

                def squares_of(src, junk, round_no):
                    for a in range(TT):
                        nc.scalar.activation(junk[a], src[:, a, :], ACT.Square,
                                             accum_out=SSQ[:, a:a + 1]).then_inc(squares_done, 1)
                    act.wait_ge(mean_done, round_no + 1)
                    nc.scalar.activation(ROOT, MS, ACT.Sqrt).then_inc(root_done, 1)

                def take_hi(gain, round_no, before):
                    for c in range(C):
                        if c % 2 == 0:
                            act.wait_ge(turned, C // 2 * round_no + c // 2 + 1)
                        nc.scalar.activation(xh3[:, c, :], chunks16[:, c, :], ACT.Copy, scale=gain[:, c:c + 1])\
                            .then_inc(hi_taken, 1)

                def hi_unit(u_landed, j, free, n0):
                    act.wait_ge(raw_landed[slot_of(n0 + j)], u_landed)
                    if free is not None:
                        act.wait_ge(unit_done, free)
                    nc.scalar.activation(w_hi[:, (n0 + j) % 2, :], raw[:, slot_of(n0 + j), :], ACT.Copy)\
                        .then_inc(hi_split, 1)

                def evacuate(p, dst, scale=1.0):
                    act.wait_ge(unit_done, unit0(p) + C)
                    h = (p % 2) * 2048
                    for q in range(2):
                        last = nc.scalar.activation(
                            dst[:, 4 * q:4 * q + 4, :],
                            flat[:, h + q * 1024:h + (q + 1) * 1024].rearrange("p (c t) -> p c t", t=T),
                            ACT.Copy, scale=scale)
                    last.then_inc(pass_out, 1)

                def pass_hi_first(p):
                    for j in range(RAWS):
                        n = unit0(p) + j
                        hi_unit(landed_at(n), j, n - 1 if n >= 2 else None, unit0(p))

                def pass_hi_rest(p):
                    with act.Fori(1, C // RAWS) as it:
                        for j in range(RAWS):
                            n = unit0(p) + j
                            hi_unit(it * 16 + landed_at(n), j, it * RAWS + (n - 1), unit0(p))

                act.wait_ge(x_landed, 16)
                squares_of(x_res, [xs[:, a, :] for a in range(TT)], NORM_MIX)
                act.wait_ge(cols_turned, 1)
                nc.scalar.activation(cols[:, :], ps[:, 7, 0:COLS], ACT.Copy).then_inc(cols_ready, 1)
                act.wait_ge(cols_ready, 1)
                take_hi(g_mix, NORM_MIX, 0)
                for n in range(GU):
                    hi_unit(landed_at(n), n, None, 0)
                for p in range(NIN):
                    pass_hi_first(p)
                    if p == 0:
                        act.wait_ge(unit_done, GU)
                        nc.scalar.activation(gate_acc, ps[:, 4, 0:T], ACT.Copy).then_inc(gates_out, 1)
                    else:
                        evacuate(p - 1, proj[PASSES_IN[p - 1]], DH ** -0.5 if PASSES_IN[p - 1] == "k" else 1.0)
                    pass_hi_rest(p)
                evacuate(NIN - 1, proj[PASSES_IN[NIN - 1]])

                act.wait_ge(gate_step_pe, 1)
                nc.scalar.activation(gate_nat, ps[:, 5, 0:T].rearrange("p (a m) -> p a m", a=TT)[:, :, P - GATES:P],
                                     ACT.Copy).then_inc(gate_step_act, 1)
                for a in range(TT):
                    act.wait_ge(v_turned, a + 1)
                    nc.scalar.activation(v_nat[:, a, :, 0:DH],
                                         natural[:, 0, a * DM:(a + 1) * DM].rearrange("p (h v) -> p h v", v=DH),
                                         ACT.Copy).then_inc(v_ready, 1)
                act.wait_ge(gate_step_dve, 3)
                nc.scalar.activation(rows[0:NH, 5, :], rows[0:NH, 4, :], ACT.Exp, scale=-1.0)\
                    .then_inc(gate_step_act, 1)
                act.wait_ge(gate_step_dve, 4)
                nc.scalar.activation(rows[0:NH, 4, :], rows[0:NH, 6, :], ACT.Ln).then_inc(gate_step_act, 1)
                act.wait_ge(gate_step_dve, 11)
                nc.scalar.activation(rows[0:NH, 6, :], rows[0:NH, 5, :], ACT.Exp, scale=-1.0)\
                    .then_inc(gate_step_act, 1)
                for h in HEADS:
                    act.wait_ge(expo_in, h + 1)
                    nc.scalar.activation(sw[:, h, :], sw[:, h, :], ACT.Exp, scale=-1.0).then_inc(expo_out, 1)
                nc.scalar.activation(proj["o"], proj["o"], ACT.Sigmoid).then_inc(o_sigmoid, 1)
                for g in range(HN):
                    jt, h = g // NH, g % NH
                    act.wait_ge(den_ready, g + 1)
                    nc.scalar.activation(h_nat[:, jt, h, :], ps[:, (4 if jt == 0 else 0) + h, 0:DH], ACT.Copy,
                                         scale=DEN[:, g:g + 1]).then_inc(h_scaled, 1)
                for g in range(HN):
                    jt, h = g // NH, g % NH
                    act.wait_ge(h_scaled, g + 1)
                    nc.scalar.activation(v_nat[:, jt, h, 0:DH], h_nat[:, jt, h, :], ACT.Square,
                                         accum_out=HSS[:, g:g + 1]).then_inc(h_squared, 1)
                act.wait_ge(h_rstd, 1)
                nc.scalar.activation(HROOT, HMS, ACT.Sqrt).then_inc(h_squared, 1)
                for half in range(2):
                    act.wait_ge(unit_done, unit0(NIN))
                    act.wait_ge(mix_ready, half + 1)
                    nc.scalar.activation(xh3[:, half * UC:(half + 1) * UC, :], mixT[:, half * UC:(half + 1) * UC, :],
                                         ACT.Copy).then_inc(hi_taken, 1)
                pass_hi_first(NIN)
                pass_hi_rest(NIN)
                pass_hi_first(NIN + 1)
                evacuate(NIN, mixoT[:, 0:UC, :])
                pass_hi_rest(NIN + 1)
                evacuate(NIN + 1, mixoT[:, UC:2 * UC, :])
                for a in range(TT):
                    act.wait_ge(x1_ready, a + 1)
                squares_of(x_res, [xs[:, a, :] for a in range(TT)], NORM_FFN)
                for s, k in enumerate((sub_keys_1, sub_keys_2)):
                    act.dma_start(keys[:, s, :], k[0]).then_inc(keys_landed, 16)
                take_hi(g_ffn, NORM_FFN, C + 2)
                pass_hi_first(NIN + 2)
                pass_hi_rest(NIN + 2)
                pass_hi_first(NIN + 3)
                evacuate(NIN + 2, qT[:, 0:UC, :])
                pass_hi_rest(NIN + 3)
                evacuate(NIN + 3, qT[:, UC:2 * UC, :])
                act.wait_ge(keys_turned, 1)
                nc.scalar.activation(keysT, ps[:, 0, 0:2 * P].rearrange("p (s n) -> p s n", s=2), ACT.Copy)\
                    .then_inc(keysT_ready, 1)
                for a in range(TT):
                    act.wait_ge(s_done, a + 1)
                    nc.scalar.activation(scores[:, a * 2 * PH:(a + 1) * 2 * PH, :],
                                         natural[:, a, :].rearrange("p (g n) -> p g n", n=NK),
                                         ACT.Copy).then_inc(s_copied, 1)

                def u_hi(j, turned_at, free):
                    act.wait_ge(u_turned, turned_at)
                    if free is not None:
                        act.wait_ge(u_done, free)
                    nc.scalar.activation(w_hi[:, j % 2, :], flat[:, (j % 2) * UW:(j % 2 + 1) * UW], ACT.Copy)\
                        .then_inc(uh_split, 1)

                def gelu_into(dst, b, done_at, free=None):
                    act.wait_ge(u_done, done_at)
                    if free is not None:
                        act.wait_ge(gated, free)
                    nc.scalar.activation(dst, ps[:, 4 + b, 0:T], ACT.Gelu).then_inc(gelu_done, 1)

                u_hi(0, 1, None)
                u_hi(1, 2, None)
                u_hi(2, 3, 1)
                gelu_into(A3[:, 0, :], 0, 2)
                u_hi(3, 4, 2)
                with act.Fori(1, PICK_TILES // 2) as it:
                    for j in range(4):
                        u_hi(j, it * 4 + (j + 1), it * 4 + (j - 1))
                        if j % 2 == 0:
                            gelu_into(A3[:, bass.ds(it * 2 + (j // 2 - 1), 1), :], (j // 2 - 1) % 2, it * 4 + j)
                act.wait_ge(soft_in, 1)
                nc.scalar.activation(shifted, shifted, ACT.Exp).then_inc(soft_out, 1)

                def hot_parts(b, token, ready, free):
                    act.wait_ge(hot_j_ready, ready)
                    if free is not None:
                        act.wait_ge(gate_block, free)
                    for t in range(4):
                        for part in range(2):
                            last = nc.scalar.activation(hot[:, b, 2 + part, t, :], hot_j[:, t, :], ACT.Copy,
                                                        scale=parts[:, part, token(t)])
                    last.then_inc(parts_ready, 1)

                def gate_body(it, first):
                    for j in range(4):
                        n = 2 * PICK_TILES + j
                        u_hi(j, it * 4 + (n + 1), it * 4 + (n - 1))
                        if first and j == 1:
                            gelu_into(A3[:, PICK_TILES - 1, :], 1, n - 1)
                        elif j % 2 == 1:
                            b = (j // 2 - 1) % 2
                            gelu_into(act_out[:, b, :], b, it * 4 + (n - 1), None if first else it * 2 - 1)
                        hot_parts(j % 2, (lambda t: slice(4 * j + t, 4 * j + t + 1)) if first else
                                  (lambda t: bass.ds(it * 16 + (4 * j + t), 1)),
                                  it * 4 + (j + 1), None if first and j < 2 else it * 4 + (j - 1))

                gate_body(0, True)
                with act.Fori(1, TB // 4) as it:
                    gate_body(it, False)

                def hi_of_turned(j, ready, free):
                    act.wait_ge(dve_turned, ready)
                    act.wait_ge(u_done, free)
                    nc.scalar.activation(
                        w_hi[:, j % 2, :].rearrange("p (c e q) -> p c e q", e=B4, q=Q32),
                        turned_u[:, j % 2, :].rearrange("p (e c q) -> p c e q", e=B4, q=Q32), ACT.Copy)\
                        .then_inc(uh_split, 1)

                with act.Fori(0, REST // 2) as it:
                    for j in range(4):
                        n = 2 * REST0 + j
                        hi_of_turned(j, it * 4 + (j + 1), it * 4 + (n - 1))
                        if j % 2 == 1:
                            b = (j // 2 - 1) % 2
                            gelu_into(act_out[:, b, :], b, it * 4 + (n - 1), it * 2 + (GATE_TILES + j // 2 - 2))
                gelu_into(act_out[:, 1, :], 1, NUU, TILES - 2 - PICK_TILES)

                act.wait_ge(gated, TILES - PICK_TILES)

                def a_hi_of(i, s, free):
                    if free is not None:
                        act.wait_ge(v_done, free)
                    nc.scalar.activation(a_hi[:, s, :], A3[:, i, :], ACT.Copy).then_inc(ah_ready, 1)

                def v_hi_of(j, landed, free):
                    act.wait_ge(raw_landed[slot_of(NPU + j)], landed)
                    if free is not None:
                        act.wait_ge(v_done, free)
                    nc.scalar.activation(v_hi[:, (NPU + j) % RAWS, :], raw[:, slot_of(NPU + j), :], ACT.Copy)\
                        .then_inc(vh_split, 1)

                for n in range(RAWS):
                    if n % 2 == 0:
                        a_hi_of(n // 2, n // 2, None)
                    v_hi_of(n, landed_at(NPU + n), None)
                with act.Fori(1, NUU // RAWS) as it:
                    for j in range(RAWS):
                        if j % 2 == 0:
                            a_hi_of(bass.ds(it * 2 + j // 2, 1), j // 2, it * RAWS + (j - 2))
                        v_hi_of(j, it * 16 + landed_at(NPU + j), it * RAWS + (j - 3))
                act.wait_ge(x2_ready, TT)
                squares_of(x1_back, [y_out[:, a, :] for a in range(TT)], NORM_FINAL)

            @block.vector
            def _(dve):
                newtons = [0]

                def chain(ins):
                    newtons[0] += 1
                    ins.then_inc(newton, 1)
                    dve.wait_ge(newton, newtons[0])

                def inverse_root(ms, root, inv, tmp):
                    chain(nc.vector.reciprocal(inv, root))
                    chain(nc.vector.tensor_tensor(tmp, inv, inv, ALU.mult))
                    chain(nc.vector.tensor_tensor(tmp, tmp, ms, ALU.mult))
                    chain(nc.vector.tensor_scalar(tmp, tmp, -0.5, 1.5, ALU.mult, ALU.add))
                    chain(nc.vector.tensor_tensor(inv, inv, tmp, ALU.mult))

                def rstd(round_no):
                    dve.wait_ge(squares_done, TT * (round_no + 1))
                    nc.vector.tensor_scalar(MS, SSQ, 1.0 / D, EPS, ALU.mult, ALU.add).then_inc(mean_done, 1)
                    dve.wait_ge(mean_done, round_no + 1)
                    dve.wait_ge(root_done, round_no + 1)
                    inverse_root(MS, ROOT, INV, TMP)

                def scale_x():
                    for a in range(TT):
                        nc.vector.tensor_scalar(xs[:, a, :], x_res[:, a, :], INV[:, a:a + 1], None, ALU.mult)\
                            .then_inc(scaled, 1)

                def take_lo(gain, hi_before):
                    for c in range(C):
                        if c % 2 == 0:
                            dve.wait_ge(hi_taken, hi_before + c + 2)
                        nc.vector.scalar_tensor_tensor(out=xl3[:, c, :], in0=chunks16[:, c, :],
                                                       scalar=gain[:, c:c + 1], in1=xh3[:, c, :].bitcast(F32),
                                                       op0=ALU.mult, op1=ALU.subtract).then_inc(lo_taken, 1)

                def lo_unit(ready, j, n0):
                    dve.wait_ge(hi_split, ready)
                    nc.vector.tensor_tensor(w_lo[:, (n0 + j) % 2, :], raw[:, slot_of(n0 + j), :],
                                            w_hi[:, (n0 + j) % 2, :].bitcast(F32), ALU.subtract)\
                        .then_inc(lo_split, 1)

                def pass_lo(p):
                    for j in range(RAWS):
                        lo_unit(unit0(p) + j + 1, j, unit0(p))
                    with dve.Fori(1, C // RAWS) as it:
                        for j in range(RAWS):
                            lo_unit(it * RAWS + (unit0(p) + j + 1), j, unit0(p))

                nc.vector.memset(v_nat[:, :, :, DH:DH + 1], 1.0).then_inc(v_ready, 1)
                rstd(NORM_MIX)
                scale_x()
                dve.wait_ge(cols_ready, 1)
                take_lo(g_mix, 0)
                for n in range(GU):
                    lo_unit(n + 1, n, 0)
                for p in range(NIN):
                    pass_lo(p)

                R = lambda n: rows[0:NH, n, :]
                gate_steps = [0]

                def gate_chain(ins):
                    gate_steps[0] += 1
                    ins.then_inc(gate_step_dve, 1)
                    dve.wait_ge(gate_step_dve, gate_steps[0])

                dve.wait_ge(small_landed, 16 * 8)
                dve.wait_ge(gate_step_pe, 2)
                gate_chain(nc.vector.tensor_scalar(R(0), ps[0:NH, 6, 0:T], bias_i[:, 0:1], None, ALU.add))
                gate_chain(nc.vector.tensor_scalar(R(1), ps[0:NH, 6, T:2 * T], bias_f[:, 0:1], None, ALU.add))
                gate_chain(nc.vector.scalar_tensor_tensor(out=R(4), in0=R(1), scalar=-1.0, in1=R(1),
                                                          op0=ALU.mult, op1=ALU.max))
                dve.wait_ge(gate_step_act, 2)
                gate_chain(nc.vector.tensor_scalar(R(6), R(5), 1.0, None, ALU.add))
                dve.wait_ge(gate_step_act, 3)
                gate_chain(nc.vector.scalar_tensor_tensor(out=R(1), in0=R(1), scalar=0.0, in1=R(4),
                                                          op0=ALU.min, op1=ALU.subtract))
                gate_chain(nc.vector.memset(R(7), 1.0))
                gate_chain(nc.vector.tensor_tensor_scan(R(2), R(7), R(1), 0.0, ALU.mult, ALU.add))
                gate_chain(nc.vector.tensor_tensor(R(3), R(0), R(2), ALU.subtract))
                gate_chain(nc.vector.tensor_tensor_scan(R(4), R(3), R(3), 0.0, ALU.max, ALU.max))
                gate_chain(nc.vector.tensor_copy(R(7), R(4)))
                gate_chain(nc.vector.tensor_tensor(R(5), R(2), R(4), ALU.add))
                dve.wait_ge(gate_step_pe, 4)
                gate_chain(nc.vector.tensor_copy(aN, ps[:, 7, 0:TT * NH].rearrange("p (a h) -> p a h", a=TT)))
                gate_chain(nc.vector.tensor_copy(limN, ps[:, 7, TT * NH:2 * TT * NH].rearrange("p (a h) -> p a h", a=TT)))
                for h in HEADS:
                    m = ps[:, 4 + h // 2, (h % 2) * T:(h % 2 + 1) * T]
                    nc.vector.tensor_scalar(sw[:, h, 0:T], m, aN[:, 0, h:h + 1], 0.0, ALU.subtract, ALU.max)
                    nc.vector.tensor_scalar(sw[:, h, T:T + P], m[:, P:T], aN[:, 1, h:h + 1], 0.0,
                                            ALU.subtract, ALU.max).then_inc(expo_in, 1)
                for h in HEADS:
                    dve.wait_ge(expo_out, h + 1)
                    nc.vector.tensor_tensor(sw[:, h, :], sw[:, h, :], causal, ALU.mult).then_inc(sw_half, 1)
                for h in HEADS:
                    dve.wait_ge(sw_half, h + 1)
                    dve.wait_ge(qk_done, h + 1)
                    nc.vector.tensor_tensor(sw[:, h, :], ps[:, h, 0:T + P], sw[:, h, :], ALU.mult)\
                        .then_inc(sw_ready, 1)
                conv_steps = [0]

                def conv_chain(ins):
                    conv_steps[0] += 1
                    ins.then_inc(conv_step, 1)
                    dve.wait_ge(conv_step, conv_steps[0])

                u = proj["cx"]
                conv_chain(nc.vector.tensor_tensor(u, proj["cc"], proj["cx"], ALU.mult))
                for c in range(UC):
                    last = nc.vector.tensor_scalar(mixT[:, c, :], u[:, c, :], taps[:, 2, c:c + 1], None, ALU.mult)
                conv_chain(last)
                for w, lag in ((1, 1), (0, 2)):
                    for c in range(UC):
                        last = nc.vector.scalar_tensor_tensor(
                            out=mixT[:, c, lag:T], in0=u[:, c, 0:T - lag], scalar=taps[:, w, c:c + 1],
                            in1=mixT[:, c, lag:T], op0=ALU.mult, op1=ALU.add)
                    conv_chain(last)
                nc.vector.tensor_tensor(mixT[:, 0:UC, :], mixT[:, 0:UC, :], proj["cb"], ALU.mult).then_inc(mix_ready, 1)
                for g in range(HN):
                    jt, h = g // NH, g % NH
                    dve.wait_ge(pv_done, g + 1)
                    last = nc.vector.tensor_copy(NQ[:, g:g + 1], ps[:, (4 if jt == 0 else 0) + h, DH:DH + 1])
                chain(last)
                chain(nc.vector.scalar_tensor_tensor(out=DEN, in0=NQ, scalar=-1.0, in1=NQ, op0=ALU.mult, op1=ALU.max))
                chain(nc.vector.tensor_tensor(DEN, DEN, limN.rearrange("p a h -> p (a h)"), ALU.max))
                nc.vector.reciprocal(DEN, DEN).then_inc(den_ready, HN)
                dve.wait_ge(h_squared, HN)
                nc.vector.tensor_scalar(HMS, HSS, 1.0 / DH, EPS, ALU.mult, ALU.add).then_inc(h_rstd, 1)
                dve.wait_ge(h_rstd, 1)
                dve.wait_ge(h_squared, HN + 1)
                inverse_root(HMS, HROOT, HINV, HTMP)
                for g in range(HN):
                    jt, h = g // NH, g % NH
                    nc.vector.tensor_scalar(h_nat[:, jt, h, :], h_nat[:, jt, h, :], HINV[:, g:g + 1], None, ALU.mult)\
                        .then_inc(h_ready, 1)
                dve.wait_ge(o_sigmoid, 1)
                dve.wait_ge(h_turned, 1)
                for c in range(UC):
                    last = nc.vector.scalar_tensor_tensor(out=mixT[:, UC + c, :], in0=chunks16[:, c, :],
                                                          scalar=g_ml[:, c:c + 1], in1=proj["o"][:, c, :],
                                                          op0=ALU.mult, op1=ALU.mult)
                last.then_inc(mix_ready, 1)
                for half in range(2):
                    dve.wait_ge(mix_ready, half + 1)
                    dve.wait_ge(hi_taken, C + half + 1)
                    s = slice(half * UC, (half + 1) * UC)
                    nc.vector.tensor_tensor(xl3[:, s, :], mixT[:, s, :], xh3[:, s, :].bitcast(F32), ALU.subtract)\
                        .then_inc(lo_taken, 1)
                for p in (NIN, NIN + 1):
                    pass_lo(p)
                for a in range(TT):
                    dve.wait_ge(mixo_turned, a + 1)
                    nc.vector.tensor_tensor(x_res[:, a, :], natural[:, a, :], x_res[:, a, :], ALU.add)\
                        .then_inc(x1_ready, 1)
                rstd(NORM_FFN)
                scale_x()
                take_lo(g_ffn, C + 2)
                for p in (NIN + 2, NIN + 3):
                    pass_lo(p)

                steps = [0]

                def top_chain(ins):
                    steps[0] += 1
                    ins.then_inc(top_step, 1)
                    dve.wait_ge(top_step, steps[0])

                def top16(src, values, places, spare):
                    top_chain(nc.vector.max(values[:, 0:8], src))
                    nc.vector.max_index(places[:, 0:8], values[:, 0:8], src)
                    top_chain(nc.vector.match_replace(spare, values[:, 0:8], src, LOWEST))
                    top_chain(nc.vector.max(values[:, 8:16], spare))
                    nc.vector.max_index(places[:, 8:16], values[:, 8:16], spare).then_inc(top_step, 1)
                    steps[0] += 1

                def u_lo(j, ready):
                    dve.wait_ge(uh_split, ready)
                    nc.vector.tensor_tensor(w_lo[:, j % 2, :], flat[:, (j % 2) * UW:(j % 2 + 1) * UW],
                                            w_hi[:, j % 2, :].bitcast(F32), ALU.subtract).then_inc(ul_split, 1)

                unit = [0]

                def next_unit():
                    u_lo(unit[0] % 4, unit[0] + 1)
                    unit[0] += 1

                dve.wait_ge(s_copied, TT)
                for k in range(TT * PH):
                    next_unit()
                    for g in (2 * k, 2 * k + 1):
                        top16(scores[:, g, :], top_v[:, g, :], top_i[:, g, :], left[:, g % 2, 0:NK])
                tv = top_v.rearrange("p (g s) k -> p g s k", s=2)
                for g in range(TT * PH):
                    next_unit()
                    top_chain(nc.vector.tensor_tensor(
                        cand[:, g, :].rearrange("p (a b) -> p a b", b=TOPK),
                        tv[:, g, 0, :].unsqueeze(2).broadcast_to([P, TOPK, TOPK]),
                        tv[:, g, 1, :].unsqueeze(1).broadcast_to([P, TOPK, TOPK]), ALU.add))
                    top16(cand[:, g, :], best_v[:, g, :], best_i[:, g, :], left[:, g % 2, :])
                next_unit()
                dve.wait_ge(top_step, steps[0])
                top_chain(nc.vector.tensor_tensor(shifted, best_v, best_v[:, :, 0:1].broadcast_to([P, TT * PH, TOPK]),
                                                  ALU.subtract))
                nc.vector.tensor_copy(total, shifted[:, :, 0]).then_inc(soft_in, 1)
                flat_i = best_i.rearrange("p g k -> p (g k)")
                top_chain(nc.vector.tensor_scalar(half_i[:, 0, :], flat_i, 4, None, ALU.logical_shift_right))
                top_chain(nc.vector.tensor_scalar(half_i[:, 1, :], flat_i, 15, None, ALU.bitwise_and))
                nc.vector.engine_nop().then_inc(cand_used, 1)
                next_unit()
                top_chain(nc.vector.tensor_copy(half_f, half_i))
                top_chain(nc.vector.tensor_copy(top_f, top_i))
                top_chain(nc.vector.tensor_copy(iota16, iota[:, 0:TOPK]))
                tf = top_f.rearrange("p (g s) k -> p g s k", s=2)
                for s in range(2):
                    pick = half_f[:, s, :].rearrange("p (g k) -> p g k", k=TOPK)
                    for g in range(0, TT * PH, 2):
                        next_unit()
                        gs = slice(g, g + 2)
                        top_chain(nc.vector.tensor_tensor(
                            match[:, gs, :, :], pick[:, gs, :].unsqueeze(3).broadcast_to([P, 2, TOPK, TOPK]),
                            iota16.unsqueeze(1).unsqueeze(1).broadcast_to([P, 2, TOPK, TOPK]), ALU.is_equal))
                        top_chain(nc.vector.tensor_tensor(
                            match[:, gs, :, :], match[:, gs, :, :],
                            tf[:, gs, s, :].unsqueeze(2).broadcast_to([P, 2, TOPK, TOPK]), ALU.mult))
                        top_chain(nc.vector.tensor_reduce(
                            found[:, s, :].rearrange("p (g k) -> p g k", k=TOPK)[:, gs, :], match[:, gs, :, :],
                            AX_X, ALU.add))
                while unit[0] < 2 * PICK_TILES:
                    next_unit()
                dve.wait_ge(soft_out, 1)
                top_chain(nc.vector.tensor_reduce(total, shifted, AX_X, ALU.add))
                top_chain(nc.vector.reciprocal(total, total))
                nc.vector.tensor_tensor(found[:, 2, :].rearrange("p (g k) -> p g k", k=TOPK), shifted,
                                        total.unsqueeze(2).broadcast_to([P, TT * PH, TOPK]), ALU.mult)\
                    .then_inc(found_ready, 1)
                dve.wait_ge(found_turned, 1)
                by_pick = flat[:, 6 * 512:6 * 512 + 3 * T]
                nc.vector.tensor_copy(picks[:, 0:2, :], by_pick[:, 0:2 * T].rearrange("p (s t) -> p s t", s=2))
                gate = by_pick[:, 2 * T:3 * T]
                top_chain(nc.vector.tensor_copy(picks[:, 2, :], gate))
                top_chain(nc.vector.tensor_tensor(rest[:, 0, :], gate, picks[:, 2, :], ALU.subtract))
                top_chain(nc.vector.tensor_copy(hot_j[:, 0:2, :].rearrange("p a n -> p (a n)"), rest[:, 0, :]))
                top_chain(nc.vector.tensor_copy(parts[:, 0, :], hot_j[:, 0:2, :].rearrange("p a n -> p (a n)")))
                top_chain(nc.vector.tensor_tensor(parts[:, 1, :], rest[:, 0, :], parts[:, 0, :], ALU.subtract))
                nc.vector.engine_nop().then_inc(picks_ready, 1)

                def hot_j_of(tokens, free):
                    if free is not None:
                        dve.wait_ge(parts_ready, free)
                        dve.wait_ge(hot_ready, free)
                    nc.vector.tensor_tensor(hot_j[:, :, :], iota[:, :].unsqueeze(1).broadcast_to([P, 4, P]),
                                            picks[:, 1, tokens].unsqueeze(2).broadcast_to([P, 4, P]),
                                            ALU.is_equal).then_inc(hot_j_ready, 1)

                def hot_i_of(b, tokens, free):
                    if free is not None:
                        dve.wait_ge(gate_block, free)
                    nc.vector.tensor_tensor(hot[:, b, 0, :, :], iota[:, :].unsqueeze(1).broadcast_to([P, 4, P]),
                                            picks[:, 0, tokens].unsqueeze(2).broadcast_to([P, 4, P]),
                                            ALU.is_equal).then_inc(hot_i_ready, 1)

                def apply_group(b, tokens, ready, applied, n_gated):
                    dve.wait_ge(gate_block, ready)
                    if applied is not None:
                        dve.wait_ge(gate_applied, applied)
                    if n_gated is not None:
                        dve.wait_ge(gated, n_gated)
                    nc.vector.tensor_tensor(A3[:, :, tokens], ps[:, 6 + b, :].rearrange("p (t i) -> p i t", t=4),
                                            A3[:, :, tokens], ALU.mult).then_inc(gate_applied, 1)

                def apply_gelu(i, b, ready, applied):
                    dve.wait_ge(gelu_done, ready)
                    if applied is not None:
                        dve.wait_ge(gate_applied, applied)
                    nc.vector.tensor_tensor(A3[:, i, :], act_out[:, b, :], A3[:, i, :], ALU.mult).then_inc(gated, 1)

                def gate_body(it, first, final):
                    for j in range(4):
                        four = lambda g: bass.ds(it * 16 + 4 * g, 4)
                        u_lo(j, it * 4 + (2 * PICK_TILES + j + 1))
                        if not (first and j < 2):
                            if first and j == 2:
                                dve.wait_ge(ones_set, 6)
                            apply_group(j % 2, four(j - 2), it * 4 + (j - 1), None if first and j == 2 else it * 4 + (j - 2),
                                        None if first and j < 4 else it * 2 + (j // 2 - 1))
                        hot_i_of(j % 2, four(j), None if first and j < 2 else it * 4 + (j - 1))
                        if not (final and j == 3):
                            hot_j_of(four(j + 1), it * 4 + (j + 1))
                        if j % 2 == 1 and not (first and j == 1):
                            i = it * 2 + (PICK_TILES + j // 2 - 1)
                            apply_gelu(bass.ds(i, 1), (j // 2 - 1) % 2,
                                       it * 2 + (PICK_TILES + j // 2), it * 4 + (j - 1))

                hot_j_of(slice(0, 4), None)
                gate_body(0, True, False)
                with dve.Fori(1, TB // 4 - 1) as it:
                    gate_body(it, False, False)
                gate_body(TB // 4 - 1, False, True)

                def turn_unit(j, landed, free):
                    s = tile_slot(j // 2)
                    if j % 2 == 0:
                        dve.wait_ge(tile_landed[s], landed)
                    if free is not None:
                        dve.wait_ge(uh_split, free)
                        dve.wait_ge(ul_split, free)
                    half = UW // B4
                    u = raw_tile[:, s, :].rearrange("p (e f) -> p e f", e=B4)
                    nc.vector.transpose(turned_u[:, j % 2, :].rearrange("p (e f) -> p e f", e=B4),
                                        u[:, :, (j % 2) * half:(j % 2 + 1) * half]).then_inc(dve_turned, 1)

                def lo_of_turned(j, ready):
                    dve.wait_ge(uh_split, ready)
                    nc.vector.tensor_tensor(
                        w_lo[:, j % 2, :].rearrange("p (c e q) -> p c e q", e=B4, q=Q32),
                        turned_u[:, j % 2, :].rearrange("p (e c q) -> p c e q", e=B4, q=Q32),
                        w_hi[:, j % 2, :].bitcast(F32).rearrange("p (c e q) -> p c e q", e=B4, q=Q32), ALU.subtract)\
                        .then_inc(ul_split, 1)

                dve.wait_ge(gate_block, TB - 1)
                turn_unit(0, tile_landed_at(REST0), None)
                apply_group(0, slice(T - 8, T - 4), TB - 1, TB - 2, GATE_TILES - 1)
                apply_group(1, slice(T - 4, T), TB, TB - 1, GATE_TILES - 1)
                with dve.Fori(0, REST // 2 - 1) as it:
                    for j in range(4):
                        k = (j + 1) % 4
                        turn_unit(k, it * 64 + tile_landed_at(REST0 + (j + 1) // 2), it * 4 + (2 * REST0 + j))
                        lo_of_turned(j, it * 4 + (2 * REST0 + j + 1))
                for j in range(4):
                    n = NUU - 4 + j
                    if j < 3:
                        turn_unit(j + 1, tile_landed_at(TILES - 2 + (j + 1) // 2), n)
                    lo_of_turned(j, n + 1)

                def a_lo_of(i, s, ready):
                    dve.wait_ge(ah_ready, ready)
                    nc.vector.tensor_tensor(a_lo[:, s, :], A3[:, i, :], a_hi[:, s, :].bitcast(F32), ALU.subtract)\
                        .then_inc(al_ready, 1)

                def v_lo_of(j, ready):
                    dve.wait_ge(vh_split, ready)
                    s = (NPU + j) % RAWS
                    nc.vector.tensor_tensor(v_lo[:, s, :], raw[:, slot_of(NPU + j), :], v_hi[:, s, :].bitcast(F32),
                                            ALU.subtract).then_inc(vl_split, 1)

                for n in range(RAWS):
                    if n % 2 == 0:
                        a_lo_of(n // 2, n // 2, n // 2 + 1)
                    v_lo_of(n, n + 1)
                with dve.Fori(1, NUU // RAWS) as it:
                    for j in range(RAWS):
                        if j % 2 == 0:
                            a_lo_of(bass.ds(it * 2 + j // 2, 1), j // 2, it * 2 + (j // 2 + 1))
                        v_lo_of(j, it * RAWS + (j + 1))
                dve.wait_ge(v_done, NUU)
                dve.wait_ge(tail_landed, 32)
                for a in range(TT):
                    nc.vector.tensor_tensor(x1_back[:, a, :], natural[:, a, :], x1_back[:, a, :], ALU.add)\
                        .then_inc(x2_ready, 1)
                rstd(NORM_FINAL)
                for a in range(TT):
                    nc.vector.scalar_tensor_tensor(out=y_out[:, a, :], in0=x1_back[:, a, :], scalar=INV[:, a:a + 1],
                                                   in1=g_final, op0=ALU.mult, op1=ALU.mult).then_inc(out_ready, 1)


_INS = ["x", "norm_mix_g", "w_in", "b_igate", "b_fgate", "conv_w", "mlstm_norm_g", "w_out", "norm_ffn_g",
        "w_query", "sub_keys_1", "sub_keys_2", "expert_u", "expert_v", "norm_final_g"]


def kernel(**inputs):
    import numpy as _np
    import concourse.bacc as _bacc
    from concourse import mybir as _mybir
    from concourse.bass_utils import run_bass_kernel_spmd as _run

    nc = _bacc.Bacc("TRN2", target_bir_lowering=False, num_devices=1)
    arrays, args = {}, []
    for name in _INS:
        a = _np.ascontiguousarray(inputs[name])
        arrays[f"in_{name}_dram"] = a
        args.append(nc.dram_tensor(f"in_{name}_dram", a.shape, _mybir.dt.from_np(a.dtype), kind="ExternalInput").ap())
    out = nc.dram_tensor("out_dram", inputs["x"].shape, _mybir.dt.float32, kind="ExternalOutput").ap()
    hybrid_layer(nc, *args, out)
    r = _run(nc, [arrays], core_ids=[0])
    return r.results[0]["out_dram"]
```

```python
from contextlib import ExitStack

import concourse.bass as bass
from concourse import mybir

ALU = mybir.AluOpType
ACT = mybir.ActivationFunctionType
AX_X = mybir.AxisListType.X
F32 = mybir.dt.float32
F32R = mybir.dt.float32r
BF16 = mybir.dt.bfloat16
U32 = mybir.dt.uint32

P = 128
EPS = 1e-6
LOWEST = -3.4028234663852886e38


def hybrid_layer(nc, x, norm_mix_g, w_in, b_igate, b_fgate, conv_w, mlstm_norm_g, w_out, norm_ffn_g,
                 w_query, sub_keys_1, sub_keys_2, expert_u, expert_v, norm_final_g, out):
    T, D = x.shape[1], x.shape[2]
    TT = T // P
    C = D // P
    NH = b_igate.shape[1]
    DC = conv_w.shape[2]
    DM = mlstm_norm_g.shape[1]
    DH = DM // NH
    NK, DK = sub_keys_1.shape[1], sub_keys_1.shape[2]
    NE = expert_u.shape[1]
    TILES = NE // P
    PH = w_query.shape[2] // (2 * DK)
    TOPK = 16
    PICKS = PH * TOPK
    UW = 1024
    UC = UW // P
    GATES = 2 * NH
    assert (T, D, TILES, PICKS, NK, DK) == (256, 2048, 128, 128, 128, 128) and DC == DM == UW

    RAWS = 4
    GU = 2
    PASSES_IN = ["q", "k", "v", "cx", "cc", "cb", "o"]
    CX, CC, CB, O = range(3, 7)
    MIX = 8
    COLUMN = {"cx": 0, "cb": DC, "cc": 2 * DC, "q": 3 * DC, "k": 3 * DC + DM, "v": 3 * DC + 2 * DM,
              "o": 3 * DC + 3 * DM}
    NIN = len(PASSES_IN)
    PASSES = NIN + 4
    NPU = GU + C * PASSES
    NUU = 2 * TILES
    TB = T // 4
    PICK_TILES, GATE_TILES = 26, TB // 2
    REST0 = PICK_TILES + GATE_TILES
    REST = TILES - REST0
    B4, Q32, C16 = 4, 32, C
    unit0 = lambda p: GU + C * p

    def half_of(p):
        return p % 2 if p < NIN + 2 else (p + 1) % 2

    def slot_of(n):
        return n % RAWS

    def landed_at(n):
        return 16 * (n // RAWS + 1)

    def tile_slot(i):
        return (i + 1) % 2

    def tile_landed_at(i):
        return 16 * (min(i, REST0 - 2 + i % 2) // 2 + 1) + 16 * B4 * max((i - REST0) // 2 + 1, 0)

    w_in2, w_out2, w_query2 = w_in[0], w_out[0], w_query[0]
    x2 = x[0].rearrange("(a p) d -> p a d", p=P)
    out2 = out[0].rearrange("(a p) d -> p a d", p=P)
    u_rows = expert_u[0].rearrange("(i p) d -> p i d", p=P)
    u_quads = expert_u[0].rearrange("(i e q) (b f) -> b q i e f", e=B4, q=Q32, b=B4)
    v_rows = expert_v[0].rearrange("(i p) d -> p i d", p=P)

    def pass_weights(p):
        if p < NIN:
            w, c0 = w_in2, COLUMN[PASSES_IN[p]]
        elif p < NIN + 2:
            w, c0 = w_out2, (p - NIN) * UW
        else:
            w, c0 = w_query2, (p - NIN - 2) * UW
        return w.rearrange("(k r) n -> r k n", r=P)[:, :, c0:c0 + UW]

    gate_cols = w_in2.rearrange("(k r) n -> r k n", r=P)[:, :, w_in2.shape[1] - P:w_in2.shape[1]]

    with ExitStack() as ctx:
        def sb(name, shape, dt=F32):
            return ctx.enter_context(nc.sbuf_tensor(name, shape, dt))

        def sem(name):
            return ctx.enter_context(nc.semaphore(name))

        x_kept = nc.dram_tensor("x_kept", (2, D, T), F32, kind="Internal").ap()
        x1_kept = nc.dram_tensor("x1_kept", (P, TT * D), F32, kind="Internal").ap()

        A = sb("A", [P, TILES * T])
        A3 = A[:, :].rearrange("p (i t) -> p i t", t=T)
        x_hi = sb("x_hi", [P, C * T], F32R)
        x_lo = sb("x_lo", [P, C * T], F32R)
        w_hi = sb("w_hi", [P, 2, UW], F32R)
        w_lo = sb("w_lo", [P, 2, UW], F32R)
        raw = sb("raw", [P, RAWS, UW])
        xh3 = x_hi[:, :].rearrange("p (c t) -> p c t", t=T)
        xl3 = x_lo[:, :].rearrange("p (c t) -> p c t", t=T)
        v_hi = x_hi[:, :].rearrange("p (s n) -> p s n", n=UW)
        v_lo = x_lo[:, :].rearrange("p (s n) -> p s n", n=UW)
        a_hi = w_hi[:, :, 0:T]
        a_lo = w_lo[:, :, 0:T]

        ident = sb("ident", [P, P])
        iota = sb("iota", [P, P], BF16)
        picks = sb("picks", [P, 3, T], BF16)
        parts = sb("parts", [P, 2, T])
        hot = sb("hot", [P, 2, 4, 4, P], BF16)
        hot_j = sb("hot_j", [P, 4, P], BF16)
        turned_u = hot[:, :, :, :, :].rearrange("p s k t n -> p (s k t n)").bitcast(F32)\
            .rearrange("p (s n) -> p s n", s=2)
        act_out = sb("act_out", [P, 2, T])
        COLS = 2 * C + UC + 3 * UC
        bias_i = sb("bias_i", [NH, 1])
        bias_f = sb("bias_f", [NH, 1])
        stat = sb("stat", [P, 64])
        ssq = sb("ssq", [P, 8])

        raw_tile = raw[:, :, :].rearrange("p (s h) n -> p s (h n)", h=2)
        area = [0]

        def work(words):
            a = A[:, area[0]:area[0] + words]
            area[0] += words
            assert area[0] <= TILES * T
            return a

        proj = {}
        for name in PASSES_IN:
            proj[name] = work(UC * T).rearrange("p (c t) -> p c t", t=T)
        x_res = work(TT * D).rearrange("p (a d) -> p a d", a=TT)
        xs = work(TT * D).rearrange("p (a d) -> p a d", a=TT)
        mixT = work(C * T).rearrange("p (c t) -> p c t", t=T)
        v_nat = work(TT * NH * (DH + 1)).rearrange("p (a h v) -> p a h v", a=TT, h=NH)
        sw = work(NH * 384).rearrange("p (h j) -> p h j", h=NH)
        causal = work(384)
        gate_acc = work(T)
        gate_nat = work(TT * GATES).rearrange("p (a g) -> p a g", a=TT)
        rows = mixT[:, UC:UC + 8, :]
        col_rows = work(P)[0:COLS, :]
        cols = work(COLS)
        g_mix, g_ffn = cols[:, 0:C], cols[:, C:2 * C]
        g_ml = cols[:, 2 * C:2 * C + UC]
        taps = cols[:, 2 * C + UC:].rearrange("p (w c) -> p w c", w=3)
        select = work(NH * P).rearrange("p (h m) -> p h m", h=NH)
        aN = work(TT * NH).rearrange("p (a h) -> p a h", a=TT)
        limN = work(TT * NH).rearrange("p (a h) -> p a h", a=TT)
        h_nat = xs.rearrange("p a (h v) -> p a h v", v=DH)[:, :, 0:NH, :]
        mixoT = A[:, 0:C * T].rearrange("p (c t) -> p c t", t=T)
        at = C * T
        qT = A[:, at:at + C * T].rearrange("p (c t) -> p c t", t=T)
        at += C * T
        scores = A[:, at:at + 2 * PH * TT * NK].rearrange("p (g n) -> p g n", n=NK)
        at += 2 * PH * TT * NK
        assert at <= NIN * UC * T
        at = NIN * UC * T + 2 * TT * D
        cand = A[:, at:at + TT * PH * 256].rearrange("p (g n) -> p g n", n=256)
        at += TT * PH * 256
        left = A[:, at:at + 512].rearrange("p (s n) -> p s n", n=256)
        at += 512
        keys = A[:, at:at + 2 * DK].rearrange("p (s d) -> p s d", s=2)
        at += 2 * DK
        keysT = A[:, at:at + 2 * NK].rearrange("p (s n) -> p s n", s=2)
        at += 2 * NK
        top_v = A[:, at:at + 2 * PH * TT * TOPK].rearrange("p (g k) -> p g k", k=TOPK)
        at += 2 * PH * TT * TOPK
        top_i = A[:, at:at + 2 * PH * TT * TOPK].bitcast(U32).rearrange("p (g k) -> p g k", k=TOPK)
        at += 2 * PH * TT * TOPK
        top_f = A[:, at:at + 2 * PH * TT * TOPK].rearrange("p (g k) -> p g k", k=TOPK)
        at += 2 * PH * TT * TOPK
        best_v = A[:, at:at + TT * PICKS].rearrange("p (g k) -> p g k", k=TOPK)
        at += TT * PICKS
        best_i = A[:, at:at + TT * PICKS].bitcast(U32).rearrange("p (g k) -> p g k", k=TOPK)
        at += TT * PICKS
        half_i = A[:, at:at + 2 * TT * PICKS].bitcast(U32).rearrange("p (s g) -> p s g", s=2)
        at += 2 * TT * PICKS
        half_f = A[:, at:at + 2 * TT * PICKS].rearrange("p (s g) -> p s g", s=2)
        at += 2 * TT * PICKS
        assert at <= TILES * T, at
        WORK_END = at
        match = scores.rearrange("p g n -> p (g n)").rearrange("p (g k a) -> p g k a", k=TOPK, a=TOPK)
        at = 12288
        found = A[:, at:at + 3 * TT * PICKS].rearrange("p (s g) -> p s g", s=3)
        at += 3 * TT * PICKS
        iota16 = A[:, at:at + TOPK]
        at += TOPK
        shifted = A[:, at:at + TT * PICKS].rearrange("p (g k) -> p g k", k=TOPK)
        at += TT * PICKS
        total = A[:, at:at + TT * PH]
        at += TT * PH
        rest = A[:, at:at + 2 * T].rearrange("p (s t) -> p s t", s=2)
        at += 2 * T
        assert at <= NIN * UC * T and PICK_TILES * T <= 8192
        x1_back = A[:, 0:TT * D].rearrange("p (a d) -> p a d", a=TT)
        g_final = A[:, TT * D:TT * D + D]
        y_out = A[:, TT * D + D:2 * TT * D + D].rearrange("p (a d) -> p a d", a=TT)
        spare = A[:, 2 * TT * D + D:3 * TT * D + D].rearrange("p (a d) -> p a d", a=TT)
        FREED = (2 * TT * D + D) // T + 2

        ps = ctx.enter_context(nc.psum_tensor("ps", [P, 8, 512], F32))
        flat = ps[:, :, :].rearrange("p b n -> p (b n)")
        chunks16 = flat.rearrange("p (c t) -> p c t", t=T)
        natural = flat.rearrange("p (a d) -> p a d", a=TT)
        back = flat[:, 2048:4096].rearrange("p (a d) -> p a d", a=TT)

        raw_landed = [sem(f"raw_landed{i}") for i in range(RAWS)]
        x_landed = [sem(f"x_landed{i}") for i in range(2 * TT)]
        mix_gain_landed, small_landed, keys_landed = (sem("mix_gain_landed"), sem("small_landed"),
                                                      sem("keys_landed"))
        cols_turned, cols_ready = sem("cols_turned"), sem("cols_ready")
        constants, masks = sem("constants"), sem("masks")
        squares_done, mean_done, root_done, rstd_done = (sem("squares_done"), sem("mean_done"),
                                                         sem("root_done"), sem("rstd_done"))
        newton, scaled, scaled_act, inv_ready, turned, hi_taken, lo_taken = (
            sem("newton"), sem("scaled"), sem("scaled_act"), sem("inv_ready"), sem("turned"), sem("hi_taken"),
            sem("lo_taken"))
        warm = sem("warm")
        half_out_act, half_out_dve = sem("half_out_act"), sem("half_out_dve")
        hi_split, lo_split, unit_done, pass_out = (sem("hi_split"), sem("lo_split"), sem("unit_done"),
                                                   sem("pass_out"))
        gates_out, gate_step_pe, gate_step_act, gate_step_dve = (
            sem("gates_out"), sem("gate_step_pe"), sem("gate_step_act"), sem("gate_step_dve"))
        v_turned, v_ready, qk_done, expo_in, expo_out, sw_half, sw_ready, pv_done = (
            sem("v_turned"), sem("v_ready"), sem("qk_done"), sem("expo_in"), sem("expo_out"),
            sem("sw_half"), sem("sw_ready"), sem("pv_done"))
        den_ready, h_scaled, h_squared, h_rstd, h_ready, h_turned = (
            sem("den_ready"), sem("h_scaled"), sem("h_squared"), sem("h_rstd"), sem("h_ready"), sem("h_turned"))
        h_out, conv_step, mix_ready = sem("h_out"), sem("conv_step"), sem("mix_ready")
        mixo_turned, x1_ready, x1_stored = sem("mixo_turned"), sem("x1_ready"), sem("x1_stored")
        keys_turned, keysT_ready, s_done, s_copied = (sem("keys_turned"), sem("keysT_ready"),
                                                      sem("s_done"), sem("s_copied"))
        top_step, soft_in, soft_out, found_ready, found_turned, picks_ready = (
            sem("top_step"), sem("soft_in"), sem("soft_out"), sem("found_ready"), sem("found_turned"),
            sem("picks_ready"))
        hot_i_ready, hot_j_ready, hot_ready, parts_ready, gate_block, gate_applied = (
            sem("hot_i_ready"), sem("hot_j_ready"), sem("hot_ready"), sem("parts_ready"), sem("gate_block"),
            sem("gate_applied"))
        tile_landed = [sem(f"tile_landed{i}") for i in range(2)]
        dve_turned, ones_set, cand_used = sem("dve_turned"), sem("ones_set"), sem("cand_used")
        x_kept_sem, x_ordered = sem("x_kept_sem"), [sem(f"x_ordered{i}") for i in range(2)]
        u_turned, uh_split, ul_split, u_done, gelu_done, gated = (
            sem("u_turned"), sem("uh_split"), sem("ul_split"), sem("u_done"), sem("gelu_done"), sem("gated"))
        ah_ready, al_ready, vh_split, vl_split, v_done = (
            sem("ah_ready"), sem("al_ready"), sem("vh_split"), sem("vl_split"), sem("v_done"))
        tail_landed, x2_ready, out_stored = sem("tail_landed"), sem("x2_ready"), sem("out_stored")
        out_ready = [sem(f"out_ready{a}") for a in range(TT)]

        HEADS = range(NH)
        QK_BANK = (6, 7, 4, 5)
        NORM_MIX, NORM_FFN, NORM_FINAL = range(3)
        MS, ROOT, INV, TMP = (stat[:, TT * i:TT * (i + 1)] for i in range(4))
        HN = TT * NH
        NQ, DEN, HSS, HMS, HROOT, HINV, HTMP = (stat[:, 8 + HN * i:8 + HN * (i + 1)] for i in range(7))
        NSQ = (2, 3, 2)
        SQ_PARTS = (((0, UW), (UW, 2 * UW)), ((0, UW), (UW, UW + 512), (UW + 512, 2 * UW)), ((0, UW), (UW, 2 * UW)))
        SQ0 = (0, NSQ[0] * TT, (NSQ[0] + NSQ[1]) * TT)
        sums = lambda r: ssq[:, 0:TT * NSQ[r]].rearrange("p (a n) -> p a n", a=TT)

        with nc.Block() as block:

            @block.sync
            def _(sp):
                for h in range(2):
                    for a in range(TT):
                        sp.dma_start(x_res[:, a, h * UW:(h + 1) * UW], x2[:, a, h * UW:(h + 1) * UW])\
                            .then_inc(x_landed[h * TT + a], 16)
                for n in range(GU):
                    sp.dma_start(raw[:, slot_of(n), :].rearrange("p (k m) -> p k m", m=P),
                                 gate_cols[:, n * UC:(n + 1) * UC, :]).then_inc(raw_landed[slot_of(n)], 16)
                for p in range(PASSES):
                    w = pass_weights(p)

                    def load(k, j):
                        sp.dma_start(raw[:, slot_of(unit0(p) + j), :], w[:, k, :])\
                            .then_inc(raw_landed[slot_of(unit0(p) + j)], 16)

                    for j in range(RAWS):
                        if unit0(p) + j >= RAWS:
                            sp.wait_ge(lo_split, unit0(p) + j - RAWS + 1)
                        load(j, j)
                    with sp.Fori(1, C // RAWS) as it:
                        for j in range(RAWS):
                            sp.wait_ge(lo_split, it * RAWS + (unit0(p) + j - RAWS + 1))
                            load(bass.ds(it * RAWS + j, 1), j)
                def load_tile(s, i):
                    sp.dma_start(raw_tile[:, s, :], u_rows[:, i, :]).then_inc(tile_landed[s], 16)

                def load_quads(s, i):
                    for b in range(B4):
                        sp.dma_start(raw_tile[b * Q32:(b + 1) * Q32, s, :].rearrange("q (e f) -> q e f", e=B4),
                                     u_quads[b, :, i, :, :]).then_inc(tile_landed[s], 16)

                for i in range(2):
                    sp.wait_ge(lo_split, NPU - 2 + 2 * i)
                    load_tile(tile_slot(i), i)
                with sp.Fori(1, REST0 // 2) as it:
                    for i in range(2):
                        sp.wait_ge(u_turned, it * 4 + (2 * i - 2))
                        load_tile(tile_slot(i), bass.ds(it * 2 + i, 1))
                for i in range(2):
                    sp.wait_ge(u_turned, 2 * REST0 + 2 * i - 2)
                    load_quads(tile_slot(i), REST0 + i)
                sp.wait_ge(x_kept_sem, 16 * 8)
                for half in range(2):
                    sp.wait_ge(u_done, 2 * REST0 - 1 + half)
                    cs = slice(half * UC, (half + 1) * UC)
                    for n, xx in enumerate((xh3, xl3)):
                        for b in range(B4):
                            sp.dma_start(xx[b * Q32:(b + 1) * Q32, cs, :].bitcast(F32),
                                         x_kept[n].rearrange("(b c q) t -> b q c t", b=B4, q=Q32)[b, :, cs, :])\
                                .then_inc(x_ordered[half], 16)
                with sp.Fori(1, REST // 2) as it:
                    for i in range(2):
                        sp.wait_ge(dve_turned, it * 4 + (2 * i - 2))
                        for b in range(B4):
                            sp.dma_start(
                                raw_tile[b * Q32:(b + 1) * Q32, tile_slot(i), :].rearrange("q (e f) -> q e f", e=B4),
                                u_quads[b, :, bass.ds(it * 2 + (REST0 + i), 1), :, :].rearrange("q i e f -> q (i e) f"))\
                                .then_inc(tile_landed[tile_slot(i)], 16)
                for n in range(RAWS):
                    sp.wait_ge(dve_turned, 2 * REST - (2 if n < 2 else 0))
                    sp.dma_start(raw[:, slot_of(NPU + n), :], v_rows[:, n // 2, (n % 2) * UW:(n % 2 + 1) * UW])\
                        .then_inc(raw_landed[slot_of(NPU + n)], 16)
                with sp.Fori(1, NUU // RAWS) as it:
                    for j in range(RAWS):
                        sp.wait_ge(vl_split, it * RAWS + (j - RAWS + 1))
                        sp.dma_start(raw[:, slot_of(NPU + j), :],
                                     v_rows[:, bass.ds(it * 2 + j // 2, 1), (j % 2) * UW:(j % 2 + 1) * UW])\
                            .then_inc(raw_landed[slot_of(NPU + j)], 16)
                for h in range(2):
                    for a in range(TT):
                        sp.wait_ge(out_ready[a], h + 1)
                        sp.dma_start(out2[:, a, h * UW:(h + 1) * UW], y_out[:, a, h * UW:(h + 1) * UW])\
                            .then_inc(out_stored, 16)
                sp.wait_ge(out_stored, 16 * TT * 2)

            @block.gpsimd
            def _(pool):
                def first_part(b, tokens, made, free):
                    pool.wait_ge(hot_j_ready, made)
                    if free is not None:
                        pool.wait_ge(gate_block, free)
                    nc.gpsimd.tensor_tensor(hot[:, b, 1, :, :], hot_j[:, :, :],
                                            picks[:, 2, tokens].unsqueeze(2).broadcast_to([P, 4, P]), ALU.mult)                        .then_inc(hot_ready, 1)

                def gelu_to_A(i, b, ready):
                    pool.wait_ge(gelu_done, ready)
                    nc.gpsimd.tensor_tensor(A3[:, i, :], act_out[:, b, :], A3[:, i, :], ALU.mult).then_inc(gated, 1)

                pool.memset(ident[:, :], 0.0).then_inc(constants, 1)
                pool.iota(iota[:, :], [[1, P]], base=0, channel_multiplier=0,
                          allow_small_or_imprecise_dtypes=True).then_inc(constants, 1)
                pool.wait_ge(constants, 2)
                pool.affine_select(out=ident[:, :], in_=ident[:, :], compare_op=ALU.not_equal, fill=1.0,
                                   base=0, pattern=[[-1, P]], channel_multiplier=1).then_inc(constants, 1)
                pool.memset(causal, 1.0).then_inc(masks, 1)
                pool.memset(select, 0.0).then_inc(masks, 1)
                pool.wait_ge(masks, 2)
                for c0 in (0, 2 * P):
                    pool.affine_select(out=causal[:, c0:c0 + P], in_=causal[:, c0:c0 + P], compare_op=ALU.is_ge,
                                       fill=0.0, base=0, pattern=[[1, P]], channel_multiplier=-1)\
                        .then_inc(masks, 1)
                pool.affine_select(out=select, in_=select, compare_op=ALU.not_equal, fill=1.0, base=0,
                                   pattern=[[-1, NH], [0, P]], channel_multiplier=1).then_inc(masks, 1)
                pool.wait_ge(x1_ready, 3 * TT)
                for n in range(4):
                    cs = slice(n * UW, (n + 1) * UW)
                    pool.dma_start(x1_kept[:, cs], x_res.rearrange("p a d -> p (a d)")[:, cs]).then_inc(x1_stored, 16)
                    pool.wait_ge(x1_stored, 16 * (n + 1))
                pool.wait_ge(lo_taken, C + MIX + C)
                for n in range(8):
                    cs = slice(n % 4 * 4, n % 4 * 4 + 4)
                    pool.dma_start(x_kept[n // 4].rearrange("(c p) t -> p c t", p=P)[:, cs, :],
                                   (xh3, xl3)[n // 4][:, cs, :].bitcast(F32)).then_inc(x_kept_sem, 16)
                    pool.wait_ge(x_kept_sem, 16 * (n + 1))
                pool.wait_ge(s_copied, 2 * TT)
                for a, b in ((PICK_TILES * T, 8192), (NIN * UC * T, NIN * UC * T + 2 * TT * D), (WORK_END, TILES * T)):
                    pool.memset(A[:, a:b], 1.0).then_inc(ones_set, 1)
                pool.wait_ge(cand_used, 1)
                pool.memset(cand, 1.0).then_inc(ones_set, 1)
                pool.wait_ge(picks_ready, 1)
                first_part(0, slice(0, 4), 1, None)
                for a, b in ((8192, NIN * UC * T), (NIN * UC * T + 2 * TT * D + TT * PH * 256, WORK_END)):
                    pool.memset(A[:, a:b], 1.0).then_inc(ones_set, 1)
                for g in range(1, 4):
                    first_part(g % 2, slice(4 * g, 4 * g + 4), g + 1, g - 1 if g >= 2 else None)
                with pool.Fori(1, TB // 4) as it:
                    for j in range(4):
                        first_part(j % 2, bass.ds(it * 16 + 4 * j, 4), it * 4 + (j + 1), it * 4 + (j - 1))
                pool.wait_ge(gate_applied, TB)
                with pool.Fori(0, REST // 2) as it:
                    gelu_to_A(bass.ds(it * 2 + (REST0 - 1), 1), 1, it * 2 + REST0)
                    gelu_to_A(bass.ds(it * 2 + REST0, 1), 0, it * 2 + (REST0 + 1))
                gelu_to_A(TILES - 1, 1, TILES)
                pool.wait_ge(al_ready, FREED)
                for n in range(4):
                    cs = slice(n * UW, (n + 1) * UW)
                    pool.dma_start(x1_back.rearrange("p a d -> p (a d)")[:, cs], x1_kept[:, cs])\
                        .then_inc(tail_landed, 16)
                    pool.wait_ge(tail_landed, 16 * (n + 1))
                pool.dma_start(g_final, norm_final_g.rearrange("(o d) -> o d", o=1).broadcast_to([P, D]))\
                    .then_inc(tail_landed, 16)

            @block.tensor
            def _(pe):
                def turn_x(round_no):
                    if round_no == NORM_MIX:
                        pe.wait_ge(mix_gain_landed, 16)
                        nc.tensor.transpose(ps[:, 7, 0:C], col_rows[0:C, :], ident[0:C, 0:C]).then_inc(cols_turned, 1)
                    for c in range(C):
                        if c == 0:
                            pe.wait_ge(scaled, 3 * round_no + TT)
                        elif c == UC:
                            pe.wait_ge(scaled, 3 * round_no + TT + 1)
                            pe.wait_ge(scaled_act, round_no + 1)
                        elif c == C - 2 and round_no == NORM_MIX:
                            pe.wait_ge(cols_ready, 1)
                        for a in range(TT):
                            last = nc.tensor.transpose(chunks16[:, c, a * P:(a + 1) * P],
                                                       xs[:, a, c * P:(c + 1) * P], ident[:, :])
                        if c % 2 == 1:
                            last.then_inc(turned, 1)

                def project(p, k0=0, k1=C):
                    acc = flat[:, half_of(p) * 2048:(half_of(p) + 1) * 2048]

                    def unit(u_wait, k, j, first):
                        s = (unit0(p) + j) % 2
                        pe.wait_ge(lo_split, u_wait)
                        for c in range(UC):
                            for n, (w, xx) in enumerate(((w_hi, xh3), (w_hi, xl3), (w_lo, xh3))):
                                last = nc.tensor.matmul(
                                    acc[:, c * T:(c + 1) * T], w[:, s, c * P:(c + 1) * P], xx[:, k, :],
                                    start=first and n == 0 and c % 2 == 0, stop=False, skip_group_check=True)
                        last.then_inc(unit_done, 1)

                    step = 4 if k0 % 4 == 0 and k1 % 4 == 0 and k1 - k0 > 4 else 2
                    if k0 == 0:
                        if 2 <= p < NIN + 2:
                            pe.wait_ge(pass_out, p - 1)
                        for j in range(step):
                            unit(unit0(p) + j + 1, j, j, j == 0)
                        k0 = step
                    if k1 == k0:
                        return
                    if k1 - k0 == step:
                        for j in range(step):
                            unit(unit0(p) + k0 + j + 1, k0 + j, j, False)
                    else:
                        with pe.Fori(k0 // step, k1 // step) as it:
                            for j in range(step):
                                unit(it * step + (unit0(p) + j + 1), bass.ds(it * step + j, 1), j, False)

                pe.wait_ge(constants, 3)
                turn_x(NORM_MIX)
                for n in range(GU):
                    pe.wait_ge(lo_split, n + 1)
                    pe.wait_ge(lo_taken, (UC + 2, C)[n])
                    for c in range(UC):
                        for m, (w, xx) in enumerate(((w_hi, xh3), (w_hi, xl3), (w_lo, xh3))):
                            last = nc.tensor.matmul(ps[:, 4, 0:T], w[:, n % 2, c * P:(c + 1) * P],
                                                    xx[:, n * UC + c, :], start=n == 0 and c == 0 and m == 0,
                                                    stop=n == GU - 1 and c == UC - 1 and m == 2)
                    last.then_inc(unit_done, 1)
                for p in range(CX):
                    if p == 1:
                        pe.wait_ge(gates_out, 1)
                    project(p)

                project(CX, 0, 6)
                def turn_v(a):
                    for c in range(UC):
                        last = nc.tensor.transpose(flat[:, UW + c * P:UW + (c + 1) * P],
                                                   proj["v"][:, c, a * P:(a + 1) * P], ident[:, :])
                    last.then_inc(v_turned, 1)

                pe.wait_ge(pass_out, CX)
                for a in range(TT):
                    last = nc.tensor.transpose(ps[:, 0, a * P:(a + 1) * P], gate_acc[:, a * P:(a + 1) * P],
                                               ident[:, :])
                last.then_inc(gate_step_pe, 1)
                pe.wait_ge(small_landed, 16 * 7)
                nc.tensor.transpose(ps[:, 0, T:T + COLS], col_rows, ident[0:COLS, 0:COLS]).then_inc(cols_turned, 1)
                turn_v(0)
                project(CX, 6, 8)
                pe.wait_ge(gate_step_act, 1)
                for g in range(2):
                    for a in range(TT):
                        last = nc.tensor.transpose(ps[0:NH, 1, g * T + a * P:g * T + (a + 1) * P],
                                                   gate_nat[:, a, g * NH:(g + 1) * NH], ident[:, :])
                last.then_inc(gate_step_pe, 1)
                pe.wait_ge(v_ready, 2)
                turn_v(1)
                project(CX, 8, 16)

                pe.wait_ge(cols_ready, 2)
                pe.wait_ge(v_ready, TT + 1)
                pe.wait_ge(gate_step_dve, 2)
                project(CC, 0, 6)
                pe.wait_ge(pass_out, CC)
                pe.wait_ge(gate_step_dve, 11)
                pe.wait_ge(masks, 5)
                for h in HEADS:
                    last = nc.tensor.matmul(ps[:, 4 + h // 2, (h % 2) * T:(h % 2 + 1) * T], select[0:NH, h, :],
                                            rows[0:NH, 4, :], start=True, stop=True)
                last.then_inc(gate_step_pe, 1)
                pe.wait_ge(gate_step_act, 4)
                for r, o in ((3, 0), (6, TT * NH)):
                    for a in range(TT):
                        last = nc.tensor.transpose(ps[:, 7, o + a * NH:o + (a + 1) * NH],
                                                   rows[0:NH, r, a * P:(a + 1) * P], ident[0:NH, 0:NH])
                last.then_inc(gate_step_pe, 1)
                project(CC, 6, 8)

                def keys_queries(h):
                    for l, j0, o in ((0, 0, 0), (1, P, T)):
                        for c in range(DH // P):
                            last = nc.tensor.matmul(ps[:, QK_BANK[h], o:o + T - j0],
                                                    proj["k"][:, h * DH // P + c, l * P:(l + 1) * P],
                                                    proj["q"][:, h * DH // P + c, j0:T],
                                                    start=c == 0, stop=c == DH // P - 1)
                    last.then_inc(qk_done, 1)

                keys_queries(0)
                pe.wait_ge(gate_step_dve, 13)
                keys_queries(1)
                project(CC, 8, 10)
                pe.wait_ge(expo_in, NH)
                keys_queries(2)
                keys_queries(3)
                project(CC, 10, 16)

                def weigh(jt):
                    for h in HEADS:
                        o = ps[:, h, 0:DH + 1]
                        if jt == 0:
                            last = nc.tensor.matmul(o, sw[:, h, 0:P], v_nat[:, 0, h, :], start=True, stop=True)
                        else:
                            nc.tensor.matmul(o, sw[:, h, P:T], v_nat[:, 0, h, :], start=True, stop=False)
                            last = nc.tensor.matmul(o, sw[:, h, T:T + P], v_nat[:, 1, h, :], start=False, stop=True)
                        last.then_inc(pv_done, 1)

                pe.wait_ge(sw_ready, NH)
                project(CB, 0, 6)
                pe.wait_ge(pass_out, CB)
                weigh(0)
                project(CB, 6, 10)
                pe.wait_ge(h_scaled, NH)
                weigh(1)
                project(CB, 10, 16)

                pe.wait_ge(h_scaled, HN)
                project(O, 0, 6)
                pe.wait_ge(pass_out, O)
                pe.wait_ge(h_ready, HN)
                for c in range(UC):
                    for a in range(TT):
                        last = nc.tensor.transpose(
                            chunks16[:, UC + c, a * P:(a + 1) * P],
                            h_nat[:, a, c * P // DH, c * P % DH:c * P % DH + P], ident[:, :])
                last.then_inc(h_turned, 1)
                project(O, 6, 16)

                pe.wait_ge(h_out, 3)
                pe.wait_ge(lo_taken, C + MIX // 2)
                project(NIN, 0, 8)
                pe.wait_ge(lo_taken, C + MIX)
                project(NIN, 8, 16)
                def turn_mixed(c0, c1):
                    for a in range(TT):
                        for c in range(c0, c1):
                            last = nc.tensor.transpose(back[:, a, (c % UC) * P:(c % UC + 1) * P],
                                                       mixoT[:, c, a * P:(a + 1) * P], ident[:, :])
                        last.then_inc(mixo_turned, 1)

                project(NIN + 1, 0, 6)
                pe.wait_ge(pass_out, NIN + 1)
                turn_mixed(0, UC)
                project(NIN + 1, 6, 16)
                pe.wait_ge(x1_ready, TT)
                pe.wait_ge(half_out_act, 1)
                turn_mixed(UC, UC + 4)
                pe.wait_ge(half_out_dve, 1)
                turn_mixed(UC + 4, C)
                turn_x(NORM_FFN)
                pe.wait_ge(lo_taken, C + MIX + UC)
                project(NIN + 2, 0, 2)
                pe.wait_ge(lo_taken, C + MIX + C)
                project(NIN + 2, 2, 16)
                project(NIN + 3, 0, 6)
                pe.wait_ge(pass_out, NIN + 2)
                pe.wait_ge(keys_landed, 32)
                for s in range(2):
                    last = nc.tensor.transpose(ps[:, 0, s * P:(s + 1) * P], keys[:, s, :], ident[:, :])
                last.then_inc(keys_turned, 1)

                def key_scores(half):
                    for a in range(TT):
                        for g in range(half * PH, (half + 1) * PH):
                            o = half * 2048 + a * UW + (g % PH) * NK
                            last = nc.tensor.matmul(flat[:, o:o + NK], qT[:, g, a * P:(a + 1) * P],
                                                    keysT[:, g % 2, :], start=True, stop=True)
                        last.then_inc(s_done, 1)

                project(NIN + 3, 6, 8)
                pe.wait_ge(keysT_ready, 1)
                key_scores(0)
                project(NIN + 3, 8, 16)
                pe.wait_ge(s_copied, TT)

                def turn_unit(j, landed, free):
                    s = tile_slot(j // 2)
                    if j % 2 == 0:
                        pe.wait_ge(tile_landed[s], landed)
                    if free is not None:
                        pe.wait_ge(ul_split, free)
                    o = (j % 2) * UW
                    for c in range(UC):
                        last = nc.tensor.transpose(flat[:, o + c * P:o + (c + 1) * P],
                                                   raw_tile[:, s, o + c * P:o + (c + 1) * P], ident[:, :])
                    last.then_inc(u_turned, 1)

                def score_unit(j, ready, free, bank0=4):
                    pe.wait_ge(ul_split, ready)
                    if free is not None:
                        pe.wait_ge(gelu_done, free)
                    for c in range(UC):
                        for n, (w, xx) in enumerate(((w_hi, xh3), (w_hi, xl3), (w_lo, xh3))):
                            last = nc.tensor.matmul(ps[:, bank0 + j // 2, 0:T], w[:, j % 2, c * P:(c + 1) * P],
                                                    xx[:, (j % 2) * UC + c, :],
                                                    start=j % 2 == 0 and c == 0 and n == 0,
                                                    stop=j % 2 == 1 and c == UC - 1 and n == 2)
                    last.then_inc(u_done, 1)

                def turn_and_score(j, it, u0):
                    turn_unit(j, it * 16 + tile_landed_at(u0 // 2 + j // 2), it * 4 + (u0 + j - 1))
                    score_unit((j - 1) % 4, it * 4 + (u0 + j),
                               None if j in (0, 2) else it * 2 + (u0 // 2 + (j - 1) // 2 - 1))

                turn_unit(0, tile_landed_at(0), None)
                turn_unit(1, None, None)
                pe.wait_ge(half_out_act, 2)
                pe.wait_ge(half_out_dve, 2)
                key_scores(1)
                pe.wait_ge(s_copied, TT + 1)
                score_unit(0, 1, None)
                turn_unit(2, tile_landed_at(1), 1)
                score_unit(1, 2, None)
                turn_unit(3, None, 2)
                score_unit(2, 3, None)
                with pe.Fori(1, PICK_TILES // 2 - 1) as it:
                    for j in range(4):
                        turn_and_score(j, it, 0)
                pe.wait_ge(found_ready, 1)
                for s in range(3):
                    for a in range(TT):
                        last = nc.tensor.transpose(flat[:, 6 * 512 + s * T + a * P:6 * 512 + s * T + (a + 1) * P],
                                                   found[:, s, a * PICKS:(a + 1) * PICKS], ident[:, :])
                last.then_inc(found_turned, 1)
                for j in range(4):
                    turn_and_score(j, PICK_TILES // 2 - 1, 0)

                def gate_tokens(b, made, applied):
                    pe.wait_ge(hot_i_ready, made)
                    pe.wait_ge(hot_ready, made)
                    pe.wait_ge(parts_ready, made)
                    if applied is not None:
                        pe.wait_ge(gate_applied, applied)
                    for t in range(4):
                        for part in range(3):
                            last = nc.tensor.matmul(ps[:, 6 + b, t * P:(t + 1) * P], hot[:, b, 1 + part, t, :],
                                                    hot[:, b, 0, t, :], start=t == 0 and part == 0,
                                                    stop=t == 3 and part == 2, skip_group_check=True)
                    last.then_inc(gate_block, 1)

                def gate_body(it, first):
                    for j in range(4):
                        turn_and_score(j, it, 2 * PICK_TILES)
                        if not (first and j == 0):
                            if first and j == 1:
                                pe.wait_ge(picks_ready, 1)
                            gate_tokens((j - 1) % 2, it * 4 + j, None if first and j < 3 else it * 4 + (j - 2))

                gate_body(0, True)
                with pe.Fori(1, TB // 4) as it:
                    gate_body(it, False)
                score_unit(3, 2 * REST0, None)
                gate_tokens(1, TB, TB - 2)

                for j in range(4):
                    if j < 2:
                        pe.wait_ge(x_ordered[j], 16 * 2 * B4)
                    if j % 2 == 0:
                        pe.wait_ge(gate_applied, TB - 1 + j // 2)
                    score_unit(j, 2 * REST0 + j + 1, None, 6)
                with pe.Fori(1, REST // 2) as it:
                    for j in range(4):
                        score_unit(j, it * 4 + (2 * REST0 + j + 1),
                                   it * 2 + (REST0 + j // 2 - 1) if j % 2 == 0 else None, 6)


                def sum_unit(j, v_ok, a_ok, first):
                    pe.wait_ge(vl_split, v_ok)
                    if j % 2 == 0:
                        pe.wait_ge(al_ready, a_ok)
                    half, s, v = j % 2, j // 2, j
                    for a in range(TT):
                        for n, (aa, vv) in enumerate(((a_hi, v_hi), (a_hi, v_lo), (a_lo, v_hi))):
                            for q in range(UW // 512):
                                last = nc.tensor.matmul(
                                    ps[:, a * 4 + half * 2 + q, :], aa[:, s, a * P:(a + 1) * P],
                                    vv[:, v, q * 512:(q + 1) * 512], start=first and n == 0, stop=False,
                                    skip_group_check=True)
                    last.then_inc(v_done, 1)

                for n in range(RAWS):
                    if n == 1:
                        pe.wait_ge(gelu_done, TILES)
                    sum_unit(n, n + 1, n // 2 + 1, n < 2)
                with pe.Fori(1, NUU // RAWS) as it:
                    for j in range(RAWS):
                        sum_unit(j, it * RAWS + (j + 1), it * 2 + (j // 2 + 1), False)

            @block.scalar
            def _(act):
                row = 0
                for v in (norm_mix_g[0], norm_ffn_g[0], mlstm_norm_g[0], conv_w[0, 0], conv_w[0, 1], conv_w[0, 2]):
                    n = v.shape[0] // P
                    act.dma_start(col_rows[row:row + n, :], v.rearrange("(c p) -> c p", p=P))\
                        .then_inc(small_landed if row else mix_gain_landed, 16)
                    row += n
                act.dma_start(bias_i[:, :], b_igate.rearrange("o h -> h o")).then_inc(small_landed, 16)
                act.dma_start(bias_f[:, :], b_fgate.rearrange("o h -> h o")).then_inc(small_landed, 16)

                def squares(src, junk, r, a, n):
                    c0, c1 = SQ_PARTS[r][n]
                    nc.scalar.activation(junk[:, a, c0:c1], src[:, a, c0:c1], ACT.Square,
                                         accum_out=sums(r)[:, a, n:n + 1]).then_inc(squares_done, 1)

                warmed = [0]

                def warm_root():
                    act.wait_ge(warm, warmed[0] + 1)
                    nc.scalar.activation(ssq[:, 7:8], ssq[:, 7:8], ACT.Sqrt).then_inc(warm, 1)
                    warmed[0] += 1

                def root(r):
                    act.wait_ge(mean_done, r + 1)
                    nc.scalar.activation(ROOT, MS, ACT.Sqrt).then_inc(root_done, 1)

                def scale_last(r):
                    act.wait_ge(inv_ready, r + 1)
                    nc.scalar.activation(xs[:, TT - 1, UW:2 * UW], x_res[:, TT - 1, UW:2 * UW], ACT.Copy,
                                         scale=INV[:, TT - 1:TT]).then_inc(scaled_act, 1)

                def take_hi(gain, round_no):
                    for c in range(C):
                        if c % 2 == 0:
                            act.wait_ge(turned, C // 2 * round_no + c // 2 + 1)
                        nc.scalar.activation(xh3[:, c, :], chunks16[:, c, :], ACT.Copy, scale=gain[:, c:c + 1])\
                            .then_inc(hi_taken, 1)

                def hi_unit(u_landed, j, free, n0):
                    act.wait_ge(raw_landed[slot_of(n0 + j)], u_landed)
                    if free is not None:
                        act.wait_ge(unit_done, free)
                    nc.scalar.activation(w_hi[:, (n0 + j) % 2, :], raw[:, slot_of(n0 + j), :], ACT.Copy)\
                        .then_inc(hi_split, 1)

                def evacuate_half(p, q, dst, scale=1.0, func=ACT.Copy, done=None):
                    act.wait_ge(unit_done, unit0(p) + C)
                    o = half_of(p) * 2048 + q * UW
                    last = nc.scalar.activation(dst[:, 4 * q:4 * q + 4, :],
                                                flat[:, o:o + UW].rearrange("p (c t) -> p c t", t=T), func, scale=scale)
                    if done is not None:
                        last.then_inc(done, 1)
                    elif q == 1:
                        last.then_inc(pass_out, 1)

                def evacuate(p, dst, scale=1.0):
                    for q in range(2):
                        evacuate_half(p, q, dst, scale)

                def pass_hi_first(p):
                    for j in range(RAWS):
                        n = unit0(p) + j
                        hi_unit(landed_at(n), j, n - 1 if n >= 2 else None, unit0(p))

                def pass_hi_rest(p):
                    with act.Fori(1, C // RAWS) as it:
                        for j in range(RAWS):
                            n = unit0(p) + j
                            hi_unit(it * 16 + landed_at(n), j, it * RAWS + (n - 1), unit0(p))

                warm_root()
                for n in range(NSQ[NORM_MIX]):
                    for a in range(TT):
                        act.wait_ge(x_landed[n * TT + a], 16)
                        squares(x_res, xs, NORM_MIX, a, n)
                root(NORM_MIX)
                act.wait_ge(cols_turned, 1)
                nc.scalar.activation(cols[:, 0:C], ps[:, 7, 0:C], ACT.Copy).then_inc(cols_ready, 1)
                scale_last(NORM_MIX)
                act.wait_ge(cols_ready, 1)
                for n in range(GU):
                    hi_unit(landed_at(n), n, None, 0)
                take_hi(g_mix, NORM_MIX)
                for p in range(CX):
                    pass_hi_first(p)
                    if p == 0:
                        act.wait_ge(unit_done, GU)
                        nc.scalar.activation(gate_acc, ps[:, 4, 0:T], ACT.Copy).then_inc(gates_out, 1)
                    else:
                        evacuate(p - 1, proj[PASSES_IN[p - 1]], DH ** -0.5 if PASSES_IN[p - 1] == "k" else 1.0)
                    pass_hi_rest(p)

                def hi_to(p, k0, k1):
                    for k in range(k0, k1):
                        n = unit0(p) + k
                        hi_unit(landed_at(n), k, n - 1, unit0(p))

                def v_natural(a):
                    act.wait_ge(v_turned, a + 1)
                    nc.scalar.activation(v_nat[:, a, :, 0:DH], flat[:, UW:2 * UW].rearrange("p (h v) -> p h v", v=DH),
                                         ACT.Copy).then_inc(v_ready, 1)

                def exponential(h):
                    act.wait_ge(expo_in, h + 1)
                    nc.scalar.activation(sw[:, h, :], sw[:, h, :], ACT.Exp, scale=-1.0).then_inc(expo_out, 1)

                def scale_h(jt):
                    act.wait_ge(den_ready, jt + 1)
                    for h in HEADS:
                        g = jt * NH + h
                        nc.scalar.activation(h_nat[:, jt, h, :], ps[:, h, 0:DH], ACT.Copy,
                                             scale=DEN[:, g:g + 1]).then_inc(h_scaled, 1)

                def square_h(jt):
                    act.wait_ge(pv_done, HN)
                    act.wait_ge(h_scaled, (jt + 1) * NH)
                    for h in HEADS:
                        g = jt * NH + h
                        nc.scalar.activation(v_nat[:, jt, h, 0:DH], h_nat[:, jt, h, :], ACT.Square,
                                             accum_out=HSS[:, g:g + 1]).then_inc(h_squared, 1)

                def mixed_hi(m):
                    act.wait_ge(mix_ready, m // 2 + 1 if m < MIX // 2 else m - MIX // 4 + 1)
                    act.wait_ge(unit_done, unit0(O) + (UC if m < MIX // 2 else C))
                    nc.scalar.activation(xh3[:, 2 * m:2 * m + 2, :], mixT[:, 2 * m:2 * m + 2, :], ACT.Copy)\
                        .then_inc(hi_taken, 1)

                hi_to(CX, 0, 5)
                evacuate_half(CX - 1, 0, proj["v"])
                hi_to(CX, 5, 6)
                evacuate_half(CX - 1, 1, proj["v"])
                hi_to(CX, 6, 8)
                act.wait_ge(gate_step_pe, 1)
                act.wait_ge(cols_turned, 2)
                nc.scalar.activation(gate_nat, ps[:, 0, 0:T].rearrange("p (a m) -> p a m", a=TT)[:, :, P - GATES:P],
                                     ACT.Copy).then_inc(gate_step_act, 1)
                nc.scalar.activation(cols[:, C:COLS], ps[:, 0, T + C:T + COLS], ACT.Copy).then_inc(cols_ready, 1)
                v_natural(0)
                hi_to(CX, 8, 10)
                v_natural(1)
                hi_to(CX, 10, 11)
                act.wait_ge(gate_step_dve, 3)
                nc.scalar.activation(rows[0:NH, 5, :], rows[0:NH, 4, :], ACT.Exp, scale=-1.0)\
                    .then_inc(gate_step_act, 1)
                hi_to(CX, 11, 13)
                act.wait_ge(gate_step_dve, 4)
                nc.scalar.activation(rows[0:NH, 4, :], rows[0:NH, 6, :], ACT.Ln).then_inc(gate_step_act, 1)
                hi_to(CX, 13, 16)
                hi_to(CC, 0, 1)
                act.wait_ge(gate_step_dve, 11)
                nc.scalar.activation(rows[0:NH, 6, :], rows[0:NH, 5, :], ACT.Exp, scale=-1.0)\
                    .then_inc(gate_step_act, 1)
                hi_to(CC, 1, 5)
                evacuate_half(CX, 0, proj["cx"])
                hi_to(CC, 5, 6)
                evacuate_half(CX, 1, proj["cx"])
                hi_to(CC, 6, 9)
                exponential(0)
                hi_to(CC, 9, 10)
                exponential(1)
                exponential(2)
                hi_to(CC, 10, 11)
                exponential(3)
                hi_to(CC, 11, 16)
                hi_to(CB, 0, 5)
                evacuate_half(CC, 0, proj["cc"])
                hi_to(CB, 5, 6)
                evacuate_half(CC, 1, proj["cc"])
                hi_to(CB, 6, 9)
                scale_h(0)
                hi_to(CB, 9, 13)
                scale_h(1)
                hi_to(CB, 13, 14)
                square_h(0)
                hi_to(CB, 14, 15)
                square_h(1)
                hi_to(CB, 15, 16)
                hi_to(O, 0, 1)
                act.wait_ge(h_rstd, 1)
                nc.scalar.activation(HROOT, HMS, ACT.Sqrt).then_inc(h_squared, 1)
                hi_to(O, 1, 5)
                evacuate_half(CB, 0, proj["cb"])
                hi_to(O, 5, 6)
                evacuate_half(CB, 1, proj["cb"])
                hi_to(O, 6, 11)
                mixed_hi(0)
                mixed_hi(1)
                hi_to(O, 11, 12)
                mixed_hi(2)
                mixed_hi(3)
                hi_to(O, 12, 16)
                hi_to(NIN, 0, 2)
                evacuate_half(O, 0, proj["o"], func=ACT.Sigmoid)
                hi_to(NIN, 2, 3)
                evacuate_half(O, 1, proj["o"], func=ACT.Sigmoid)
                hi_to(NIN, 3, 5)
                mixed_hi(4)
                mixed_hi(5)
                hi_to(NIN, 5, 6)
                mixed_hi(6)
                mixed_hi(7)
                hi_to(NIN, 6, 16)
                hi_to(NIN + 1, 0, 5)
                evacuate_half(NIN, 0, mixoT)
                hi_to(NIN + 1, 5, 6)
                evacuate_half(NIN, 1, mixoT)
                hi_to(NIN + 1, 6, 10)
                for a in range(TT):
                    act.wait_ge(x1_ready, a + 1)
                    squares(x_res, xs, NORM_FFN, a, 0)
                    hi_to(NIN + 1, 10 + a, 11 + a)
                for s, k in enumerate((sub_keys_1, sub_keys_2)):
                    act.dma_start(keys[:, s, :], k[0]).then_inc(keys_landed, 16)
                hi_to(NIN + 1, 12, 16)
                hi_to(NIN + 2, 0, 1)
                evacuate_half(NIN + 1, 0, mixoT[:, UC:2 * UC, :], done=half_out_act)
                hi_to(NIN + 2, 1, 2)
                warm_root()
                for n in range(1, NSQ[NORM_FFN]):
                    for a in range(TT):
                        act.wait_ge(x1_ready, n * TT + a + 1)
                        squares(x_res, xs, NORM_FFN, a, n)
                root(NORM_FFN)
                scale_last(NORM_FFN)
                act.wait_ge(cols_ready, 2)
                take_hi(g_ffn, NORM_FFN)
                hi_to(NIN + 2, 2, 4)
                pass_hi_rest(NIN + 2)
                hi_to(NIN + 3, 0, 5)
                evacuate_half(NIN + 2, 0, qT)
                hi_to(NIN + 3, 5, 6)
                evacuate_half(NIN + 2, 1, qT)
                hi_to(NIN + 3, 6, 8)
                act.wait_ge(keys_turned, 1)
                nc.scalar.activation(keysT, ps[:, 0, 0:2 * P].rearrange("p (s n) -> p s n", s=2), ACT.Copy)\
                    .then_inc(keysT_ready, 1)

                def copy_scores(half, a):
                    act.wait_ge(s_done, half * TT + a + 1)
                    o = half * 2048 + a * UW
                    g0 = a * 2 * PH + half * PH
                    nc.scalar.activation(scores[:, g0:g0 + PH, :], flat[:, o:o + UW].rearrange("p (g n) -> p g n", n=NK),
                                         ACT.Copy).then_inc(s_copied, 1)

                hi_to(NIN + 3, 8, 10)
                copy_scores(0, 0)
                copy_scores(0, 1)
                hi_to(NIN + 3, 10, 16)
                evacuate_half(NIN + 3, 0, qT[:, UC:2 * UC, :], done=half_out_act)

                def u_hi(j, turned_at, free):
                    act.wait_ge(u_turned, turned_at)
                    if free is not None:
                        act.wait_ge(u_done, free)
                    nc.scalar.activation(w_hi[:, j % 2, :], flat[:, (j % 2) * UW:(j % 2 + 1) * UW], ACT.Copy)\
                        .then_inc(uh_split, 1)

                def gelu_into(dst, b, done_at, free=None, bank0=4):
                    act.wait_ge(u_done, done_at)
                    if free is not None:
                        act.wait_ge(gated, free)
                    nc.scalar.activation(dst, ps[:, bank0 + b, 0:T], ACT.Gelu).then_inc(gelu_done, 1)

                act.wait_ge(unit_done, NPU)
                u_hi(0, 1, None)
                copy_scores(1, 0)
                u_hi(1, 2, None)
                copy_scores(1, 1)
                u_hi(2, 3, 1)
                gelu_into(A3[:, 0, :], 0, 2)
                u_hi(3, 4, 2)

                def pick_bodies(it0, it1):
                    with act.Fori(it0, it1) as it:
                        for j in range(4):
                            u_hi(j, it * 4 + (j + 1), it * 4 + (j - 1))
                            if j % 2 == 1:
                                gelu_into(A3[:, bass.ds(it * 2 + (j // 2 - 1), 1), :], (j // 2 - 1) % 2, it * 4 + (j - 1))

                SOFT = PICK_TILES // 2 - 4
                pick_bodies(1, SOFT)
                act.wait_ge(soft_in, 1)
                nc.scalar.activation(shifted, shifted, ACT.Exp).then_inc(soft_out, 1)
                pick_bodies(SOFT, PICK_TILES // 2)

                def hot_parts(b, token, ready, free):
                    act.wait_ge(hot_j_ready, ready)
                    if free is not None:
                        act.wait_ge(gate_block, free)
                    for t in range(4):
                        for part in range(2):
                            last = nc.scalar.activation(hot[:, b, 2 + part, t, :], hot_j[:, t, :], ACT.Copy,
                                                        scale=parts[:, part, token(t)])
                    last.then_inc(parts_ready, 1)

                def gate_body(it, first):
                    for j in range(4):
                        n = 2 * PICK_TILES + j
                        u_hi(j, it * 4 + (n + 1), it * 4 + (n - 1))
                        if first and j == 1:
                            gelu_into(A3[:, PICK_TILES - 1, :], 1, n - 1)
                        elif j % 2 == 1:
                            b = (j // 2 - 1) % 2
                            gelu_into(act_out[:, b, :], b, it * 4 + (n - 1), None if first else it * 2 - 1)
                        hot_parts(j % 2, (lambda t: slice(4 * j + t, 4 * j + t + 1)) if first else
                                  (lambda t: bass.ds(it * 16 + (4 * j + t), 1)),
                                  it * 4 + (j + 1), None if first and j < 2 else it * 4 + (j - 1))

                gate_body(0, True)
                with act.Fori(1, TB // 4) as it:
                    gate_body(it, False)

                def hi_of_turned(j, ready, free):
                    act.wait_ge(dve_turned, ready)
                    act.wait_ge(u_done, free)
                    nc.scalar.activation(
                        w_hi[:, j % 2, :].rearrange("p (c e q) -> p c e q", e=B4, q=Q32),
                        turned_u[:, j % 2, :].rearrange("p (e c q) -> p c e q", e=B4, q=Q32), ACT.Copy)\
                        .then_inc(uh_split, 1)

                def rest_body(it, first):
                    for j in range(4):
                        n = 2 * REST0 + j
                        hi_of_turned(j, it * 4 + (j + 1), it * 4 + (n - 1))
                        if j % 2 == 1:
                            b = (j // 2 - 1) % 2
                            gelu_into(act_out[:, b, :], b, it * 4 + (n - 1), it * 2 + (GATE_TILES + j // 2 - 2),
                                      4 if first and j == 1 else 6)

                rest_body(0, True)
                with act.Fori(1, REST // 2) as it:
                    rest_body(it, False)

                def a_hi_of(i, s, free):
                    if free is not None:
                        act.wait_ge(v_done, free)
                    nc.scalar.activation(a_hi[:, s, :], A3[:, i, :], ACT.Copy).then_inc(ah_ready, 1)

                def v_hi_of(j, landed, free):
                    act.wait_ge(raw_landed[slot_of(NPU + j)], landed)
                    if free is not None:
                        act.wait_ge(v_done, free)
                    nc.scalar.activation(v_hi[:, j, :], raw[:, slot_of(NPU + j), :], ACT.Copy)\
                        .then_inc(vh_split, 1)

                act.wait_ge(gate_applied, TB)
                act.wait_ge(u_done, NUU - 1)
                a_hi_of(0, 0, None)
                for n in range(2):
                    v_hi_of(n, landed_at(NPU + n), None)
                gelu_into(act_out[:, 1, :], 1, NUU, TILES - 2 - PICK_TILES, 6)
                a_hi_of(1, 1, None)
                for n in range(2, RAWS):
                    v_hi_of(n, landed_at(NPU + n), None)
                act.wait_ge(gated, TILES - PICK_TILES)
                with act.Fori(1, NUU // RAWS) as it:
                    for j in range(RAWS):
                        if j % 2 == 0:
                            a_hi_of(bass.ds(it * 2 + j // 2, 1), j // 2, it * RAWS + (j - 2))
                        v_hi_of(j, it * 16 + landed_at(NPU + j), it * RAWS + (j - 3))
                warm_root()
                for n in range(NSQ[NORM_FINAL]):
                    for a in range(TT):
                        act.wait_ge(x2_ready, n * TT + a + 1)
                        squares(x1_back, spare, NORM_FINAL, a, n)
                root(NORM_FINAL)
                act.wait_ge(inv_ready, NORM_FINAL + 1)
                act.wait_ge(scaled, 3 * NORM_FINAL + 2 * TT)
                for h in range(2):
                    cs = slice(h * UW, (h + 1) * UW)
                    nc.scalar.activation(y_out[:, 1, cs], y_out[:, 1, cs], ACT.Copy, scale=INV[:, 1:2])\
                        .then_inc(out_ready[1], 1)

            @block.vector
            def _(dve):
                newtons = [0]

                def chain(ins):
                    newtons[0] += 1
                    ins.then_inc(newton, 1)
                    dve.wait_ge(newton, newtons[0])

                def inverse_root(ms, root, inv, tmp):
                    chain(nc.vector.reciprocal(inv, root))
                    chain(nc.vector.scalar_tensor_tensor(out=tmp, in0=inv, scalar=-0.5, in1=inv, op0=ALU.mult,
                                                         op1=ALU.mult))
                    chain(nc.vector.tensor_tensor(tmp, tmp, ms, ALU.mult))
                    chain(nc.vector.scalar_tensor_tensor(out=inv, in0=tmp, scalar=1.5, in1=inv, op0=ALU.add,
                                                         op1=ALU.mult))

                def rstd(r, meanwhile=None):
                    dve.wait_ge(squares_done, SQ0[r] + TT * NSQ[r])
                    chain(nc.vector.tensor_reduce(TMP, sums(r), AX_X, ALU.add))
                    nc.vector.tensor_scalar(MS, TMP, 1.0 / D, EPS, ALU.mult, ALU.add).then_inc(mean_done, 1)
                    if meanwhile is not None:
                        meanwhile()
                    dve.wait_ge(mean_done, r + 1)
                    dve.wait_ge(root_done, r + 1)
                    inverse_root(MS, ROOT, INV, TMP)
                    nc.vector.engine_nop().then_inc(inv_ready, 1)

                def scale_x():
                    for a, h in ((0, 0), (1, 0), (0, 1)):
                        nc.vector.tensor_scalar(xs[:, a, h * UW:(h + 1) * UW], x_res[:, a, h * UW:(h + 1) * UW],
                                                INV[:, a:a + 1], None, ALU.mult).then_inc(scaled, 1)

                def take_lo(gain, hi_before, c0=0, c1=C):
                    for c in range(c0, c1):
                        if c % 2 == 0:
                            dve.wait_ge(hi_taken, hi_before + c + 2)
                        nc.vector.scalar_tensor_tensor(out=xl3[:, c, :], in0=chunks16[:, c, :],
                                                       scalar=gain[:, c:c + 1], in1=xh3[:, c, :].bitcast(F32),
                                                       op0=ALU.mult, op1=ALU.subtract).then_inc(lo_taken, 1)

                def lo_unit(ready, j, n0):
                    dve.wait_ge(hi_split, ready)
                    nc.vector.tensor_tensor(w_lo[:, (n0 + j) % 2, :], raw[:, slot_of(n0 + j), :],
                                            w_hi[:, (n0 + j) % 2, :].bitcast(F32), ALU.subtract)\
                        .then_inc(lo_split, 1)

                def pass_lo(p):
                    for j in range(RAWS):
                        lo_unit(unit0(p) + j + 1, j, unit0(p))
                    with dve.Fori(1, C // RAWS) as it:
                        for j in range(RAWS):
                            lo_unit(it * RAWS + (unit0(p) + j + 1), j, unit0(p))

                nc.vector.memset(ssq[:, 7:8], 1.0).then_inc(warm, 1)
                nc.vector.memset(v_nat[:, :, :, DH:DH + 1], 1.0).then_inc(v_ready, 1)
                rstd(NORM_MIX)
                scale_x()
                for n in range(GU):
                    lo_unit(n + 1, n, 0)
                dve.wait_ge(cols_ready, 1)
                take_lo(g_mix, 0)
                for p in range(CX):
                    pass_lo(p)

                def lo_to(p, k0, k1):
                    for k in range(k0, k1):
                        lo_unit(unit0(p) + k + 1, k, unit0(p))

                R = lambda n: rows[0:NH, n, :]
                gate_steps = [0]

                def gate_chain(ins):
                    gate_steps[0] += 1
                    ins.then_inc(gate_step_dve, 1)
                    dve.wait_ge(gate_step_dve, gate_steps[0])

                def exponent(h):
                    m = ps[:, 4 + h // 2, (h % 2) * T:(h % 2 + 1) * T]
                    nc.vector.tensor_scalar(sw[:, h, 0:T], m, aN[:, 0, h:h + 1], 0.0, ALU.subtract, ALU.max)
                    nc.vector.tensor_scalar(sw[:, h, T:T + P], m[:, P:T], aN[:, 1, h:h + 1], 0.0,
                                            ALU.subtract, ALU.max).then_inc(expo_in, 1)

                def mask(h):
                    dve.wait_ge(expo_out, h + 1)
                    nc.vector.tensor_tensor(sw[:, h, :], sw[:, h, :], causal, ALU.mult).then_inc(sw_half, 1)

                def weights(h):
                    dve.wait_ge(sw_half, h + 1)
                    dve.wait_ge(qk_done, h + 1)
                    nc.vector.tensor_tensor(sw[:, h, :], ps[:, QK_BANK[h], 0:T + P], sw[:, h, :], ALU.mult)\
                        .then_inc(sw_ready, 1)

                def denominators(jt):
                    gs = slice(jt * NH, (jt + 1) * NH)
                    dve.wait_ge(pv_done, (jt + 1) * NH)
                    chain(nc.vector.tensor_copy(NQ[:, gs], ps[:, 0:NH, DH]))
                    chain(nc.vector.scalar_tensor_tensor(out=DEN[:, gs], in0=NQ[:, gs], scalar=-1.0, in1=NQ[:, gs],
                                                         op0=ALU.mult, op1=ALU.max))
                    chain(nc.vector.tensor_tensor(DEN[:, gs], DEN[:, gs], limN[:, jt, :], ALU.max))
                    nc.vector.reciprocal(DEN[:, gs], DEN[:, gs]).then_inc(den_ready, 1)

                def normalise_h(jt):
                    for h in HEADS:
                        g = jt * NH + h
                        nc.vector.tensor_scalar(h_nat[:, jt, h, :], h_nat[:, jt, h, :], HINV[:, g:g + 1], None,
                                                ALU.mult).then_inc(h_ready, 1)

                u = proj["cx"]
                conv_steps = [0]

                def conv(tap, c0, c1):
                    if conv_steps[0]:
                        dve.wait_ge(conv_step, conv_steps[0])
                    if tap is None:
                        nc.vector.tensor_tensor(u[:, c0:c1, :], proj["cc"][:, c0:c1, :], u[:, c0:c1, :], ALU.mult)\
                            .then_inc(conv_step, 1)
                        conv_steps[0] += 1
                        return
                    for c in range(c0, c1):
                        if tap == 2:
                            last = nc.vector.tensor_scalar(mixT[:, c, :], u[:, c, :], taps[:, 2, c:c + 1], None, ALU.mult)
                        else:
                            lag = 2 - tap
                            last = nc.vector.scalar_tensor_tensor(
                                out=mixT[:, c, lag:T], in0=u[:, c, 0:T - lag], scalar=taps[:, tap, c:c + 1],
                                in1=mixT[:, c, lag:T], op0=ALU.mult, op1=ALU.add)
                    last.then_inc(conv_step, 1)
                    conv_steps[0] += 1

                def conv_gate(c0, c1):
                    dve.wait_ge(conv_step, conv_steps[0])
                    nc.vector.tensor_tensor(mixT[:, c0:c1, :], mixT[:, c0:c1, :], proj["cb"][:, c0:c1, :], ALU.mult)\
                        .then_inc(mix_ready, 1)

                def h_transposed(c0, c1):
                    for c in range(c0, c1):
                        last = nc.vector.tensor_scalar(mixT[:, UC + c, :], chunks16[:, UC + c, :], g_ml[:, c:c + 1],
                                                       None, ALU.mult)
                    last.then_inc(h_out, 1)

                def output_gate(m):
                    nc.vector.tensor_tensor(mixT[:, 2 * m:2 * m + 2, :], mixT[:, 2 * m:2 * m + 2, :],
                                            proj["o"][:, 2 * m - UC:2 * m - UC + 2, :], ALU.mult).then_inc(mix_ready, 1)

                def mixed_lo(m):
                    dve.wait_ge(hi_taken, C + m + 1)
                    nc.vector.tensor_tensor(xl3[:, 2 * m:2 * m + 2, :], mixT[:, 2 * m:2 * m + 2, :],
                                            xh3[:, 2 * m:2 * m + 2, :].bitcast(F32), ALU.subtract).then_inc(lo_taken, 1)

                lo_to(CX, 0, 10)
                dve.wait_ge(small_landed, 16 * 7)
                dve.wait_ge(gate_step_pe, 2)
                gate_chain(nc.vector.tensor_scalar(R(0), ps[0:NH, 1, 0:T], bias_i[:, 0:1], None, ALU.add))
                gate_chain(nc.vector.tensor_scalar(R(1), ps[0:NH, 1, T:2 * T], bias_f[:, 0:1], None, ALU.add))
                gate_chain(nc.vector.scalar_tensor_tensor(out=R(4), in0=R(1), scalar=-1.0, in1=R(1),
                                                          op0=ALU.mult, op1=ALU.max))
                lo_to(CX, 10, 12)
                dve.wait_ge(gate_step_act, 2)
                gate_chain(nc.vector.tensor_scalar(R(6), R(5), 1.0, None, ALU.add))
                lo_to(CX, 12, 14)
                dve.wait_ge(gate_step_act, 3)
                gate_chain(nc.vector.scalar_tensor_tensor(out=R(1), in0=R(1), scalar=0.0, in1=R(4),
                                                          op0=ALU.min, op1=ALU.subtract))
                gate_chain(nc.vector.memset(R(7), 1.0))
                gate_chain(nc.vector.tensor_tensor_scan(R(2), R(7), R(1), 0.0, ALU.mult, ALU.add))
                lo_to(CX, 14, 15)
                gate_chain(nc.vector.tensor_tensor(R(3), R(0), R(2), ALU.subtract))
                gate_chain(nc.vector.tensor_tensor_scan(R(4), R(3), R(3), 0.0, ALU.max, ALU.max))
                lo_to(CX, 15, 16)
                gate_chain(nc.vector.tensor_copy(R(7), R(4)))
                gate_chain(nc.vector.tensor_tensor(R(5), R(2), R(4), ALU.add))
                lo_to(CC, 0, 8)
                dve.wait_ge(gate_step_pe, 4)
                gate_chain(nc.vector.tensor_copy(aN, ps[:, 7, 0:TT * NH].rearrange("p (a h) -> p a h", a=TT)))
                gate_chain(nc.vector.tensor_copy(limN, ps[:, 7, TT * NH:2 * TT * NH].rearrange("p (a h) -> p a h", a=TT)))
                exponent(0)
                lo_to(CC, 8, 9)
                exponent(1)
                exponent(2)
                lo_to(CC, 9, 10)
                exponent(3)
                lo_to(CC, 10, 11)
                mask(0)
                mask(1)
                lo_to(CC, 11, 12)
                mask(2)
                mask(3)
                lo_to(CC, 12, 13)
                weights(0)
                weights(1)
                lo_to(CC, 13, 14)
                weights(2)
                weights(3)
                lo_to(CC, 14, 16)
                lo_to(CB, 0, 7)
                dve.wait_ge(cols_ready, 2)
                dve.wait_ge(pass_out, CB)
                conv(None, 0, 4)
                lo_to(CB, 7, 8)
                denominators(0)
                lo_to(CB, 8, 9)
                conv(None, 4, 8)
                lo_to(CB, 9, 10)
                conv(2, 0, 4)
                lo_to(CB, 10, 11)
                conv(2, 4, 8)
                lo_to(CB, 11, 12)
                denominators(1)
                lo_to(CB, 12, 13)
                conv(1, 0, 3)
                lo_to(CB, 13, 14)
                conv(1, 3, 6)
                lo_to(CB, 14, 15)
                conv(1, 6, 8)
                lo_to(CB, 15, 16)
                dve.wait_ge(h_squared, HN)
                nc.vector.tensor_scalar(HMS, HSS, 1.0 / DH, EPS, ALU.mult, ALU.add).then_inc(h_rstd, 1)
                conv(0, 0, 3)
                lo_to(O, 0, 1)
                conv(0, 3, 6)
                lo_to(O, 1, 2)
                dve.wait_ge(h_rstd, 1)
                dve.wait_ge(h_squared, HN + 1)
                inverse_root(HMS, HROOT, HINV, HTMP)
                conv(0, 6, 8)
                lo_to(O, 2, 3)
                normalise_h(0)
                lo_to(O, 3, 4)
                normalise_h(1)
                lo_to(O, 4, 7)
                dve.wait_ge(pass_out, O)
                conv_gate(0, 4)
                lo_to(O, 7, 8)
                conv_gate(4, 8)
                lo_to(O, 8, 9)
                dve.wait_ge(h_turned, 1)
                h_transposed(0, 3)
                lo_to(O, 9, 10)
                h_transposed(3, 6)
                lo_to(O, 10, 11)
                h_transposed(6, 8)
                lo_to(O, 11, 12)
                mixed_lo(0)
                mixed_lo(1)
                lo_to(O, 12, 13)
                mixed_lo(2)
                mixed_lo(3)
                lo_to(O, 13, 16)
                lo_to(NIN, 0, 4)
                dve.wait_ge(pass_out, NIN)
                dve.wait_ge(h_out, 3)
                output_gate(4)
                output_gate(5)
                lo_to(NIN, 4, 5)
                output_gate(6)
                output_gate(7)
                lo_to(NIN, 5, 6)
                mixed_lo(4)
                mixed_lo(5)
                lo_to(NIN, 6, 7)
                mixed_lo(6)
                mixed_lo(7)
                lo_to(NIN, 7, 16)

                def x1_part(n, a, turned_at):
                    c0, c1 = SQ_PARTS[NORM_FFN][n]
                    dve.wait_ge(mixo_turned, turned_at)
                    o = c0 % UW
                    nc.vector.tensor_tensor(x_res[:, a, c0:c1], back[:, a, o:o + c1 - c0], x_res[:, a, c0:c1], ALU.add)\
                        .then_inc(x1_ready, 1)

                def second_half(p, dst):
                    dve.wait_ge(unit_done, unit0(p) + C)
                    o = half_of(p) * 2048 + UW
                    nc.vector.tensor_copy(dst, flat[:, o:o + UW].rearrange("p (c t) -> p c t", t=T))\
                        .then_inc(half_out_dve, 1)

                lo_to(NIN + 1, 0, 8)
                x1_part(0, 0, 1)
                lo_to(NIN + 1, 8, 9)
                x1_part(0, 1, 2)
                lo_to(NIN + 1, 9, 16)
                lo_to(NIN + 2, 0, 1)
                second_half(NIN + 1, mixoT[:, UC + 4:C, :])
                for n in (1, 2):
                    for a in range(TT):
                        x1_part(n, a, TT * n + a + 1)
                rstd(NORM_FFN)
                scale_x()
                take_lo(g_ffn, C + MIX, 0, UC)
                lo_to(NIN + 2, 1, 2)
                take_lo(g_ffn, C + MIX, UC, C)
                lo_to(NIN + 2, 2, 16)

                steps = [0]

                def top_chain(ins):
                    steps[0] += 1
                    ins.then_inc(top_step, 1)
                    dve.wait_ge(top_step, steps[0])

                def top16(rows):
                    for src, values, places, spare in rows:
                        last = nc.vector.max(values[:, 0:8], src)
                    top_chain(last)
                    for src, values, places, spare in rows:
                        nc.vector.max_index(places[:, 0:8], values[:, 0:8], src)
                        last = nc.vector.match_replace(spare, values[:, 0:8], src, LOWEST)
                    top_chain(last)
                    for src, values, places, spare in rows:
                        last = nc.vector.max(values[:, 8:16], spare)
                    top_chain(last)
                    for src, values, places, spare in rows:
                        last = nc.vector.max_index(places[:, 8:16], values[:, 8:16], spare)
                    steps[0] += 1
                    last.then_inc(top_step, 1)

                def best_places(*groups):
                    if steps[0]:
                        dve.wait_ge(top_step, steps[0])
                    top16([(scores[:, g, :], top_v[:, g, :], top_i[:, g, :], left[:, g % 2, 0:NK]) for g in groups])

                lo_to(NIN + 3, 0, 11)
                dve.wait_ge(s_copied, 1)
                for g in range(5):
                    best_places(g)
                    lo_to(NIN + 3, 11 + g, 12 + g)
                second_half(NIN + 3, qT[:, C - 4:C, :])
                best_places(5)
                best_places(6, 7)

                def u_lo(j, ready):
                    dve.wait_ge(uh_split, ready)
                    nc.vector.tensor_tensor(w_lo[:, j % 2, :], flat[:, (j % 2) * UW:(j % 2 + 1) * UW],
                                            w_hi[:, j % 2, :].bitcast(F32), ALU.subtract).then_inc(ul_split, 1)

                unit = [0]

                def next_unit():
                    u_lo(unit[0] % 4, unit[0] + 1)
                    unit[0] += 1

                for a, half in ((1, 0), (0, 1), (1, 1)):
                    for k in range(PH // 2):
                        next_unit()
                        dve.wait_ge(s_copied, half * TT + a + 1)
                        g = a * 2 * PH + half * PH + 2 * k
                        best_places(g, g + 1)
                tv = top_v.rearrange("p (g s) k -> p g s k", s=2)
                for g in range(TT * PH):
                    next_unit()
                    dve.wait_ge(top_step, steps[0])
                    top_chain(nc.vector.tensor_tensor(
                        cand[:, g, :].rearrange("p (a b) -> p a b", b=TOPK),
                        tv[:, g, 0, :].unsqueeze(2).broadcast_to([P, TOPK, TOPK]),
                        tv[:, g, 1, :].unsqueeze(1).broadcast_to([P, TOPK, TOPK]), ALU.add))
                    top16([(cand[:, g, :], best_v[:, g, :], best_i[:, g, :], left[:, g % 2, :])])
                next_unit()
                dve.wait_ge(top_step, steps[0])
                top_chain(nc.vector.tensor_tensor(shifted, best_v, best_v[:, :, 0:1].broadcast_to([P, TT * PH, TOPK]),
                                                  ALU.subtract))
                nc.vector.tensor_copy(total, shifted[:, :, 0]).then_inc(soft_in, 1)
                flat_i = best_i.rearrange("p g k -> p (g k)")
                top_chain(nc.vector.tensor_scalar(half_i[:, 0, :], flat_i, 4, None, ALU.logical_shift_right))
                top_chain(nc.vector.tensor_scalar(half_i[:, 1, :], flat_i, 15, None, ALU.bitwise_and))
                nc.vector.engine_nop().then_inc(cand_used, 1)
                next_unit()
                top_chain(nc.vector.tensor_copy(half_f, half_i))
                top_chain(nc.vector.tensor_copy(top_f, top_i))
                top_chain(nc.vector.tensor_copy(iota16, iota[:, 0:TOPK]))
                tf = top_f.rearrange("p (g s) k -> p g s k", s=2)
                for s in range(2):
                    pick = half_f[:, s, :].rearrange("p (g k) -> p g k", k=TOPK)
                    for g in range(0, TT * PH, 2):
                        next_unit()
                        gs = slice(g, g + 2)
                        top_chain(nc.vector.tensor_tensor(
                            match[:, gs, :, :], pick[:, gs, :].unsqueeze(3).broadcast_to([P, 2, TOPK, TOPK]),
                            iota16.unsqueeze(1).unsqueeze(1).broadcast_to([P, 2, TOPK, TOPK]), ALU.is_equal))
                        top_chain(nc.vector.tensor_tensor(
                            match[:, gs, :, :], match[:, gs, :, :],
                            tf[:, gs, s, :].unsqueeze(2).broadcast_to([P, 2, TOPK, TOPK]), ALU.mult))
                        top_chain(nc.vector.tensor_reduce(
                            found[:, s, :].rearrange("p (g k) -> p g k", k=TOPK)[:, gs, :], match[:, gs, :, :],
                            AX_X, ALU.add))
                next_unit()
                dve.wait_ge(soft_out, 1)
                top_chain(nc.vector.tensor_reduce(total, shifted, AX_X, ALU.add))
                top_chain(nc.vector.reciprocal(total, total))
                nc.vector.tensor_tensor(found[:, 2, :].rearrange("p (g k) -> p g k", k=TOPK), shifted,
                                        total.unsqueeze(2).broadcast_to([P, TT * PH, TOPK]), ALU.mult)\
                    .then_inc(found_ready, 1)
                while unit[0] < 2 * PICK_TILES - 3:
                    next_unit()
                dve.wait_ge(found_turned, 1)
                by_pick = flat[:, 6 * 512:6 * 512 + 3 * T]
                nc.vector.tensor_copy(picks[:, 0:2, :], by_pick[:, 0:2 * T].rearrange("p (s t) -> p s t", s=2))
                gate = by_pick[:, 2 * T:3 * T]
                top_chain(nc.vector.tensor_copy(picks[:, 2, :], gate))
                next_unit()
                top_chain(nc.vector.tensor_tensor(rest[:, 0, :], gate, picks[:, 2, :], ALU.subtract))
                top_chain(nc.vector.tensor_copy(hot_j[:, 0:2, :].rearrange("p a n -> p (a n)"), rest[:, 0, :]))
                top_chain(nc.vector.tensor_copy(parts[:, 0, :], hot_j[:, 0:2, :].rearrange("p a n -> p (a n)")))
                top_chain(nc.vector.tensor_tensor(parts[:, 1, :], rest[:, 0, :], parts[:, 0, :], ALU.subtract))
                nc.vector.engine_nop().then_inc(picks_ready, 1)
                next_unit()
                next_unit()

                def hot_j_of(tokens, free):
                    if free is not None:
                        dve.wait_ge(parts_ready, free)
                        dve.wait_ge(hot_ready, free)
                    nc.vector.tensor_tensor(hot_j[:, :, :], iota[:, :].unsqueeze(1).broadcast_to([P, 4, P]),
                                            picks[:, 1, tokens].unsqueeze(2).broadcast_to([P, 4, P]),
                                            ALU.is_equal).then_inc(hot_j_ready, 1)

                def hot_i_of(b, tokens, free):
                    if free is not None:
                        dve.wait_ge(gate_block, free)
                    nc.vector.tensor_tensor(hot[:, b, 0, :, :], iota[:, :].unsqueeze(1).broadcast_to([P, 4, P]),
                                            picks[:, 0, tokens].unsqueeze(2).broadcast_to([P, 4, P]),
                                            ALU.is_equal).then_inc(hot_i_ready, 1)

                def apply_group(b, tokens, ready, applied, n_gated):
                    dve.wait_ge(gate_block, ready)
                    if applied is not None:
                        dve.wait_ge(gate_applied, applied)
                    if n_gated is not None:
                        dve.wait_ge(gated, n_gated)
                    nc.vector.tensor_tensor(A3[:, :, tokens], ps[:, 6 + b, :].rearrange("p (t i) -> p i t", t=4),
                                            A3[:, :, tokens], ALU.mult).then_inc(gate_applied, 1)

                def apply_gelu(i, b, ready, applied):
                    dve.wait_ge(gelu_done, ready)
                    if applied is not None:
                        dve.wait_ge(gate_applied, applied)
                    nc.vector.tensor_tensor(A3[:, i, :], act_out[:, b, :], A3[:, i, :], ALU.mult).then_inc(gated, 1)

                def gate_body(it, first, final):
                    for j in range(4):
                        four = lambda g: bass.ds(it * 16 + 4 * g, 4)
                        u_lo(j, it * 4 + (2 * PICK_TILES + j + 1))
                        if not (first and j < 2):
                            if first and j == 2:
                                dve.wait_ge(ones_set, 6)
                            apply_group(j % 2, four(j - 2), it * 4 + (j - 1), None if first and j == 2 else it * 4 + (j - 2),
                                        None if first and j < 4 else it * 2 + (j // 2 - 1))
                        hot_i_of(j % 2, four(j), None if first and j < 2 else it * 4 + (j - 1))
                        if not (final and j == 3):
                            hot_j_of(four(j + 1), it * 4 + (j + 1))
                        if j % 2 == 1 and not (first and j == 1):
                            i = it * 2 + (PICK_TILES + j // 2 - 1)
                            apply_gelu(bass.ds(i, 1), (j // 2 - 1) % 2,
                                       it * 2 + (PICK_TILES + j // 2), it * 4 + (j - 1))

                hot_j_of(slice(0, 4), None)
                gate_body(0, True, False)
                with dve.Fori(1, TB // 4 - 1) as it:
                    gate_body(it, False, False)
                gate_body(TB // 4 - 1, False, True)

                def turn_unit(j, landed, free):
                    s = tile_slot(j // 2)
                    if j % 2 == 0:
                        dve.wait_ge(tile_landed[s], landed)
                    if free is not None:
                        dve.wait_ge(uh_split, free)
                        dve.wait_ge(ul_split, free)
                    half = UW // B4
                    u = raw_tile[:, s, :].rearrange("p (e f) -> p e f", e=B4)
                    nc.vector.transpose(turned_u[:, j % 2, :].rearrange("p (e f) -> p e f", e=B4),
                                        u[:, :, (j % 2) * half:(j % 2 + 1) * half]).then_inc(dve_turned, 1)

                def lo_of_turned(j, ready):
                    dve.wait_ge(uh_split, ready)
                    nc.vector.tensor_tensor(
                        w_lo[:, j % 2, :].rearrange("p (c e q) -> p c e q", e=B4, q=Q32),
                        turned_u[:, j % 2, :].rearrange("p (e c q) -> p c e q", e=B4, q=Q32),
                        w_hi[:, j % 2, :].bitcast(F32).rearrange("p (c e q) -> p c e q", e=B4, q=Q32), ALU.subtract)\
                        .then_inc(ul_split, 1)

                dve.wait_ge(gate_block, TB - 1)
                turn_unit(0, tile_landed_at(REST0), None)
                apply_group(0, slice(T - 8, T - 4), TB - 1, TB - 2, GATE_TILES - 1)
                apply_group(1, slice(T - 4, T), TB, TB - 1, GATE_TILES - 1)
                with dve.Fori(0, REST // 2 - 1) as it:
                    for j in range(4):
                        k = (j + 1) % 4
                        turn_unit(k, it * 64 + tile_landed_at(REST0 + (j + 1) // 2), it * 4 + (2 * REST0 + j))
                        lo_of_turned(j, it * 4 + (2 * REST0 + j + 1))
                for j in range(4):
                    n = NUU - 4 + j
                    if j < 3:
                        turn_unit(j + 1, tile_landed_at(TILES - 2 + (j + 1) // 2), n)
                    lo_of_turned(j, n + 1)

                def a_lo_of(i, s, ready):
                    dve.wait_ge(ah_ready, ready)
                    nc.vector.tensor_tensor(a_lo[:, s, :], A3[:, i, :], a_hi[:, s, :].bitcast(F32), ALU.subtract)\
                        .then_inc(al_ready, 1)

                def v_lo_of(j, ready):
                    dve.wait_ge(vh_split, ready)
                    nc.vector.tensor_tensor(v_lo[:, j, :], raw[:, slot_of(NPU + j), :], v_hi[:, j, :].bitcast(F32),
                                            ALU.subtract).then_inc(vl_split, 1)

                for n in range(RAWS):
                    if n % 2 == 0:
                        a_lo_of(n // 2, n // 2, n // 2 + 1)
                    v_lo_of(n, n + 1)
                with dve.Fori(1, NUU // RAWS) as it:
                    for j in range(RAWS):
                        if j % 2 == 0:
                            a_lo_of(bass.ds(it * 2 + j // 2, 1), j // 2, it * 2 + (j // 2 + 1))
                        v_lo_of(j, it * RAWS + (j + 1))
                def x2_times_gain(a, cs, ready):
                    dve.wait_ge(x2_ready, ready)
                    nc.vector.tensor_tensor(y_out[:, a, cs], x1_back[:, a, cs], g_final[:, cs], ALU.mult)\
                        .then_inc(scaled, 1)

                dve.wait_ge(tail_landed, 16 * 5)
                for h in range(2):
                    cs = slice(h * UW, (h + 1) * UW)
                    dve.wait_ge(v_done, NUU - 1 + h)
                    for a in range(TT):
                        nc.vector.tensor_tensor(x1_back[:, a, cs], natural[:, a, cs], x1_back[:, a, cs], ALU.add)\
                            .then_inc(x2_ready, 1)
                    for a in range(TT - h):
                        x2_times_gain(a, cs, h * TT + a + 1)
                rstd(NORM_FINAL, lambda: x2_times_gain(1, slice(UW, 2 * UW), 2 * TT))
                dve.wait_ge(scaled, 3 * NORM_FINAL + 2 * TT)
                for h in range(2):
                    cs = slice(h * UW, (h + 1) * UW)
                    nc.vector.tensor_scalar(y_out[:, 0, cs], y_out[:, 0, cs], INV[:, 0:1], None, ALU.mult)\
                        .then_inc(out_ready[0], 1)


_INS = ["x", "norm_mix_g", "w_in", "b_igate", "b_fgate", "conv_w", "mlstm_norm_g", "w_out", "norm_ffn_g",
        "w_query", "sub_keys_1", "sub_keys_2", "expert_u", "expert_v", "norm_final_g"]


def kernel(**inputs):
    import numpy as _np
    import concourse.bacc as _bacc
    from concourse import mybir as _mybir
    from concourse.bass_utils import run_bass_kernel_spmd as _run

    nc = _bacc.Bacc("TRN2", target_bir_lowering=False, num_devices=1)
    arrays, args = {}, []
    for name in _INS:
        a = _np.ascontiguousarray(inputs[name])
        arrays[f"in_{name}_dram"] = a
        args.append(nc.dram_tensor(f"in_{name}_dram", a.shape, _mybir.dt.from_np(a.dtype), kind="ExternalInput").ap())
    out = nc.dram_tensor("out_dram", inputs["x"].shape, _mybir.dt.float32, kind="ExternalOutput").ap()
    hybrid_layer(nc, *args, out)
    r = _run(nc, [arrays], core_ids=[0])
    return r.results[0]["out_dram"]
```
